# Optimizing a Trainium2 kernel written in Bass

```python
import jax, jax.numpy as jnp
from jax import lax
import numpy as np
import math

D_MODEL = 1024
BATCH = 1
SEQ = 256
DEPTH = 1

DN_HEADS = 8
DN_HEAD_DIM = 64
DN_WIDTH = DN_HEADS * DN_HEAD_DIM
DN_CONV = 3
DN_CHUNK = 64
ATT_GROUPS = ((128, 1), (512, 4), (2048, 16))
N_GROUPS = 3
ATT_HEADS_PER_GROUP = 8
ATT_HEAD_DIM = 64
ATT_HEADS = N_GROUPS * ATT_HEADS_PER_GROUP
ATT_WIDTH = ATT_HEADS * ATT_HEAD_DIM
ATT_OUT_WIDTH = ATT_HEADS_PER_GROUP * ATT_HEAD_DIM
ATT_BLOCK = 64
ALIBI_MAX = 8.0
D_FF = 2816
FFN_CONV = 3
IN_PROJ_SIZES = (3 * DN_WIDTH, DN_WIDTH, 2 * DN_HEADS, 2 * DN_HEADS,
                 ATT_WIDTH, ATT_WIDTH, ATT_WIDTH, D_MODEL, D_MODEL)
D_IN_PROJ = 3 * DN_WIDTH + DN_WIDTH + 4 * DN_HEADS + 3 * ATT_WIDTH + 2 * D_MODEL
EPS = 1e-6
NEG_INF = -1e30


def rms_norm(x, w):
    xf = x.astype(jnp.float32)
    y = xf * lax.rsqrt(jnp.mean(xf * xf, axis=-1, keepdims=True) + EPS)
    return (y * w.astype(jnp.float32)).astype(x.dtype)

def l2_normalize(t):
    tf = t.astype(jnp.float32)
    return tf * lax.rsqrt(jnp.sum(tf * tf, axis=-1, keepdims=True) + EPS)

def depthwise_conv_centred(x, w):
    width, c = w.shape
    return lax.conv_general_dilated(
        x, w[:, None, :].astype(x.dtype), window_strides=(1,),
        padding=[((width - 1) // 2, width // 2)],
        dimension_numbers=('NWC', 'WIO', 'NWC'), feature_group_count=c)

def alibi_slopes(n):
    return 2.0 ** (-ALIBI_MAX * jnp.arange(1, n + 1, dtype=jnp.float32) / n)

def gated_delta_rule_chunked(q, k, v, g, beta):
    f32 = jnp.float32
    n, h, t, dk = q.shape
    dv = v.shape[-1]
    c = DN_CHUNK
    nc = t // c
    q = q.astype(f32).reshape(n, h, nc, c, dk) * (dk ** -0.5)
    k = k.astype(f32).reshape(n, h, nc, c, dk)
    v = v.astype(f32).reshape(n, h, nc, c, dv)
    beta = beta.astype(f32).reshape(n, h, nc, c)
    g = jnp.cumsum(g.astype(f32).reshape(n, h, nc, c), axis=-1)
    idx = jnp.arange(c)
    incl = idx[:, None] >= idx[None, :]
    strict = idx[:, None] > idx[None, :]
    decay = jnp.exp(jnp.where(incl, g[..., :, None] - g[..., None, :], -jnp.inf))
    kb = k * beta[..., None]
    a_low = jnp.where(strict, jnp.einsum('nhcid,nhcjd->nhcij', kb, k) * decay, 0.0)
    eye = jnp.eye(c, dtype=f32)
    tmat = lax.linalg.triangular_solve(eye + a_low, jnp.broadcast_to(eye, a_low.shape),
                                       left_side=True, lower=True, unit_diagonal=True)
    u = jnp.einsum('nhcij,nhcjv->nhciv', tmat, v * beta[..., None])
    w = jnp.einsum('nhcij,nhcjk->nhcik', tmat, kb * jnp.exp(g)[..., None])
    qk = jnp.einsum('nhcid,nhcjd->nhcij', q, k) * decay
    g_last = g[..., -1]
    q_dec = q * jnp.exp(g)[..., None]
    k_dec = k * jnp.exp(g_last[..., None] - g)[..., None]
    xs = tuple(jnp.moveaxis(arr, 2, 0) for arr in (u, w, qk, q_dec, k_dec, g_last))

    def step(state, inp):
        u_i, w_i, qk_i, qd_i, kd_i, gl_i = inp
        v_new = u_i - jnp.einsum('nhck,nhkv->nhcv', w_i, state)
        o_i = jnp.einsum('nhck,nhkv->nhcv', qd_i, state) + jnp.einsum('nhij,nhjv->nhiv', qk_i, v_new)
        state = state * jnp.exp(gl_i)[..., None, None] + jnp.einsum('nhck,nhcv->nhkv', kd_i, v_new)
        return state, o_i

    _, o = lax.scan(step, jnp.zeros((n, h, dk, dv), f32), xs)
    return jnp.moveaxis(o, 0, 2).reshape(n, h, t, dv)

def dilated_window_attention(q, k, v, slopes, dilation, radius):
    b, s, h, dh = q.shape
    blk = ATT_BLOCK
    sub = s // dilation
    nb = -(-sub // blk)
    lp = nb * blk

    def to_sub(a):
        return a.reshape(b, sub, dilation, h, dh).transpose(0, 2, 3, 1, 4)

    qs = jnp.pad(to_sub(q), ((0, 0),) * 3 + ((0, lp - sub), (0, 0))).reshape(b, dilation, h, nb, blk, dh)

    def windows(a):
        ap = jnp.pad(to_sub(a), ((0, 0),) * 3 + ((blk, lp - sub + blk), (0, 0)))
        ap = ap.reshape(b, dilation, h, nb + 2, blk, dh)
        return jnp.concatenate([ap[:, :, :, 0:nb], ap[:, :, :, 1:nb + 1], ap[:, :, :, 2:nb + 2]], axis=-2)

    kw, vw = windows(k), windows(v)
    blocks = jnp.arange(nb)[:, None, None]
    qi = blocks * blk + jnp.arange(blk)[None, :, None]
    kj = (blocks - 1) * blk + jnp.arange(3 * blk)[None, None, :]
    rel = jnp.abs(qi - kj)
    valid = (rel <= radius) & (kj >= 0) & (kj < sub)
    scores = jnp.einsum('bdhnqe,bdhnke->bdhnqk', qs, kw) * (dh ** -0.5)
    scores = scores - slopes[:, None, None, None] * (rel * dilation).astype(jnp.float32)
    scores = jnp.where(valid, scores, NEG_INF)
    m = jnp.max(scores, axis=-1, keepdims=True)
    lse = m + jnp.log(jnp.sum(jnp.exp(scores - m), axis=-1, keepdims=True))
    o = jnp.einsum('bdhnqk,bdhnke->bdhnqe', jnp.exp(scores - lse), vw)
    o = o.reshape(b, dilation, h, lp, dh)[:, :, :, :sub].transpose(0, 3, 1, 2, 4).reshape(b, s, h, dh)
    lse = lse.reshape(b, dilation, h, lp)[..., :sub].transpose(0, 3, 1, 2).reshape(b, s, h)
    return o, lse

def hybrid_block(x, norm1_w, w_in, dn_conv_w, dn_a_log, dn_dt_bias, dn_out_norm_w,
                 attn_q_norm_w, attn_k_norm_w, w_dn_out, w_attn_out, w_o,
                 norm2_w, w_ffn_up, ffn_conv_w, w_ffn_down):
    f32 = jnp.float32
    b, s, _ = x.shape
    h = rms_norm(x, norm1_w)
    proj = h @ w_in
    points = np.cumsum(np.array(IN_PROJ_SIZES))[:-1].tolist()
    qkv_a, z_a, a_in, b_in, q_b, k_b, v_b, gate_a, gate_b = jnp.split(proj, points, axis=-1)

    qkv_a = jax.nn.silu(depthwise_conv_centred(qkv_a, dn_conv_w))
    q_a, k_a, v_a = [t.reshape(b, s, DN_HEADS, DN_HEAD_DIM).transpose(0, 2, 1, 3)
                     for t in jnp.split(qkv_a, 3, axis=-1)]
    q_a, k_a = l2_normalize(q_a), l2_normalize(k_a)
    a_dir = a_in.astype(f32).reshape(b, s, 2, DN_HEADS)
    beta = jax.nn.sigmoid(b_in.astype(f32).reshape(b, s, 2, DN_HEADS))
    g = -jnp.exp(dn_a_log.astype(f32)) * jax.nn.softplus(a_dir + dn_dt_bias.astype(f32))
    g = g.transpose(2, 0, 3, 1)
    beta = beta.transpose(2, 0, 3, 1)
    both = lambda t: jnp.concatenate([t, jnp.flip(t, axis=2)], axis=0)
    o2 = gated_delta_rule_chunked(both(q_a), both(k_a), both(v_a),
                                  jnp.concatenate([g[0], jnp.flip(g[1], axis=2)], axis=0),
                                  jnp.concatenate([beta[0], jnp.flip(beta[1], axis=2)], axis=0))
    o_a = (o2[:b] + jnp.flip(o2[b:], axis=2)).transpose(0, 2, 1, 3)
    z = z_a.astype(f32).reshape(b, s, DN_HEADS, DN_HEAD_DIM)
    o_a = rms_norm(o_a, dn_out_norm_w) * jax.nn.silu(z)
    y_a = o_a.reshape(b, s, DN_WIDTH).astype(x.dtype) @ w_dn_out

    heads = lambda t: t.astype(f32).reshape(b, s, N_GROUPS, ATT_HEADS_PER_GROUP, ATT_HEAD_DIM)
    q_b = rms_norm(heads(q_b), attn_q_norm_w)
    k_b = rms_norm(heads(k_b), attn_k_norm_w)
    v_b = heads(v_b)
    slopes = alibi_slopes(ATT_HEADS).reshape(N_GROUPS, ATT_HEADS_PER_GROUP)
    outs, lses = [], []
    for gi, (window, dil) in enumerate(ATT_GROUPS):
        o_g, l_g = dilated_window_attention(q_b[:, :, gi], k_b[:, :, gi], v_b[:, :, gi],
                                            slopes[gi], dil, window // (2 * dil))
        outs.append(o_g)
        lses.append(l_g)
    wts = jax.nn.softmax(jnp.stack(lses), axis=0)
    o_b = jnp.einsum('gbsh,gbshe->bshe', wts, jnp.stack(outs))
    y_b = o_b.reshape(b, s, ATT_OUT_WIDTH).astype(x.dtype) @ w_attn_out

    mixed = jax.nn.sigmoid(gate_a) * y_a + jax.nn.sigmoid(gate_b) * y_b
    x = x + mixed @ w_o

    h2 = rms_norm(x, norm2_w)
    gate, up = jnp.split(depthwise_conv_centred(h2 @ w_ffn_up, ffn_conv_w), 2, axis=-1)
    return x + (jax.nn.silu(gate) * up) @ w_ffn_down

def first_inputs(seed: int = 0) -> dict:
    key = jax.random.key(seed)
    ks = jax.random.split(key, 17)
    f32 = jnp.float32
    normal = lambda k, shape, scale: jax.random.normal(k, shape, f32) * scale
    dt = jnp.exp(jax.random.uniform(ks[5], (DEPTH, 2, DN_HEADS), f32, np.log(1e-3), np.log(1e-1)))
    return {
        "x": normal(ks[0], (BATCH, SEQ, D_MODEL), 1.0),
        "norm1_w": 1.0 + normal(ks[1], (DEPTH, D_MODEL), 0.05),
        "w_in": normal(ks[2], (DEPTH, D_MODEL, D_IN_PROJ), D_MODEL ** -0.5),
        "dn_conv_w": normal(ks[3], (DEPTH, DN_CONV, 3 * DN_WIDTH), DN_CONV ** -0.5),
        "dn_a_log": jnp.log(jax.random.uniform(ks[4], (DEPTH, 2, DN_HEADS), f32, 1.0, 16.0)),
        "dn_dt_bias": dt + jnp.log(-jnp.expm1(-dt)),
        "dn_out_norm_w": 1.0 + normal(ks[6], (DEPTH, DN_HEAD_DIM), 0.05),
        "attn_q_norm_w": 1.0 + normal(ks[7], (DEPTH, ATT_HEAD_DIM), 0.05),
        "attn_k_norm_w": 1.0 + normal(ks[8], (DEPTH, ATT_HEAD_DIM), 0.05),
        "w_dn_out": normal(ks[9], (DEPTH, DN_WIDTH, D_MODEL), DN_WIDTH ** -0.5),
        "w_attn_out": normal(ks[10], (DEPTH, ATT_OUT_WIDTH, D_MODEL), ATT_OUT_WIDTH ** -0.5),
        "w_o": normal(ks[11], (DEPTH, D_MODEL, D_MODEL), D_MODEL ** -0.5),
        "norm2_w": 1.0 + normal(ks[12], (DEPTH, D_MODEL), 0.05),
        "w_ffn_up": normal(ks[13], (DEPTH, D_MODEL, 2 * D_FF), D_MODEL ** -0.5),
        "ffn_conv_w": normal(ks[14], (DEPTH, FFN_CONV, 2 * D_FF), FFN_CONV ** -0.5),
        "w_ffn_down": normal(ks[15], (DEPTH, D_FF, D_MODEL), D_FF ** -0.5),
    }

def first_block(x, norm1_w, w_in, dn_conv_w, dn_a_log, dn_dt_bias, dn_out_norm_w,
              attn_q_norm_w, attn_k_norm_w, w_dn_out, w_attn_out, w_o,
              norm2_w, w_ffn_up, ffn_conv_w, w_ffn_down):
    for layer in range(DEPTH):
        x = hybrid_block(x, norm1_w[layer], w_in[layer], dn_conv_w[layer], dn_a_log[layer],
                         dn_dt_bias[layer], dn_out_norm_w[layer], attn_q_norm_w[layer],
                         attn_k_norm_w[layer], w_dn_out[layer], w_attn_out[layer], w_o[layer],
                         norm2_w[layer], w_ffn_up[layer], ffn_conv_w[layer], w_ffn_down[layer])
    return x


DEPTH_2 = 2

CHUNK = 64
Q_BLOCK = 128
NORM_EPS = 1e-6
DA_HEADS = 4
DA_DK = 64
DA_DV = 2 * DA_DK
HG_HEADS = 4
HG_DK = 128
HG_DV = 128
ML_HEADS = 4
ML_DK = 128
ML_DV = 128
ML_CONV = 4
N_BRANCH = 3
BRANCH_W = 512
N_EXPERTS = 8
TOP_K = 2
N_DENSE = (DEPTH_2 + 1) // 2
N_MOE = DEPTH_2 // 2

A_QK = DA_HEADS * DA_DK
COLS = (('a_q1', A_QK), ('a_q2', A_QK), ('a_k1', A_QK), ('a_k2', A_QK),
        ('a_v', DA_HEADS * DA_DV),
        ('b_q', HG_HEADS * HG_DK), ('b_f', HG_HEADS * HG_DK),
        ('b_i', HG_HEADS * HG_DV), ('b_g', HG_HEADS * HG_DV),
        ('c_qk', 2 * ML_HEADS * ML_DK), ('c_v', ML_HEADS * ML_DV),
        ('c_o', ML_HEADS * ML_DV), ('c_i', ML_HEADS), ('c_f', ML_HEADS),
        ('gate', N_BRANCH * D_MODEL))
COL_NAMES = tuple(n for n, _ in COLS)
COL_OFFSETS = tuple(int(v) for v in np.cumsum([s for _, s in COLS])[:-1])
D_IN = sum(s for _, s in COLS)


def _rmsnorm(x, w):
    xf = x.astype(jnp.float32)
    y = xf * lax.rsqrt(jnp.mean(xf * xf, axis=-1, keepdims=True) + NORM_EPS)
    return (y * w.astype(jnp.float32)).astype(x.dtype)

def _modulate(xn, shift, scale):
    return xn * (1.0 + scale[:, None, :]) + shift[:, None, :]

def _swiglu(h, w1, w3, w2):
    return (jax.nn.silu(h @ w1) * (h @ w3)) @ w2

def _causal_conv(u, w, b):
    K = w.shape[0]
    S = u.shape[1]
    up = jnp.pad(u, ((0, 0), (K - 1, 0), (0, 0)))
    y = up[:, 0:S] * w[0] + b
    for j in range(1, K):
        y = y + up[:, j:j + S] * w[j]
    return y

def _diff_attention(q1, q2, k1, k2, v, lam, lam_init, qn_w, kn_w, subln_w):
    B, S, H, dk = q1.shape
    dv = v.shape[-1]
    f32 = jnp.float32
    q = _rmsnorm(jnp.stack([q1, q2], axis=2).astype(f32), qn_w) * (dk ** -0.5)
    k = _rmsnorm(jnp.stack([k1, k2], axis=2).astype(f32), kn_w)
    q = q.transpose(0, 3, 2, 1, 4)
    k = k.transpose(0, 3, 2, 1, 4)
    vf = v.astype(f32).transpose(0, 2, 1, 3)
    slopes = jnp.asarray(2.0 ** (-8.0 * np.arange(1, H + 1) / H), dtype=f32)
    kpos = jnp.arange(S)
    kchunk = kpos // CHUNK

    def block(j):
        start = j * Q_BLOCK
        qb = lax.dynamic_slice_in_dim(q, start, Q_BLOCK, axis=3)
        qpos = start + jnp.arange(Q_BLOCK)
        s = jnp.einsum('bhmqd,bhmkd->bhmqk', qb, k)
        dist = jnp.abs(qpos[:, None] - kpos[None, :]).astype(f32)
        mask = kchunk[None, :] <= (qpos // CHUNK)[:, None]
        s = jnp.where(mask, s - (slopes[:, None, None] * dist)[None, :, None], -jnp.inf)
        p = jax.nn.softmax(s, axis=-1)
        a = p[:, :, 0] - lam * p[:, :, 1]
        return jnp.einsum('bhqk,bhkd->bhqd', a, vf)

    o = lax.map(block, jnp.arange(S // Q_BLOCK))
    o = o.transpose(1, 0, 3, 2, 4).reshape(B, S, H, dv)
    o = _rmsnorm(o, subln_w) * (1.0 - lam_init)
    return o.reshape(B, S, H * dv).astype(v.dtype)

def _hgrn2(q, f_pre, i, g, lb, gnorm_w):
    B, S, H, dk = q.shape
    dv = i.shape[-1]
    n = S // CHUNK
    f32 = jnp.float32
    qf = jax.nn.silu(q.astype(f32))
    lb = lb.astype(f32).reshape(H, dk)
    logf = jnp.logaddexp(jnp.log(lb), jnp.log1p(-lb) + jax.nn.log_sigmoid(f_pre.astype(f32)))
    kf = -jnp.expm1(logf)
    vf = i.astype(f32)

    def to_chunks(t):
        return t.reshape(B, n, CHUNK, H, t.shape[-1]).transpose(1, 0, 3, 2, 4)

    causal = jnp.tril(jnp.ones((CHUNK, CHUNK), dtype=bool))

    def step(state, inp):
        qc, kc, vc, lfc = inp
        b = jnp.cumsum(lfc, axis=2)
        o_inter = jnp.einsum('bhtd,bhde->bhte', qc * jnp.exp(b), state)
        diff = b[:, :, :, None, :] - b[:, :, None, :, :]
        dec = jnp.exp(jnp.where(causal[:, :, None], diff, -jnp.inf))
        att = jnp.einsum('bhtd,bhsd,bhtsd->bhts', qc, kc, dec)
        o_intra = jnp.einsum('bhts,bhse->bhte', att, vc)
        b_last = b[:, :, -1:, :]
        state = (jnp.exp(b_last[:, :, 0, :])[..., None] * state
                 + jnp.einsum('bhsd,bhse->bhde', kc * jnp.exp(b_last - b), vc))
        return state, o_inter + o_intra

    s0 = jnp.zeros((B, H, dk, dv), f32)
    _, o = lax.scan(step, s0, (to_chunks(qf), to_chunks(kf), to_chunks(vf), to_chunks(logf)))
    o = o.transpose(1, 0, 3, 2, 4).reshape(B, S, H, dv)
    o = _rmsnorm(o, gnorm_w) * jax.nn.silu(g.astype(f32))
    return o.reshape(B, S, H * dv).astype(g.dtype)

def _mlstm(q, k, v, o_pre, i_pre, f_pre, norm_w):
    B, S, H, dk = q.shape
    dv = v.shape[-1]
    n = S // CHUNK
    f32 = jnp.float32
    qf = q.astype(f32)
    kf = k.astype(f32) * (dk ** -0.5)
    vf = v.astype(f32)
    ig = i_pre.astype(f32)
    lf = jax.nn.log_sigmoid(f_pre.astype(f32))

    def to_chunks(t):
        return t.reshape(B, n, CHUNK, H, t.shape[-1]).transpose(1, 0, 3, 2, 4)

    def gate_chunks(t):
        return t.reshape(B, n, CHUNK, H).transpose(1, 0, 3, 2)

    causal = jnp.tril(jnp.ones((CHUNK, CHUNK), dtype=bool))

    def step(carry, inp):
        C, nv, m = carry
        qc, kc, vc, igc, lfc = inp
        b = jnp.cumsum(lfc, axis=-1)
        log_d = jnp.where(causal, b[..., :, None] - b[..., None, :] + igc[..., None, :], -jnp.inf)
        log_inter = b + m[..., None]
        m_t = jnp.maximum(log_inter, jnp.max(log_d, axis=-1))
        w_intra = jnp.exp(log_d - m_t[..., None]) * jnp.einsum('bhtd,bhsd->bhts', qc, kc)
        w_inter = jnp.exp(log_inter - m_t)
        num = (w_inter[..., None] * jnp.einsum('bhtd,bhde->bhte', qc, C)
               + jnp.einsum('bhts,bhse->bhte', w_intra, vc))
        dot = w_inter * jnp.einsum('bhtd,bhd->bht', qc, nv) + jnp.sum(w_intra, axis=-1)
        h = num / jnp.maximum(jnp.abs(dot), jnp.exp(-m_t))[..., None]
        g = b[..., -1]
        log_w = g[..., None] - b + igc
        m_new = jnp.maximum(g + m, jnp.max(log_w, axis=-1))
        w_s = jnp.exp(log_w - m_new[..., None])
        decay = jnp.exp(g + m - m_new)
        C = decay[..., None, None] * C + jnp.einsum('bhs,bhsd,bhse->bhde', w_s, kc, vc)
        nv = decay[..., None] * nv + jnp.einsum('bhs,bhsd->bhd', w_s, kc)
        return (C, nv, m_new), h

    init = (jnp.zeros((B, H, dk, dv), f32), jnp.zeros((B, H, dk), f32), jnp.zeros((B, H), f32))
    _, h = lax.scan(step, init, (to_chunks(qf), to_chunks(kf), to_chunks(vf),
                                 gate_chunks(ig), gate_chunks(lf)))
    h = h.transpose(1, 0, 3, 2, 4).reshape(B, S, H, dv)
    h = _rmsnorm(h, norm_w) * jax.nn.sigmoid(o_pre.astype(f32))
    return h.reshape(B, S, H * dv).astype(v.dtype)

def _mixer(h, w_in, conv_w, conv_b, qn_w, kn_w, lq1, lk1, lq2, lk2, subln_w, lam_init,
           lb, gnorm_w, ib, fb, cnorm_w, w_branch, w_out):
    B, S, _ = h.shape
    f32 = jnp.float32
    parts = dict(zip(COL_NAMES, jnp.split(w_in, COL_OFFSETS, axis=1)))

    def proj(name):
        return h @ parts[name]

    def heads(t, nh):
        return t.reshape(B, S, nh, -1)

    lam = (jnp.exp(jnp.sum(lq1.astype(f32) * lk1.astype(f32)))
           - jnp.exp(jnp.sum(lq2.astype(f32) * lk2.astype(f32))) + lam_init)
    y_a = _diff_attention(heads(proj('a_q1'), DA_HEADS), heads(proj('a_q2'), DA_HEADS),
                          heads(proj('a_k1'), DA_HEADS), heads(proj('a_k2'), DA_HEADS),
                          heads(proj('a_v'), DA_HEADS), lam, lam_init, qn_w, kn_w, subln_w)
    y_b = _hgrn2(heads(proj('b_q'), HG_HEADS), heads(proj('b_f'), HG_HEADS),
                 heads(proj('b_i'), HG_HEADS), heads(proj('b_g'), HG_HEADS), lb, gnorm_w)
    qk = jax.nn.silu(_causal_conv(proj('c_qk'), conv_w, conv_b))
    c_q, c_k = jnp.split(qk, 2, axis=-1)
    y_c = _mlstm(heads(c_q, ML_HEADS), heads(c_k, ML_HEADS), heads(proj('c_v'), ML_HEADS),
                 heads(proj('c_o'), ML_HEADS), proj('c_i') + ib, proj('c_f') + fb, cnorm_w)
    gates = jax.nn.sigmoid(proj('gate')).reshape(B, S, N_BRANCH, D_MODEL)
    merged = (gates[:, :, 0] * (y_a @ w_branch[0])
              + gates[:, :, 1] * (y_b @ w_branch[1])
              + gates[:, :, 2] * (y_c @ w_branch[2]))
    return merged @ w_out

def _moe(h, router_w, router_b, w1, w3, w2):
    f32 = jnp.float32
    logits = (h @ router_w).astype(f32) + router_b.astype(f32)
    probs = jax.nn.softmax(logits, axis=-1)
    top_p, top_i = lax.top_k(probs, TOP_K)
    top_p = top_p / jnp.sum(top_p, axis=-1, keepdims=True)
    combine = jnp.sum(jax.nn.one_hot(top_i, N_EXPERTS, dtype=f32) * top_p[..., None], axis=-2)
    out = jnp.zeros_like(h)
    for e in range(N_EXPERTS):
        out = out + combine[..., e:e + 1].astype(h.dtype) * _swiglu(h, w1[e], w3[e], w2[e])
    return out

def second_inputs(seed: int = 0) -> dict:
    key = jax.random.key(seed)
    ks = jax.random.split(key, 32)
    f32 = jnp.float32
    D = D_MODEL

    def nrm(k, shape, scale):
        return scale * jax.random.normal(k, shape, f32)

    def gain(k, shape):
        return 1.0 + 0.02 * jax.random.normal(k, shape, f32)

    return {
        'x': nrm(ks[0], (BATCH, SEQ, D), 1.0),
        'c': nrm(ks[1], (BATCH, D), 1.0),
        'w_mod': nrm(ks[2], (DEPTH_2, D, 6 * D), 0.5 * D ** -0.5),
        'b_mod': nrm(ks[3], (DEPTH_2, 6 * D), 0.02),
        'norm1_w': gain(ks[4], (DEPTH_2, D)),
        'norm2_w': gain(ks[5], (DEPTH_2, D)),
        'w_in': nrm(ks[6], (DEPTH_2, D, D_IN), D ** -0.5),
        'c_conv_w': nrm(ks[7], (DEPTH_2, ML_CONV, 2 * ML_HEADS * ML_DK), ML_CONV ** -0.5),
        'c_conv_b': nrm(ks[8], (DEPTH_2, 2 * ML_HEADS * ML_DK), 0.02),
        'a_qnorm_w': gain(ks[9], (DEPTH_2, DA_DK)),
        'a_knorm_w': gain(ks[10], (DEPTH_2, DA_DK)),
        'a_lambda_q1': nrm(ks[11], (DEPTH_2, DA_DK), 0.1),
        'a_lambda_k1': nrm(ks[12], (DEPTH_2, DA_DK), 0.1),
        'a_lambda_q2': nrm(ks[13], (DEPTH_2, DA_DK), 0.1),
        'a_lambda_k2': nrm(ks[14], (DEPTH_2, DA_DK), 0.1),
        'a_subln_w': gain(ks[15], (DEPTH_2, DA_DV)),
        'b_lb_logits': nrm(ks[16], (DEPTH_2, HG_HEADS * HG_DK), 1.0),
        'b_gnorm_w': gain(ks[17], (DEPTH_2, HG_DV)),
        'c_igate_b': nrm(ks[18], (DEPTH_2, ML_HEADS), 0.1),
        'c_fgate_b': jnp.linspace(3.0, 6.0, ML_HEADS, dtype=f32)[None, :] + nrm(ks[19], (DEPTH_2, ML_HEADS), 0.1),
        'c_norm_w': gain(ks[20], (DEPTH_2, ML_DV)),
        'w_branch': nrm(ks[21], (DEPTH_2, N_BRANCH, BRANCH_W, D), BRANCH_W ** -0.5),
        'w_out': nrm(ks[22], (DEPTH_2, D, D), D ** -0.5),
        'ffn_w1': nrm(ks[23], (N_DENSE, D, D_FF), D ** -0.5),
        'ffn_w3': nrm(ks[24], (N_DENSE, D, D_FF), D ** -0.5),
        'ffn_w2': nrm(ks[25], (N_DENSE, D_FF, D), D_FF ** -0.5),
        'moe_router_w': nrm(ks[26], (N_MOE, D, N_EXPERTS), D ** -0.5),
        'moe_router_b': nrm(ks[27], (N_MOE, N_EXPERTS), 0.01),
        'moe_w1': nrm(ks[28], (N_MOE, N_EXPERTS, D, D_FF), D ** -0.5),
        'moe_w3': nrm(ks[29], (N_MOE, N_EXPERTS, D, D_FF), D ** -0.5),
        'moe_w2': nrm(ks[30], (N_MOE, N_EXPERTS, D_FF, D), D_FF ** -0.5),
    }

def second_block(x, c, w_mod, b_mod, norm1_w, norm2_w, w_in, c_conv_w, c_conv_b,
              a_qnorm_w, a_knorm_w, a_lambda_q1, a_lambda_k1, a_lambda_q2, a_lambda_k2,
              a_subln_w, b_lb_logits, b_gnorm_w, c_igate_b, c_fgate_b, c_norm_w,
              w_branch, w_out, ffn_w1, ffn_w3, ffn_w2,
              moe_router_w, moe_router_b, moe_w1, moe_w3, moe_w2):
    lb_all = jnp.cumsum(jax.nn.softmax(b_lb_logits.astype(jnp.float32), axis=0), axis=0)
    lb_all = lb_all - lb_all[:1]
    cond = jax.nn.silu(c)
    for l in range(DEPTH_2):
        mod = cond @ w_mod[l] + b_mod[l]
        sh1, sc1, g1, sh2, sc2, g2 = jnp.split(mod, 6, axis=-1)
        lam_init = 0.8 - 0.6 * math.exp(-0.3 * l)
        h = _modulate(_rmsnorm(x, norm1_w[l]), sh1, sc1)
        y = _mixer(h, w_in[l], c_conv_w[l], c_conv_b[l], a_qnorm_w[l], a_knorm_w[l],
                   a_lambda_q1[l], a_lambda_k1[l], a_lambda_q2[l], a_lambda_k2[l],
                   a_subln_w[l], lam_init, lb_all[l], b_gnorm_w[l],
                   c_igate_b[l], c_fgate_b[l], c_norm_w[l], w_branch[l], w_out[l])
        x = x + g1[:, None, :] * y
        h = _modulate(_rmsnorm(x, norm2_w[l]), sh2, sc2)
        if l % 2 == 0:
            i = l // 2
            y = _swiglu(h, ffn_w1[i], ffn_w3[i], ffn_w2[i])
        else:
            i = l // 2
            y = _moe(h, moe_router_w[i], moe_router_b[i], moe_w1[i], moe_w3[i], moe_w2[i])
        x = x + g2[:, None, :] * y
    return x


def setup_inputs(seed=0):
    out = dict(first_inputs(seed))
    for name, value in second_inputs(seed + 1).items():
        if name != "x":
            out[name + "_2"] = value
    return out


def reference(
    x, norm1_w, w_in, dn_conv_w, dn_a_log, dn_dt_bias, dn_out_norm_w, attn_q_norm_w,
    attn_k_norm_w, w_dn_out, w_attn_out, w_o, norm2_w, w_ffn_up, ffn_conv_w, w_ffn_down, c_2,
    w_mod_2, b_mod_2, norm1_w_2, norm2_w_2, w_in_2, c_conv_w_2, c_conv_b_2, a_qnorm_w_2,
    a_knorm_w_2, a_lambda_q1_2, a_lambda_k1_2, a_lambda_q2_2, a_lambda_k2_2, a_subln_w_2,
    b_lb_logits_2, b_gnorm_w_2, c_igate_b_2, c_fgate_b_2, c_norm_w_2, w_branch_2, w_out_2,
    ffn_w1_2, ffn_w3_2, ffn_w2_2, moe_router_w_2, moe_router_b_2, moe_w1_2, moe_w3_2, moe_w2_2,
):
    x = first_block(
        x, norm1_w, w_in, dn_conv_w, dn_a_log, dn_dt_bias, dn_out_norm_w, attn_q_norm_w,
        attn_k_norm_w, w_dn_out, w_attn_out, w_o, norm2_w, w_ffn_up, ffn_conv_w, w_ffn_down,
    )
    return second_block(
        x, c_2, w_mod_2, b_mod_2, norm1_w_2, norm2_w_2, w_in_2, c_conv_w_2, c_conv_b_2,
        a_qnorm_w_2, a_knorm_w_2, a_lambda_q1_2, a_lambda_k1_2, a_lambda_q2_2, a_lambda_k2_2,
        a_subln_w_2, b_lb_logits_2, b_gnorm_w_2, c_igate_b_2, c_fgate_b_2, c_norm_w_2,
        w_branch_2, w_out_2, ffn_w1_2, ffn_w3_2, ffn_w2_2, moe_router_w_2, moe_router_b_2,
        moe_w1_2, moe_w3_2, moe_w2_2,
    )


_drawn_inputs = setup_inputs


def setup_inputs(seed=0):
    import zlib

    import numpy as np

    out = dict(_drawn_inputs(seed))
    spreads = {}
    factors = {'attn_q_norm_w': 5.659,
     'attn_k_norm_w': 5.367,
     'norm1_w_2': 7.156,
     'norm2_w_2': 4.037,
     'c_conv_b_2': 200.0,
     'a_qnorm_w_2': 8.0,
     'a_knorm_w_2': 8.0,
     'a_lambda_q2_2': 6.724,
     'a_lambda_k2_2': 3.206,
     'a_subln_w_2': 44.078,
     'b_lb_logits_2': 5.346,
     'b_gnorm_w_2': 8.0,
     'c_igate_b_2': 64.0,
     'c_norm_w_2': 46.805,
     'moe_router_b_2': 20.791,
     'c_conv_w_2': 2.682,
     'a_lambda_q1_2': 8.0,
     'a_lambda_k1_2': 7.286}
    for name, (base, spread) in spreads.items():
        noise = np.random.default_rng([zlib.crc32(name.encode()), seed]).standard_normal(out[name].shape)
        drawn = base * np.exp(spread * noise) if base else spread * noise
        out[name] = __import__('jax').numpy.asarray(drawn.astype(out[name].dtype))
    for name, factor in factors.items():
        out[name] = (out[name] * factor).astype(out[name].dtype)
    return out
```

```python
from contextlib import ExitStack, contextmanager

import numpy as np

import concourse.bass as bass
from concourse import mybir

F32 = mybir.dt.float32
F32R = mybir.dt.float32r
I32 = mybir.dt.int32
ACT = mybir.ActivationFunctionType
ALU = mybir.AluOpType
AX = mybir.AxisListType

P = 128
S = 256
ST = S // P
D = 1024
KD = D // P
CH = 64
NCH = S // CH
DFF = 2816
NF = DFF // P
NE = 8
EPS = 1e-6
BIG = 1e30
BANK = 512
SLOT = 8
RAW = 11
SPLIT = 3
LOOK = 2
UPS = 2 * KD // SLOT
EXPERT_SLOTS = (2 * NF * KD + KD * NF) // SLOT

PAIRS0 = 4


def stream_plan():
    plan = [("dn_in", 16, "gemm"), ("att_in", 36, "gemm"), ("gates0", 2 * 4 * 3, "gemm"),
            ("out0", KD, "gemm"), ("ffn0", EXPERT_SLOTS, "gemm")]
    for l in (1, 2):
        plan += [(f"mod{l}", 48, "mod"), (f"a_in{l}", 12, "gemm"), (f"b_in{l}", 16, "gemm"),
                 (f"c_in{l}", 16, "gemm"), (f"gates{l}", 3 * 4 * 3, "gemm"), (f"out{l}", KD, "gemm"),
                 (f"ffn{l}", EXPERT_SLOTS * (NE if l == 2 else 1), "gemm")]
    return plan


class Kern:

    def __init__(self, nc, ctx, dram):
        self.nc, self.ctx, self.dram = nc, ctx, dram
        self.kind, self.index, self.start = [], [], {}
        seen = {"gemm": 0, "mod": 0}
        for name, slots, kind in stream_plan():
            self.start[name] = len(self.kind)
            for _ in range(slots):
                self.kind.append(kind)
                self.index.append(seen[kind])
                seen[kind] += 1
        self.slots = len(self.kind)
        self.to_clear = []
        self.loaded = self.hi_done = self.lo_done = 0

        self.x = self.sbuf("x", [P, KD, S])
        self.h = self.sbuf("h", [P, KD, S])
        self.h_hi = self.sbuf("h_hi", [P, KD, S], F32R)
        self.h_lo = self.sbuf("h_lo", [P, KD, S], F32R)
        self.raw = self.sbuf("raw_ring", [P, RAW, SLOT * P])
        self.w_hi = self.sbuf("w_hi_ring", [P, SPLIT, SLOT * P], F32R)
        self.w_lo = self.sbuf("w_lo_ring", [P, SPLIT, SLOT * P], F32R)
        self.ident = self.sbuf("ident", [P, P])
        self.ones = self.sbuf("ones", [P, P])
        self.head_ones = self.sbuf("head_ones", [P, P])
        self.eps = self.sbuf("eps", [P, 1])
        self.ps = ctx.enter_context(nc.psum_tensor("ps", [P, 8 * BANK], F32))
        self.raw_loaded = [ctx.enter_context(nc.semaphore(f"raw_loaded{i}")) for i in range(RAW)]
        self.hi_ready = ctx.enter_context(nc.semaphore("hi_ready"))
        self.slot_split = ctx.enter_context(nc.semaphore("slot_split"))
        self.slot_used = ctx.enter_context(nc.semaphore("slot_used"))
        self.mod_used = ctx.enter_context(nc.semaphore("mod_used"))
        self.outer = ctx

    def sbuf(self, name, shape, dt=F32, ctx=None):
        return (ctx or self.ctx).enter_context(self.nc.sbuf_tensor(name, shape, dt))

    def bank(self, i, n=1):
        return self.ps[:, i * BANK:(i + n) * BANK]

    def raw_ready(self, eng, n):
        eng.wait_ge(self.raw_loaded[n % RAW], 16 * (n // RAW + 1))

    def load_slots(self, sp, upto):
        for n in range(self.loaded, min(upto, self.slots)):
            if n >= RAW:
                m = n - RAW
                sp.wait_ge(self.mod_used if self.kind[m] == "mod" else self.slot_split, self.index[m] + 1)
            sp.dma_start(self.raw[:, n % RAW, :], self.dram["stream"][n]).then_inc(self.raw_loaded[n % RAW], 16)
        self.loaded = max(self.loaded, min(upto, self.slots))

    def run_end(self, n):
        while n < self.slots and self.kind[n] == "gemm":
            n += 1
        return n

    def split_hi(self, act, upto):
        for n in range(self.hi_done, upto):
            s = self.index[n]
            self.raw_ready(act, n)
            if s >= SPLIT:
                act.wait_ge(self.slot_used, s - SPLIT + 1)
            act.activation(self.w_hi[:, s % SPLIT, :], self.raw[:, n % RAW, :], ACT.Copy).then_inc(self.hi_ready, 1)
        self.hi_done = max(self.hi_done, upto)

    def split_lo(self, dve, upto):
        for n in range(self.lo_done, upto):
            s = self.index[n]
            self.raw_ready(dve, n)
            dve.wait_ge(self.hi_ready, s + 1)
            dve.tensor_tensor(self.w_lo[:, s % SPLIT, :], self.raw[:, n % RAW, :],
                              self.w_hi[:, s % SPLIT, :].bitcast(F32), ALU.subtract).then_inc(self.slot_split, 1)
        self.lo_done = max(self.lo_done, upto)


class Chain:

    def __init__(self, eng, sem):
        self.eng, self.sem, self.n = eng, sem, 0

    def __call__(self, ins):
        ins.then_inc(self.sem, 1)
        self.n += 1
        self.eng.wait_ge(self.sem, self.n)


@contextmanager
def stage(k, name):
    cleared = k.to_clear
    for s in cleared:
        k.nc.gpsimd.sem_clear(s)
    mine = []
    with ExitStack() as c:
        def sem(what):
            mine.append(k.nc.alloc_semaphore(f"{name}_{what}"))
            return mine[-1]

        def buf(what, shape, dt=F32):
            return k.sbuf(f"{name}_{what}", shape, dt, c)
        yield c.enter_context(k.nc.Block()), sem, buf
    for s in cleared:
        k.nc.release_semaphore(s)
    k.to_clear = mine


def bc(ap, shape):
    return ap.to_broadcast(shape)


def projection(k, name, phase, units, rhs, evac_act=None, evac_dve=None, flush_act=None, flush_dve=None,
               banks=4, first_bank=0, sems=(), bufs=(), freed=None):
    start = k.start[phase] if isinstance(phase, str) else phase
    ends, t = [], 0
    for kt in units:
        t += 2 * kt
        ends.append(start + (t + SLOT - 1) // SLOT)
    end = ends[-1]
    limit = k.run_end(start)
    with stage(k, name) as (block, sem, buf):
        s = {x: sem(x) for x in ("bank_freed", *sems)}
        b = {x: buf(x, sh) for x, sh in bufs}
        bank = lambda u: k.bank(first_bank + u % banks)

        @block.sync
        def _(sp):
            k.load_slots(sp, end + RAW)

        @block.scalar
        def _(act):
            for u in range(len(units)):
                k.split_hi(act, min(ends[u] + LOOK, limit))
                if evac_act:
                    act.wait_ge(k.slot_used, k.index[ends[u] - 1] + 1)
                    evac_act(act, u, bank(u), s, b)
            if flush_act:
                flush_act(act, s, b)

        @block.vector
        def _(dve):
            for u in range(len(units)):
                k.split_lo(dve, min(ends[u] + LOOK, limit))
                if evac_dve:
                    dve.wait_ge(k.slot_used, k.index[ends[u] - 1] + 1)
                    evac_dve(dve, u, bank(u), s, b)
            if flush_dve:
                flush_dve(dve, s, b)

        @block.tensor
        def _(pe):
            t = 0
            for u, kt in enumerate(units):
                if u >= banks and freed:
                    freed(pe, s, u - banks)
                elif u >= banks:
                    pe.wait_ge(s["bank_freed"], u - banks + 1)
                hi, lo = rhs(u)
                t = multiply_unit(k, pe, start, t, kt, hi, lo, bank(u))


def multiply_unit(k, pe, start, t, kt, hi, lo, out, split_at=None):
    for half in range(2):
        for kk in range(kt):
            n = start + t // SLOT
            i = k.index[n]
            if t % SLOT == 0:
                pe.wait_ge(k.slot_split, (split_at or (lambda v: v))(i + 1))
            w = bass.ts(t % SLOT, P)
            w_hi, w_lo = k.w_hi[:, i % SPLIT, w], k.w_lo[:, i % SPLIT, w]
            o = out[:, half * S:(half + 1) * S]
            pe.matmul(o, w_hi, hi[:, kk, :], start=(kk == 0), stop=False)
            pe.matmul(o, w_hi, lo[:, kk, :], start=False, stop=False)
            mm = pe.matmul(o, w_lo, hi[:, kk, :], start=False, stop=(kk == kt - 1))
            if t % SLOT == SLOT - 1:
                mm.then_inc(k.slot_used, 1)
            t += 1
    return t


def split_activation(eng, chain, src, hi, lo):
    chain(eng.tensor_copy(hi, src))
    chain(eng.tensor_tensor(lo, src, hi.bitcast(F32), ALU.subtract))


def norm_stream(k, name, scale, shift=None):
    with stage(k, name) as (block, sem, buf):
        sq, rs = buf("sq", [P, KD, S]), buf("rs", [P, S])
        lnv = buf("ln", [P, S])
        sq_ready, sum_ready, ln_ready, rs_ready, scaled, shifted, steps = map(
            sem, ("sq_ready", "sum_ready", "ln_ready", "rs_ready", "scaled", "shifted", "steps"))

        @block.gpsimd
        def _(pool):
            pool.tensor_tensor(sq[:, 4:8, :], k.x[:, 4:8, :], k.x[:, 4:8, :], ALU.mult).then_inc(sq_ready, 1)

        @block.vector
        def _(dve):
            dve.tensor_tensor(sq[:, 0:4, :], k.x[:, 0:4, :], k.x[:, 0:4, :], ALU.mult).then_inc(sq_ready, 1)
            dve.wait_ge(rs_ready, 1)
            for i in range(KD):
                dve.scalar_tensor_tensor(out=k.h[:, i, :], in0=k.x[:, i, :], scalar=scale[:, i:i + 1],
                                         in1=rs[:], op0=ALU.mult, op1=ALU.mult).then_inc(scaled, 1)
            if shift is None:
                dve.wait_ge(scaled, KD)
            else:
                dve.wait_ge(shifted, KD)
            split_activation(dve, Chain(dve, steps), k.h[:], k.h_hi[:], k.h_lo[:])

        @block.tensor
        def _(pe):
            pe.wait_ge(sq_ready, 2)
            for i in range(KD):
                mm = pe.matmul(k.ps[:, 0:S], k.ones[:], sq[:, i, :], start=(i == 0), stop=(i == KD - 1))
            mm.then_inc(sum_ready, 1)

        @block.scalar
        def _(act):
            act.wait_ge(sum_ready, 1)
            act.activation(lnv[:], k.ps[:, 0:S], ACT.Ln, scale=1.0 / D, bias=k.eps[:]).then_inc(ln_ready, 1)
            act.wait_ge(ln_ready, 1)
            act.activation(rs[:], lnv[:], ACT.Exp, scale=-0.5).then_inc(rs_ready, 1)
            if shift is not None:
                for i in range(KD):
                    act.wait_ge(scaled, i + 1)
                    act.activation(k.h[:, i, :], k.h[:, i, :], ACT.Identity, bias=shift[:, i:i + 1]).then_inc(shifted, 1)


def norm_heads(k, name, items, ones, width, n=4):
    with stage(k, name) as (block, sem, buf):
        sq = buf("sq", [P, 2, n * S])
        rs = buf("rs", [P, 2, n * S])
        sq_ready, sum_ready, ln_ready, rs_ready, done, steps = map(
            sem, ("sq_ready", "sum_ready", "ln_ready", "rs_ready", "done", "steps"))

        @block.gpsimd
        def _(pool):
            for g, (src, dst, w, after) in enumerate(items):
                if g >= 2:
                    pool.wait_ge(sum_ready, g - 1)
                pool.tensor_tensor(sq[:, g % 2, :], src, src, ALU.mult).then_inc(sq_ready, 1)

        @block.tensor
        def _(pe):
            for g in range(len(items)):
                pe.wait_ge(sq_ready, g + 1)
                if g >= 4:
                    pe.wait_ge(ln_ready, g - 3)
                for c in range(n * S // BANK):
                    mm = pe.matmul(k.bank((g % 4) * 2 + c), ones, sq[:, g % 2, bass.ts(c, BANK)],
                                   start=True, stop=True)
                mm.then_inc(sum_ready, 1)

        @block.scalar
        def _(act):
            for g in range(len(items)):
                act.wait_ge(sum_ready, g + 1)
                if g >= 2:
                    act.wait_ge(done, g - 1)
                act.activation(rs[:, g % 2, :], k.ps[:, (g % 4) * 2 * BANK:(g % 4) * 2 * BANK + n * S], ACT.Ln,
                               scale=1.0 / width, bias=k.eps[:]).then_inc(ln_ready, 1)
                act.wait_ge(ln_ready, g + 1)
                act.activation(rs[:, g % 2, :], rs[:, g % 2, :], ACT.Exp, scale=-0.5).then_inc(rs_ready, 1)

        @block.vector
        def _(dve):
            last = Chain(dve, steps)
            for g, (src, dst, w, after) in enumerate(items):
                dve.wait_ge(rs_ready, g + 1)
                ins = dve.scalar_tensor_tensor(out=dst, in0=src, scalar=w, in1=rs[:, g % 2, :],
                                               op0=ALU.mult, op1=ALU.mult)
                if after is None:
                    ins.then_inc(done, 1)
                else:
                    last(ins)
                    dve.tensor_tensor(dst, dst, after, ALU.mult).then_inc(done, 1)


def gated_branches(k, name, phase, branches, merged_hi, merged_lo):
    nb = len(branches)
    units = [KD, KD // 2] * (4 * nb)

    def rhs(u):
        return branches[(u // 2) % nb] if u % 2 else (k.h_hi[:], k.h_lo[:])

    def freed(pe, s, v):
        pe.wait_ge(s["product_done"] if v % 2 else s["gate_ready"], v // 2 + 1)

    def evac_act(act, u, ps, s, b):
        if u % 2 == 0:
            if u >= 4:
                act.wait_ge(s["product_done"], u // 2 - 1)
            act.activation(b["gate"][:, (u // 2) % 2, :], ps, ACT.Sigmoid).then_inc(s["gate_ready"], 1)

    def evac_dve(dve, u, ps, s, b):
        if u % 2 == 0:
            return
        g, dd, first, last = u // 2, u // 2 // nb, (u // 2) % nb == 0, (u // 2) % nb == nb - 1
        dve.wait_ge(s["gate_ready"], g + 1)
        acc = b["acc"][:]
        dve.tensor_tensor(acc if first else b["term"][:], ps, b["gate"][:, g % 2, :],
                          ALU.mult).then_inc(s["product_done"], 1)
        dve.wait_ge(s["product_done"], g + 1)
        if not first:
            dve.tensor_tensor(acc, acc, b["term"][:], ALU.add).then_inc(s["summed"], 1)
            dve.wait_ge(s["summed"], g - dd)
        if last:
            hi, lo = merged_hi[:, 2 * dd:2 * dd + 2, :], merged_lo[:, 2 * dd:2 * dd + 2, :]
            dve.tensor_copy(hi, acc).then_inc(s["merged"], 1)
            dve.wait_ge(s["merged"], 2 * dd + 1)
            dve.tensor_tensor(lo, acc, hi.bitcast(F32), ALU.subtract).then_inc(s["merged"], 1)
            dve.wait_ge(s["merged"], 2 * dd + 2)

    projection(k, name, phase, units, rhs, evac_act, evac_dve, freed=freed,
               sems=("gate_ready", "product_done", "summed", "merged"),
               bufs=(("gate", [P, 2, BANK]), ("acc", [P, BANK]), ("term", [P, BANK])))


def residual_projection(k, name, phase, units, hi, lo, gain=None, first_bank=0):
    def evac_dve(dve, u, ps, s, b):
        for half in range(2):
            i = 2 * u + half
            o = ps[:, half * S:(half + 1) * S]
            if gain is None:
                ins = dve.tensor_tensor(k.x[:, i, :], o, k.x[:, i, :], ALU.add)
            else:
                ins = dve.scalar_tensor_tensor(out=k.x[:, i, :], in0=o, scalar=gain[:, i:i + 1],
                                               in1=k.x[:, i, :], op0=ALU.mult, op1=ALU.add)
        ins.then_inc(s["bank_freed"], 1)

    projection(k, name, phase, units, lambda u: (hi, lo), None, evac_dve, first_bank=first_bank)


def plain_projection(k, name, phase, n_units, place):
    def evac_act(act, u, ps, s, b):
        dst, f = place(u)
        act.activation(dst, ps, f).then_inc(s["bank_freed"], 1)

    projection(k, name, phase, [KD] * n_units, lambda u: (k.h_hi[:], k.h_lo[:]), evac_act)


def conv_projection(k, name, phase, n_units, n_conv, place, taps, shift, bias=None):
    nt = len(taps)

    def evac_act(act, u, ps, s, b):
        if u >= n_conv:
            if u == n_conv:
                silu(act, u - 1, s, b)
            dst, f = place(u)
            act.activation(dst, ps, f).then_inc(s["bank_freed"], 1)
            return
        if u >= 2:
            act.wait_ge(s["silu_done"], u - 1)
        for half in range(2):
            i = 2 * u + half
            o, t = ps[:, half * S:(half + 1) * S], b["conv"][:, u % 2, half * S:(half + 1) * S]
            if bias is None:
                ins = act.activation(t, o, ACT.Copy, scale=taps[shift][:, i:i + 1])
            else:
                ins = act.activation(t, o, ACT.Identity, scale=taps[shift][:, i:i + 1], bias=bias[:, i:i + 1])
            ins.then_inc(s["centre"], 1)
        if u >= 1:
            silu(act, u - 1, s, b)

    def silu(act, u, s, b):
        act.wait_ge(s["bank_freed"], u + 1)
        act.activation(place(u)[0], b["conv"][:, u % 2, :], ACT.Silu).then_inc(s["silu_done"], 1)

    def flush_act(act, s, b):
        if n_conv == n_units:
            silu(act, n_units - 1, s, b)

    def evac_dve(dve, u, ps, s, b):
        if u >= n_conv:
            return
        dve.wait_ge(s["centre"], 2 * u + 2)
        for j in range(nt):
            if j == shift:
                continue
            d = j - shift
            for half in range(2):
                i = 2 * u + half
                a, z = max(0, -d), S - max(0, d)
                o = ps[:, half * S + a + d:half * S + z + d]
                t = b["conv"][:, u % 2, half * S + a:half * S + z]
                ins = dve.scalar_tensor_tensor(out=t, in0=o, scalar=taps[j][:, i:i + 1], in1=t,
                                               op0=ALU.mult, op1=ALU.add)
                ins.then_inc(s["tap"], 1)
                if half == 1 and (j, half) != last_tap:
                    tapped = 2 * (nt - 1) * u + 2 * (j + 1 - (j > shift))
                    dve.wait_ge(s["tap"], tapped)
        dve.wait_ge(s["tap"], 2 * (nt - 1) * (u + 1))
        dve.sem_inc(s["bank_freed"], 1)

    last_tap = (nt - 1 if shift != nt - 1 else nt - 2, 1)
    projection(k, name, phase, [KD] * n_units, lambda u: (k.h_hi[:], k.h_lo[:]), evac_act, evac_dve,
               flush_act=flush_act, sems=("centre", "tap", "silu_done"), bufs=(("conv", [P, 2, BANK]),))


def feed_forward(k, name, phase, gain=None, conv=None):
    with ExitStack() as c:
        g_hi = k.sbuf(f"{name}_g_hi", [P, NF, S], F32R, c)
        g_lo = k.sbuf(f"{name}_g_lo", [P, NF, S], F32R, c)

        def finish(dve, f, gate, up, s, b):
            g = b["g"][:, f % 2, :]
            dve.tensor_tensor(g, up, gate, ALU.mult).then_inc(s["product"], 1)
            dve.wait_ge(s["product"], f + 1)
            dve.tensor_copy(g_hi[:, f, :], g).then_inc(s["rounded"], 1)
            dve.wait_ge(s["rounded"], f + 1)
            dve.tensor_tensor(g_lo[:, f, :], g, g_hi[:, f, :].bitcast(F32), ALU.subtract).then_inc(s["g_split"], 1)

        if conv is None:
            def evac_act(act, f, ps, s, b):
                if f >= 2:
                    act.wait_ge(s["product"], f - 1)
                act.activation(b["gate"][:, f % 2, 0:S], ps[:, 0:S], ACT.Silu).then_inc(s["gate_ready"], 1)

            def evac_dve(dve, f, ps, s, b):
                dve.wait_ge(s["gate_ready"], f + 1)
                finish(dve, f, b["gate"][:, f % 2, 0:S], ps[:, S:2 * S], s, b)

            freed = lambda pe, s, v: pe.wait_ge(s["product"], v + 1)
            flush_act = flush_dve = None
        else:
            def silu(act, f, s, b):
                act.wait_ge(s["convolved"], f + 1)
                act.activation(b["gate"][:, f % 2, 0:S], b["gate"][:, f % 2, 0:S], ACT.Silu).then_inc(s["gate_ready"], 1)

            def evac_act(act, f, ps, s, b):
                if f >= 2:
                    act.wait_ge(s["product"], f - 1)
                for half in range(2):
                    act.activation(b["gate"][:, f % 2, half * S:(half + 1) * S], ps[:, half * S:(half + 1) * S],
                                   ACT.Copy, scale=conv[1][:, half * NF + f:half * NF + f + 1]).then_inc(s["centre"], 1)
                if f >= 1:
                    silu(act, f - 1, s, b)

            def product(dve, f, s, b):
                dve.wait_ge(s["gate_ready"], f + 1)
                t = b["gate"][:, f % 2, :]
                finish(dve, f, t[:, 0:S], t[:, S:2 * S], s, b)

            def evac_dve(dve, f, ps, s, b):
                dve.wait_ge(s["centre"], 2 * f + 2)
                t = b["gate"][:, f % 2, :]
                for j, (a, z) in ((0, (1, S)), (2, (0, S - 1))):
                    for half in range(2):
                        o = half * S
                        w = conv[j][:, half * NF + f:half * NF + f + 1]
                        ins = dve.scalar_tensor_tensor(out=t[:, o + a:o + z], in0=ps[:, o + a + j - 1:o + z + j - 1],
                                                       scalar=w, in1=t[:, o + a:o + z], op0=ALU.mult, op1=ALU.add)
                        ins.then_inc(s["tap"] if (j, half) != (2, 1) else s["convolved"], 1)
                    if j == 0:
                        dve.wait_ge(s["tap"], 3 * f + 2)
                dve.wait_ge(s["tap"], 3 * f + 3)
                dve.wait_ge(s["convolved"], f + 1)
                if f >= 1:
                    product(dve, f - 1, s, b)

            freed = lambda pe, s, v: pe.wait_ge(s["convolved"], v + 1)
            flush_act = lambda act, s, b: silu(act, NF - 1, s, b)
            flush_dve = lambda dve, s, b: product(dve, NF - 1, s, b)

        projection(k, f"{name}_up", phase, [KD] * NF, lambda u: (k.h_hi[:], k.h_lo[:]), evac_act, evac_dve,
                   flush_act, flush_dve, freed=freed,
                   sems=("centre", "tap", "convolved", "gate_ready", "product", "rounded", "g_split"),
                   bufs=(("gate", [P, 2, BANK]), ("g", [P, 2, S])))
        residual_projection(k, f"{name}_down", k.start[phase] + 2 * NF * KD // SLOT, [NF] * (KD // 2), g_hi[:], g_lo[:],
                            gain, first_bank=4)


def to_token_major(k, name, items):
    flat = [(src[:, t * P:(t + 1) * P], dst[t]) for src, dst in items for t in range(ST)]
    assert len(flat) <= 32
    with stage(k, name) as (block, sem, buf):
        transposed, moved = sem("transposed"), sem("moved")

        @block.tensor
        def _(pe):
            for i, (src, dst) in enumerate(flat):
                mm = pe.transpose(k.bank(i // 4 % 8)[:, bass.ts(i % 4, P)], src, k.ident[:])
                if i % 4 == 3:
                    mm.then_inc(transposed, 1)

        def move(e, q):
            def go(eng):
                for g in range(q, len(flat) // 4, 2):
                    eng.wait_ge(transposed, g + 1)
                    for i in range(4 * g, 4 * g + 4):
                        o = k.bank(g % 8)[:, bass.ts(i % 4, P)]
                        if e == "dve":
                            ins = eng.tensor_copy(flat[i][1], o)
                        else:
                            ins = eng.activation(flat[i][1], o, ACT.Copy)
                    ins.then_inc(moved, 1)
            return go

        block.vector(move("dve", 0))
        block.scalar(move("act", 1))


def window_attention(k, name, q, kk, vt, dist, o_hi, o_lo):
    G = 3
    H = 8
    slope = lambda g, h: 2.0 ** (-8.0 * (g * H + h + 1) / (G * H))
    its = [(hp, t, par) for hp in range(H // 2) for t in range(ST) for par in range(2)]
    n = len(its)
    with stage(k, name) as (block, sem, buf):
        sc = buf("scores", [P, 2, G * S])
        pt = buf("pt", [P, 2, 2 * G, P])
        out = buf("out", [P, H // 2, S])
        nmax, l, rl = buf("nmax", [P, 2]), buf("l", [P, 2]), buf("rl", [P, 2])
        qk_done, biased, max_ready, exp_done, recip, probs, turned, moved, pv_done, out_ready, rounded = map(
            sem, ("qk_done", "biased", "max_ready", "exp_done", "recip", "probs", "turned", "moved", "pv_done",
                  "out_ready", "rounded"))
        score = lambda i: k.bank(2 * its[i][2], 2)

        @block.tensor
        def _(pe):
            def qk(i):
                hp, t, par = its[i]
                if i >= 2:
                    pe.wait_ge(biased, G * (i - 1))
                rows = slice(64 * par, 64 * par + 64)
                for g in range(G):
                    mm = pe.matmul(score(i)[:, bass.ts(g, S)], q[rows, g * 4 + hp, bass.ts(t, P)],
                                   kk[rows, g * 4 + hp, :], start=True, stop=True)
                mm.then_inc(qk_done, 1)

            def turn(i):
                pe.wait_ge(probs, i + 1)
                if i >= 1:
                    pe.wait_ge(moved, 2 * i)
                for j in range(2 * G):
                    mm = pe.transpose(k.bank(4, 2)[:, bass.ts(j, P)], sc[:, i % 2, bass.ts(j, P)], k.ident[:])
                mm.then_inc(turned, 1)

            def pv(i):
                hp, t, par = its[i]
                pe.wait_ge(moved, 2 * i + 2)
                if i >= 2:
                    pe.wait_ge(out_ready, i - 1)
                for j in range(2 * G):
                    g, st = j // 2, j % 2
                    mm = pe.matmul(k.bank(6 + par)[64 * par:64 * par + 64, 0:P],
                                   vt[:, st, g * 4 + hp, 64 * par:64 * par + 64], pt[:, i % 2, j, :],
                                   start=(j == 0), stop=(j == 2 * G - 1))
                mm.then_inc(pv_done, 1)

            for i in range(n + 2):
                if i < n:
                    qk(i)
                if 1 <= i <= n:
                    turn(i - 1)
                if i >= 2:
                    pv(i - 2)

        @block.vector
        def _(dve):
            def bias(i):
                hp, t, par = its[i]
                dve.wait_ge(qk_done, i + 1)
                if i >= 2:
                    dve.wait_ge(turned, i - 1)
                for g in range(G):
                    dve.scalar_tensor_tensor(out=sc[:, i % 2, bass.ts(g, S)], in0=dist[:, t, g, :],
                                             scalar=-slope(g, 2 * hp + par), in1=score(i)[:, bass.ts(g, S)],
                                             op0=ALU.mult, op1=ALU.add).then_inc(biased, 1)
                dve.wait_ge(biased, G * (i + 1))
                dve.tensor_reduce(nmax[:, i % 2:i % 2 + 1], sc[:, i % 2, :], AX.X, ALU.max,
                                  negate=True).then_inc(max_ready, 1)

            def normalise(i):
                dve.wait_ge(exp_done, i + 1)
                dve.reciprocal(rl[:, i % 2:i % 2 + 1], l[:, i % 2:i % 2 + 1]).then_inc(recip, 1)
                dve.wait_ge(recip, i + 1)
                dve.tensor_scalar(sc[:, i % 2, :], sc[:, i % 2, :], rl[:, i % 2:i % 2 + 1], None,
                                  ALU.mult).then_inc(probs, 1)

            def store(i):
                hp, t, par = its[i]
                dve.wait_ge(pv_done, i + 1)
                dve.tensor_copy(out[64 * par:64 * par + 64, hp, bass.ts(t, P)],
                                k.bank(6 + par)[64 * par:64 * par + 64, 0:P]).then_inc(out_ready, 1)

            for i in range(n + 3):
                if i < n:
                    bias(i)
                if 1 <= i <= n:
                    normalise(i - 1)
                if i >= 3:
                    store(i - 3)
            dve.wait_ge(out_ready, n)
            split_activation(dve, Chain(dve, rounded), out[:], o_hi, o_lo)

        @block.scalar
        def _(act):
            def expo(i):
                act.wait_ge(max_ready, i + 1)
                act.activation(sc[:, i % 2, :], sc[:, i % 2, :], ACT.Exp, bias=nmax[:, i % 2:i % 2 + 1],
                               accum_out=l[:, i % 2:i % 2 + 1]).then_inc(exp_done, 1)

            def move(i):
                act.wait_ge(turned, i + 1)
                if i >= 2:
                    act.wait_ge(pv_done, i - 1)
                act.activation(pt[:, i % 2, 0:4, :], k.bank(4), ACT.Copy).then_inc(moved, 1)
                act.activation(pt[:, i % 2, 4:6, :], k.bank(5)[:, 0:2 * P], ACT.Copy).then_inc(moved, 1)

            for i in range(n + 1):
                if i < n:
                    expo(i)
                if i >= 1:
                    move(i - 1)


NU = NCH * PAIRS0
UW = NU * CH


def halves():
    for par in range(2):
        yield par, slice(64 * par, 64 * par + 64)


def dn_gates(k, wab, dtb, alog, g, beta):
    with stage(k, "dng") as (block, sem, buf):
        sa, sb, ab, e1, l1, e2, na = (buf(x, [P, 2, NU]) for x in ("sa", "sb", "abs", "e1", "l1", "e2", "na"))
        ea = buf("ea", [P, 8])
        projected, dsteps, asteps = map(sem, ("projected", "vector_steps", "scalar_steps"))
        o = k.bank(0)[:, 0:64].rearrange("q (c n d p) -> q c n d p", c=NCH, n=2, d=2)

        @block.tensor
        def _(pe):
            for c in range(NCH):
                for par, rows in halves():
                    for i in range(KD):
                        mm = pe.matmul(k.bank(0)[rows, bass.ts(c, 16)], k.h[:, i, bass.ts(c, CH)],
                                       wab[:, i, par, :], start=(i == 0), stop=(i == KD - 1))
            mm.then_inc(projected, 1)

        @block.vector
        def _(dve):
            step = Chain(dve, dsteps)
            dve.wait_ge(projected, 1)
            for d in range(2):
                step(dve.tensor_tensor(sa[:, d].rearrange("q (c p) -> q c p", c=NCH), o[:, :, 0, d, :],
                                       bc(dtb[:, 4 * d:4 * d + 4].unsqueeze(1), [P, NCH, 4]), ALU.add))
                step(dve.tensor_copy(sb[:, d].rearrange("q (c p) -> q c p", c=NCH), o[:, :, 1, d, :]))
            step(dve.scalar_tensor_tensor(out=ab[:], in0=sa[:], scalar=-1.0, in1=sa[:], op0=ALU.mult, op1=ALU.max))
            dve.wait_ge(asteps, 4)
            step(dve.scalar_tensor_tensor(out=l1[:], in0=sa[:], scalar=0.0, in1=l1[:], op0=ALU.max, op1=ALU.add))
            step(dve.tensor_scalar(ea[:], ea[:], -1.0, None, ALU.mult))
            for d in range(2):
                step(dve.tensor_tensor(g[:, d].rearrange("q (c p) -> q c p", c=NCH),
                                       l1[:, d].rearrange("q (c p) -> q c p", c=NCH),
                                       bc(ea[:, 4 * d:4 * d + 4].unsqueeze(1), [P, NCH, 4]), ALU.mult))
            step(dve.tensor_scalar(e2[:], e2[:], 1.0, None, ALU.add))
            step(dve.reciprocal(beta, e2[:]))

        @block.scalar
        def _(act):
            step = Chain(act, asteps)
            act.wait_ge(dsteps, 5)
            step(act.activation(e1[:], ab[:], ACT.Exp, scale=-1.0))
            step(act.activation(l1[:], e1[:], ACT.Ln, bias=1.0))
            step(act.activation(e2[:], sb[:], ACT.Exp, scale=-1.0))
            step(act.activation(ea[:], alog[:], ACT.Exp))


def dn_decays(k, c, g, beta, A, q, ee, bg):
    gm, decay, qd, bm = A["gm"], A["decay"], A["qd"], A["bm"]
    units = lambda t, d: t[:, d * UW:(d + 1) * UW].rearrange("q (u i) -> q u i", i=CH)
    with stage(k, "dnd") as (block, sem, buf):
        gm_ready, bm_ready, sums, exps, qd_done, ee_sum, ee_done = map(
            sem, ("gm_ready", "bm_ready", "sums", "exps", "qd_done", "ee_sum", "ee_done"))

        def spread(eng, dst, col, pattern, d, s):
            eng.tensor_tensor(units(dst, d), bc(col[:, d].unsqueeze(2), [P, NU, CH]),
                              bc(pattern.unsqueeze(1), [P, NU, CH]), ALU.mult).then_inc(s, 1)

        @block.gpsimd
        def _(pool):
            spread(pool, bm, beta, c["eye64"], 0, bm_ready)
            spread(pool, bm, beta, c["eye64"], 1, bm_ready)

        @block.vector
        def _(dve):
            spread(dve, gm, g, c["tri"][:, 0], 0, gm_ready)
            spread(dve, gm, g, c["tri"][:, 1], 1, gm_ready)
            for d in range(2):
                dve.wait_ge(exps, 3 + 3 * d)
                for p in range(PAIRS0):
                    u = units(qd, d).rearrange("q (c p) i -> q c p i", p=PAIRS0)[:, :, p, :]
                    dve.tensor_tensor(u, u, q[:, p, :].rearrange("q (c i) -> q c i", c=NCH), ALU.mult).then_inc(qd_done, 1)
            dve.wait_ge(ee_done, 1)
            dve.tensor_tensor(bg, beta, ee[:, 0], ALU.mult).then_inc(qd_done, 1)

        @block.tensor
        def _(pe):
            for d in range(2):
                pe.wait_ge(gm_ready, d + 1)
                for i in range(2):
                    mm = pe.matmul(k.bank(2 * d + i), c["seg"][:, d, :], gm[:, bass.ts(2 * d + i, BANK)],
                                   start=True, stop=True).then_inc(sums, 1)
                for i in range(2):
                    mm = pe.matmul(k.bank(4 + 2 * d + i), k.head_ones[:], gm[:, bass.ts(2 * d + i, BANK)],
                                   start=True, stop=True).then_inc(sums, 1)
            pe.wait_ge(exps, 1)
            for d in range(2):
                for i, m in enumerate((c["cum"][:, d, :], c["seg"][:, d, :], k.head_ones[:])):
                    mm = pe.matmul(k.bank(0)[:, (2 * i + d) * NU:(2 * i + d + 1) * NU], m, g[:, d, :],
                                   start=True, stop=True)
            mm.then_inc(ee_sum, 1)

        @block.scalar
        def _(act):
            for n, (d, what) in enumerate(((0, 0), (0, 1), (1, 0), (1, 1))):
                act.wait_ge(sums, 2 * n + 2)
                if what == 0:
                    for i in range(2):
                        act.activation(decay[:, bass.ts(2 * d + i, BANK)], k.bank(2 * d + i), ACT.Exp).then_inc(exps, 1)
                else:
                    act.activation(qd[:, d * UW:(d + 1) * UW], k.bank(4 + 2 * d, 2), ACT.Exp).then_inc(exps, 1)
            act.wait_ge(ee_sum, 1)
            act.activation(ee.rearrange("q a d u -> q (a d u)"), k.bank(0)[:, 0:6 * NU], ACT.Exp).then_inc(ee_done, 1)


def dn_systems(k, c, A, q, kk):
    decay, qk, bm = A["decay"], A["qk"], A["bm"]
    units = lambda t, d: t[:, d * UW:(d + 1) * UW].rearrange("q (u i) -> q u i", i=CH)
    with stage(k, "dns") as (block, sem, buf):
        betas, grams, steps = map(sem, ("betas", "grams", "steps"))

        @block.tensor
        def _(pe):
            for i in range(4):
                mm = pe.matmul(k.bank(i), k.head_ones[:], bm[:, bass.ts(i, BANK)], start=True, stop=True)
            mm.then_inc(betas, 1)
            for rhs, first in ((q, 6), (kk, 4)):
                for ch in range(NCH):
                    for p in range(PAIRS0):
                        u = ch * PAIRS0 + p
                        for par, rows in halves():
                            mm = pe.matmul(k.bank(first, 2)[rows, bass.ts(u, CH)], kk[rows, p, bass.ts(ch, CH)],
                                           rhs[rows, p, bass.ts(ch, CH)], start=True, stop=True)
                mm.then_inc(grams, 1)

        @block.vector
        def _(dve):
            step = Chain(dve, steps)
            for d in range(2):
                step(dve.tensor_tensor(units(decay, d), units(decay, d),
                                       bc(c["tri"][:, d].unsqueeze(1), [P, NU, CH]), ALU.mult))
            dve.wait_ge(betas, 1)
            dve.wait_ge(grams, 1)
            for d in range(2):
                w = slice(d * UW, (d + 1) * UW)
                step(dve.tensor_tensor(qk[:, w], k.bank(6, 2), decay[:, w], ALU.mult))
                step(dve.tensor_tensor(decay[:, w], k.bank(2 * d, 2), decay[:, w], ALU.mult))
            dve.wait_ge(grams, 2)
            for d in range(2):
                w = slice(d * UW, (d + 1) * UW)
                step(dve.tensor_tensor(decay[:, w], k.bank(4, 2), decay[:, w], ALU.mult))


def dn_inverse(k, c, A):
    b, y, t, rs, bl = A["decay"], A["y"], A["t"], A["r"], A["bl"]
    units = lambda x, d: x[:, d * UW:(d + 1) * UW].rearrange("q (u i) -> q u i", i=CH)
    levels = 6
    with stage(k, "dni") as (block, sem, buf):
        bl_ready, y_ready, t_ready, r_done, r_moved, z_done, zt_done = map(
            sem, ("bl_ready", "y_ready", "t_ready", "r_done", "r_moved", "z_done", "zt_done"))

        def each(f):
            for u in range(NU):
                for par, rows in halves():
                    mm = f(u, rows)
            return mm

        @block.gpsimd
        def _(pool):
            for l in range(levels):
                for d in range(2):
                    if l >= 2:
                        pool.wait_ge(r_done, 2 * (l - 1) + d + 1)
                    elif l == 1:
                        pool.wait_ge(y_ready, d + 1)
                    pool.tensor_tensor(units(bl, d), units(b, d), bc(c["lev"][:, d, l].unsqueeze(1), [P, NU, CH]),
                                       ALU.mult).then_inc(bl_ready, 1)

        @block.vector
        def _(dve):
            for d in range(2):
                dve.wait_ge(bl_ready, d + 1)
                dve.tensor_tensor(units(y, d), bc(c["eye64"].unsqueeze(1), [P, NU, CH]), units(bl, d),
                                  ALU.subtract).then_inc(y_ready, 1)
            for l in range(1, levels):
                for d in range(2):
                    w = slice(d * UW, (d + 1) * UW)
                    n = 2 * (l - 1) + d
                    dve.wait_ge(y_ready, n + 1)
                    if l < levels - 1:
                        dve.wait_ge(zt_done, n + 1)
                        dve.wait_ge(t_ready, n + 1)
                        dve.tensor_tensor(t[:, w], t[:, w], k.bank(6, 2), ALU.subtract).then_inc(t_ready, 1)
                    dve.wait_ge(z_done, n + 1)
                    dve.tensor_tensor(y[:, w], y[:, w], k.bank(4, 2), ALU.subtract).then_inc(y_ready, 1)

        @block.tensor
        def _(pe):
            def product(first, d, lhs, rhs):
                return each(lambda u, rows: pe.matmul(k.bank(first, 2)[rows, bass.ts(u, CH)],
                                                      lhs[rows, bass.ts(d * NU + u, CH)],
                                                      rhs[rows, bass.ts(d * NU + u, CH)] if rhs is not None
                                                      else c["eye64"][rows, :], start=True, stop=True))
            for d in range(2):
                pe.wait_ge(y_ready, d + 1)
                product(2 * d, d, y, None).then_inc(r_done, 1)
            for l in range(1, levels):
                for d in range(2):
                    n = 2 * l + d
                    pe.wait_ge(bl_ready, n + 1)
                    pe.wait_ge(t_ready, n - 1)
                    pe.wait_ge(r_moved, n - 1)
                    product(2 * d, d, bl, t).then_inc(r_done, 1)
                for d in range(2):
                    n = 2 * l + d
                    pe.wait_ge(r_moved, n + 1)
                    pe.wait_ge(y_ready, n)
                    if l < levels - 1:
                        product(6, d, y, rs).then_inc(zt_done, 1)
                    product(4, d, rs, y).then_inc(z_done, 1)

        @block.scalar
        def _(act):
            for l in range(levels):
                for d in range(2):
                    n = 2 * l + d
                    w = slice(d * UW, (d + 1) * UW)
                    act.wait_ge(r_done, n + 1)
                    if l == 0:
                        act.activation(t[:, w], k.bank(2 * d, 2), ACT.Copy).then_inc(t_ready, 1)
                        act.sem_inc(r_moved, 1)
                    else:
                        if l >= 2:
                            act.wait_ge(z_done, n - 3)
                        act.activation(rs[:, w], k.bank(2 * d, 2), ACT.Copy).then_inc(r_moved, 1)


def dn_prepare(k, c, A, ktm, vtm, kk, v, beta, ee, bg):
    y = A["y"]
    units = lambda x, d: x[:, d * UW:(d + 1) * UW].rearrange("q (u i) -> q u i", i=CH)
    with stage(k, "dnp") as (block, sem, buf):
        turned, moved, scaled, w_done, w_moved = map(sem, ("turned", "moved", "scaled", "w_done", "w_moved"))

        @block.tensor
        def _(pe):
            for first, src in ((0, kk), (2, v)):
                for ch in range(NCH):
                    for p in range(PAIRS0):
                        for par, rows in halves():
                            mm = pe.matmul(k.bank(first, 2)[rows, bass.ts(ch * PAIRS0 + p, CH)],
                                           src[rows, p, bass.ts(ch, CH)], c["eye64"][rows, :], start=True, stop=True)
                mm.then_inc(turned, 1)
            for d in range(2):
                pe.wait_ge(scaled, d + 1)
                for u in range(NU):
                    for par, rows in halves():
                        mm = pe.matmul(k.bank(4 + 2 * d, 2)[rows, bass.ts(u, CH)], A["kb"][rows, bass.ts(d * NU + u, CH)],
                                       y[rows, bass.ts(d * NU + u, CH)], start=True, stop=True)
                mm.then_inc(w_done, 1)

        @block.scalar
        def _(act):
            act.wait_ge(turned, 1)
            act.activation(ktm, k.bank(0, 2), ACT.Copy).then_inc(moved, 1)
            act.wait_ge(turned, 2)
            act.activation(vtm, k.bank(2, 2), ACT.Copy).then_inc(moved, 1)
            for d in range(2):
                act.wait_ge(w_done, d + 1)
                act.activation(A["wn"][:, d * UW:(d + 1) * UW], k.bank(4 + 2 * d, 2), ACT.Copy, scale=-1.0).then_inc(w_moved, 1)

        def scale(eng, dst, src, col, d):
            eng.tensor_tensor(units(dst, d), src.rearrange("q (u i) -> q u i", i=CH),
                              bc(col[:, d].unsqueeze(2), [P, NU, CH]), ALU.mult).then_inc(scaled, 1)

        @block.vector
        def _(dve):
            dve.wait_ge(moved, 1)
            for d in range(2):
                scale(dve, A["kb"], ktm, bg, d)
            dve.wait_ge(moved, 2)
            for d in range(2):
                scale(dve, A["vb"], vtm, beta, d)

        @block.gpsimd
        def _(pool):
            pool.wait_ge(scaled, 2)
            for d in range(2):
                scale(pool, A["kd"], ktm, ee[:, 1], d)


def dn_scan(k, A, ee, state, vn, o):
    y, vb, wn, qd, qk, kd = (A[x] for x in ("y", "vb", "wn", "qd", "qk", "kd"))
    with stage(k, "dnr") as (block, sem, buf):
        v_done, v_moved, o_done, o_added, up_done, decayed, state_ready = map(
            sem, ("v_done", "v_moved", "o_done", "o_added", "up_done", "decayed", "state_ready"))

        def cells(s):
            for d in range(2):
                ch = (s, NCH - 1 - s)[d]
                for p in range(PAIRS0):
                    u = (d * NCH + ch) * PAIRS0 + p
                    for par, rows in halves():
                        yield rows, bass.ts(d * PAIRS0 + p, CH), bass.ts(u, CH)

        @block.tensor
        def _(pe):
            for s in range(NCH):
                if s >= 1:
                    pe.wait_ge(state_ready, s)
                if s >= 2:
                    pe.wait_ge(v_moved, s - 1)
                for rows, w, u in cells(s):
                    mm = pe.matmul(k.bank(s % 2)[rows, w], y[rows, u], vb[rows, u], start=True, stop=(s == 0))
                    if s:
                        mm = pe.matmul(k.bank(s % 2)[rows, w], wn[rows, u], state[rows, w], start=False, stop=True)
                mm.then_inc(v_done, 1)
                pe.wait_ge(v_moved, s + 1)
                if s < NCH - 1:
                    for rows, w, u in cells(s):
                        mm = pe.matmul(k.bank(4 + s % 2)[rows, w], kd[rows, u], vn[rows, w], start=True, stop=True)
                    mm.then_inc(up_done, 1)
                if s >= 2:
                    pe.wait_ge(o_added, 2 * (s - 1))
                for rows, w, u in cells(s):
                    if s:
                        pe.matmul(k.bank(2 + s % 2)[rows, w], state[rows, w], qd[rows, u], start=True, stop=False)
                    mm = pe.matmul(k.bank(2 + s % 2)[rows, w], vn[rows, w], qk[rows, u], start=(s == 0), stop=True)
                mm.then_inc(o_done, 1)

        @block.scalar
        def _(act):
            for s in range(NCH):
                act.wait_ge(v_done, s + 1)
                if s >= 1:
                    act.wait_ge(o_done, s)
                act.activation(vn, k.bank(s % 2), ACT.Copy).then_inc(v_moved, 1)

        @block.vector
        def _(dve):
            n = 0
            for s in range(NCH):
                if s < NCH - 1:
                    dve.wait_ge(up_done, s + 1)
                    if s == 0:
                        dve.tensor_copy(state, k.bank(4)).then_inc(state_ready, 1)
                    else:
                        dve.wait_ge(o_done, s + 1)
                        for d in range(2):
                            ch = (s, NCH - 1 - s)[d]
                            sd = state[:, d * 256:(d + 1) * 256].rearrange("q (p v) -> q p v", v=64)
                            dve.tensor_tensor(sd, sd, bc(ee[:, 2, d, ch * 4:ch * 4 + 4].unsqueeze(2), [P, 4, 64]),
                                              ALU.mult).then_inc(decayed, 1)
                        dve.wait_ge(decayed, 2 * s)
                        dve.tensor_tensor(state, state, k.bank(4 + s % 2), ALU.add).then_inc(state_ready, 1)
                dve.wait_ge(o_done, s + 1)
                for d in range(2):
                    ch = (s, NCH - 1 - s)[d]
                    dst = o[:, :, bass.ts(ch, CH)]
                    src = k.bank(2 + s % 2)[:, d * 256:(d + 1) * 256].rearrange("q (p i) -> q p i", i=CH)
                    if s < 2:
                        dve.tensor_copy(dst, src).then_inc(o_added, 1)
                    else:
                        dve.wait_ge(o_added, 4)
                        dve.tensor_tensor(dst, dst, src, ALU.add).then_inc(o_added, 1)


def split_stage(k, name, src, hi, lo):
    with stage(k, name) as (block, sem, buf):
        steps = sem("steps")

        @block.vector
        def _(dve):
            split_activation(dve, Chain(dve, steps), src, hi, lo)


def load_stage(k, name, loads, prefetch=False):
    with stage(k, name) as (block, sem, buf):
        loaded = sem("loaded")

        if prefetch:
            @block.sync
            def _(sp):
                k.load_slots(sp, RAW)

        @block.scalar
        def _(act):
            for dst, src in loads:
                act.dma_start(dst, src).then_inc(loaded, 16)
            act.wait_ge(loaded, 16 * len(loads))


def first_block(k):
    d = k.dram
    with ExitStack() as c0:
        par = k.sbuf("cols0", [P, COLS0], F32, c0)
        col = {n: par[:, a:z] for n, (a, z) in COL0.items()}
        with ExitStack() as c1:
            y_hi = k.sbuf("mix_hi", [P, 2, 4, S], F32R, c1)
            y_lo = k.sbuf("mix_lo", [P, 2, 4, S], F32R, c1)
            with ExitStack() as c2:
                wab = k.sbuf("wab", [P, KD, 2, 16], F32, c2)
                tab = k.sbuf("dn_tables", [P, DN_TABLE], F32, c2)
                qkv = k.sbuf("qkv", [P, 12, S], F32, c2)
                z = k.sbuf("z", [P, 4, S], F32, c2)
                cols = k.sbuf("dn_cols", [P, 10, NU], F32, c2)
                load_stage(k, "load0", [(k.x[:], d["x_t"]), (par[:], d["cols0"]), (wab[:], d["wab"]), (tab[:], d["dn_tables"]),
                                        (k.ident[:], d["ident"]), (k.ones[:], d["ones"]), (k.head_ones[:], d["head_ones"]),
                                        (k.eps[:], d["eps"])], prefetch=True)
                c = {"seg": tab[:, 0:256].rearrange("q (d j) -> q d j", d=2),
                     "cum": tab[:, 256:512].rearrange("q (d j) -> q d j", d=2),
                     "tri": tab[:, 512:640].rearrange("q (d j) -> q d j", d=2),
                     "eye64": tab[:, 640:704],
                     "lev": tab[:, 704:1472].rearrange("q (d l j) -> q d l j", d=2, l=6)}
                norm_stream(k, "n01", col["norm1"])

                def place(u):
                    if u < 6:
                        return qkv[:, 2 * u:2 * u + 2, :], ACT.Silu
                    return z[:, 2 * u - 12:2 * u - 10, :], ACT.Silu
                taps = [col["dn_conv"][:, 12 * j:12 * j + 12] for j in range(3)]
                conv_projection(k, "dnx", "dn_in", 8, 6, place, taps, 1)
                q, kk, v = qkv[:, 0:4, :], qkv[:, 4:8, :], qkv[:, 8:12, :]
                fl = lambda t: t.rearrange("q a s -> q (a s)")
                norm_heads(k, "dnn", [(fl(q), fl(q), 64 ** -0.5, None), (fl(kk), fl(kk), 1.0, None)],
                           k.head_ones[:], 1.0)
                cc = cols[:]
                g, beta, bg = cc[:, 0:2], cc[:, 2:4], cc[:, 4:6]
                with ExitStack() as c3:
                    ee_t = k.sbuf("dn_ee", [P, 3, 2, NU], F32, c3)
                    ee = ee_t[:]
                    names = ("a0", "a1", "a2", "a3", "a4", "a5", "a6")
                    a = {n: k.sbuf(f"dn_{n}", [P, 2 * UW], F32, c3) for n in names}
                    A = {"gm": a["a0"], "bm": a["a1"], "decay": a["a2"], "qk": a["a3"], "qd": a["a4"],
                         "y": a["a0"], "t": a["a1"], "r": a["a5"], "bl": a["a6"],
                         "kb": a["a1"], "vb": a["a2"], "kd": a["a5"], "wn": a["a6"]}
                    dn_gates(k, wab, col["dtb"], col["alog"], g, beta)
                    dn_decays(k, c, g, beta, A, q, ee, bg)
                    dn_systems(k, c, A, q, kk)
                    dn_inverse(k, c, A)
                    ktm = k.sbuf("dn_ktm", [P, UW], F32, c3)
                    vtm = fl(q)
                    dn_prepare(k, c, A, ktm[:], vtm, kk, v, beta, ee, bg)
                    state, vn = fl(qkv[:, 4:6, :]), fl(qkv[:, 6:8, :])
                    dn_scan(k, A, ee, state, vn, v)
                norm_heads(k, "dno", [(fl(v), fl(v), col["dn_norm"], fl(z[:]))], k.head_ones[:], 64.0)
                split_stage(k, "dnsplit", v, y_hi[:, 0], y_lo[:, 0])
            with ExitStack() as c2:
                dist = k.sbuf("att_dist", [P, ST, 3, S], F32, c2)
                qt = k.sbuf("att_q", [P, 12, S], F32, c2)
                kt = k.sbuf("att_k", [P, 12, S], F32, c2)
                load_stage(k, "load1", [(dist[:], d["att_dist"])])
                vt = k.sbuf("att_vt", [P, ST, 12, P], F32, c2)
                with ExitStack() as c3:
                    vf = k.sbuf("att_v", [P, 12, S], F32, c3)
                    dst = (qt, kt, vf)
                    plain_projection(k, "atx", "att_in", 18,
                                     lambda u: (dst[u // 6][:, 2 * (u % 6):2 * (u % 6) + 2, :], ACT.Copy))
                    to_token_major(k, "att", [(vf[:, i, :], [vt[:, t, i, :] for t in range(ST)]) for i in range(12)])
                items = [(fl(t[:, 4 * i:4 * i + 4, :]), fl(t[:, 4 * i:4 * i + 4, :]), col[w], None)
                         for t, w in ((qt, "qn"), (kt, "kn")) for i in range(3)]
                norm_heads(k, "atn", items, k.head_ones[:], 64.0)
                scale_columns(k, "ats", qt[:], 64 ** -0.5)
                window_attention(k, "atw", qt[:], kt[:], vt[:], dist[:], y_hi[:, 1], y_lo[:, 1])
            with ExitStack() as c2:
                m_hi = k.sbuf("merged_hi", [P, KD, S], F32R, c2)
                m_lo = k.sbuf("merged_lo", [P, KD, S], F32R, c2)
                gated_branches(k, "gb0", "gates0", [(y_hi[:, i], y_lo[:, i]) for i in range(2)], m_hi, m_lo)
                residual_projection(k, "wo0", "out0", [KD] * 4, m_hi[:], m_lo[:])
        norm_stream(k, "n02", col["norm2"])
        feed_forward(k, "ff0", "ffn0", conv=[col["ffn_conv"][:, 2 * NF * j:2 * NF * (j + 1)] for j in range(3)])


def scale_columns(k, name, t, by):
    with stage(k, name) as (block, sem, buf):
        scaled = sem("scaled")

        @block.vector
        def _(dve):
            dve.tensor_scalar(t, t, by, None, ALU.mult).then_inc(scaled, 1)


def modulation(k, name, phase, cond, bias, mod):
    start = k.start[phase]
    k.hi_done = k.lo_done = start + 48
    with stage(k, name) as (block, sem, buf):
        cs = buf("cond", [P, KD])
        cond_ready, product = sem("cond_ready"), sem("product")

        @block.sync
        def _(sp):
            k.load_slots(sp, start + 48 + RAW)

        @block.scalar
        def _(act):
            act.activation(cs[:], cond, ACT.Silu).then_inc(cond_ready, 1)

        @block.tensor
        def _(pe):
            pe.wait_ge(cond_ready, 1)
            for f in range(48):
                k.raw_ready(pe, start + f)
                for i in range(KD):
                    mm = pe.matmul(k.bank(0)[:, f:f + 1], k.raw[:, (start + f) % RAW, bass.ts(i, P)], cs[:, i:i + 1],
                                   start=(i == 0), stop=(i == KD - 1))
                mm.then_inc(k.mod_used, 1)

        @block.vector
        def _(dve):
            dve.wait_ge(k.mod_used, k.index[start + 47] + 1)
            dve.tensor_tensor(mod, k.bank(0)[:, 0:48], bias, ALU.add).then_inc(product, 1)


def block_columns(k, name, col, mod, out, lam, lam_init, lb, layer):
    with stage(k, name) as (block, sem, buf):
        prod, sums, ex = buf("prod", [P, 2, 64]), buf("sums", [P, 2]), buf("ex", [P, 2])
        lo, e, tot, r = buf("lmax", [P, 4]), buf("e", [P, 2, 4]), buf("tot", [P, 4]), buf("r", [P, 4])
        vsteps, ssteps = sem("vector_steps"), sem("scalar_steps")
        lbv, ln1m, lnlb, one_m, inf = (lb[:, i] for i in range(5))

        @block.vector
        def _(dve):
            step = Chain(dve, vsteps)
            for i in range(2):
                step(dve.tensor_tensor(prod[:, i, :], lam[:, 2 * i, :], lam[:, 2 * i + 1, :], ALU.mult))
            step(dve.tensor_reduce(sums[:], prod[:], AX.X, ALU.add))
            step(dve.tensor_tensor(lo[:], col["lb0"], col["lb1"], ALU.max))
            step(dve.tensor_tensor(e[:, 0, :], col["lb0"], lo[:], ALU.subtract))
            step(dve.tensor_tensor(e[:, 1, :], col["lb1"], lo[:], ALU.subtract))
            for i, (norm, sc) in enumerate((("norm1", 8), ("norm2", 32))):
                step(dve.scalar_tensor_tensor(out=out["scale"][:, 8 * i:8 * i + 8], in0=mod[:, sc:sc + 8], scalar=1.0,
                                              in1=col[norm], op0=ALU.add, op1=ALU.mult))
            dve.wait_ge(ssteps, 2)
            step(dve.tensor_tensor(out["lam"], ex[:, 1:2], ex[:, 0:1], ALU.subtract))
            step(dve.tensor_scalar(out["lam"], out["lam"], -lam_init, None, ALU.add))
            step(dve.tensor_scalar(out["subln"], col["subln"], 1.0 - lam_init, None, ALU.mult))
            step(dve.tensor_tensor(tot[:], e[:, 0, :], e[:, 1, :], ALU.add))
            step(dve.reciprocal(r[:], tot[:]))
            step(dve.tensor_tensor(e[:, 0, :], e[:, 0, :], r[:], ALU.mult))
            step(dve.tensor_tensor(e[:, 1, :], e[:, 1, :], r[:], ALU.mult))
            if layer == 1:
                step(dve.memset(lbv, 0.0))
            else:
                step(dve.tensor_tensor(tot[:], e[:, 0, :], e[:, 1, :], ALU.add))
                step(dve.tensor_tensor(lbv, tot[:], e[:, 0, :], ALU.subtract))
            step(dve.tensor_scalar(one_m, lbv, -1.0, 1.0, ALU.mult, ALU.add))
            step(dve.tensor_scalar(ln1m, one_m, 1e-18, None, ALU.max))
            step(dve.tensor_scalar(lnlb, lbv, 1e-18, None, ALU.max))
            step(dve.tensor_scalar(inf, lbv, 1e-18, -BIG, ALU.is_lt, ALU.mult))
            dve.wait_ge(ssteps, 4)
            step(dve.tensor_tensor(lnlb, lnlb, inf, ALU.add))

        @block.scalar
        def _(act):
            step = Chain(act, ssteps)
            act.wait_ge(vsteps, 6)
            step(act.activation(ex[:], sums[:], ACT.Exp))
            step(act.activation(e[:], e[:], ACT.Exp))
            act.wait_ge(vsteps, 8 + 7 + (1 if layer == 1 else 2) + 4)
            step(act.activation(ln1m, ln1m, ACT.Ln))
            step(act.activation(lnlb, lnlb, ACT.Ln))


def diff_attention(k, name, qk, vt, dist, nlam, out):
    H = 4
    slope = lambda h: 2.0 ** (-8.0 * (h + 1) / H)
    its = [(h, t) for h in range(H) for t in range(ST)]
    n = len(its)
    with stage(k, name) as (block, sem, buf):
        sc, a = buf("scores", [P, 2, 2 * S]), buf("a", [P, 2, S])
        pt = buf("pt", [P, 2, 2, P])
        nmax, l, rl = buf("nmax", [P, 2, 2]), buf("l", [P, 2, 2]), buf("rl", [P, 2, 2])
        qk_done, biased, max_ready, exp_done, steps, combined, turned, moved, pv_done, out_ready = map(
            sem, ("qk_done", "biased", "max_ready", "exp_done", "steps", "combined", "turned", "moved", "pv_done",
                  "out_ready"))

        @block.tensor
        def _(pe):
            def scores(i):
                h, t = its[i]
                if i >= 2:
                    pe.wait_ge(biased, i - 1)
                rows = slice(64 * (h % 2), 64 * (h % 2) + 64)
                for m in range(2):
                    mm = pe.matmul(k.bank(i % 2)[:, bass.ts(m, S)], qk[rows, 2 * m + h // 2, bass.ts(t, P)],
                                   qk[rows, 4 + 2 * m + h // 2, :], start=True, stop=True)
                mm.then_inc(qk_done, 1)

            def turn(i):
                pe.wait_ge(combined, i + 1)
                if i >= 2:
                    pe.wait_ge(moved, i - 1)
                for j in range(2):
                    mm = pe.transpose(k.bank(2 + i % 2)[:, bass.ts(j, P)], a[:, i % 2, bass.ts(j, P)], k.ident[:])
                mm.then_inc(turned, 1)

            def pv(i):
                h, t = its[i]
                pe.wait_ge(moved, i + 1)
                if i >= 2:
                    pe.wait_ge(out_ready, i - 1)
                for j in range(2):
                    mm = pe.matmul(k.bank(4 + i % 2)[:, 0:P], vt[:, j, h, :], pt[:, i % 2, j, :],
                                   start=(j == 0), stop=(j == 1))
                mm.then_inc(pv_done, 1)

            for i in range(n + 2):
                if i < n:
                    scores(i)
                if 1 <= i <= n:
                    turn(i - 1)
                if i >= 2:
                    pv(i - 2)

        @block.vector
        def _(dve):
            step = Chain(dve, steps)

            def bias(i):
                h, t = its[i]
                dve.wait_ge(qk_done, i + 1)
                if i >= 2:
                    dve.wait_ge(combined, i - 1)
                s = sc[:, i % 2, :].rearrange("p (m s) -> p m s", m=2)
                dve.scalar_tensor_tensor(out=s, in0=bc(dist[:, t, :].unsqueeze(1), [P, 2, S]), scalar=-slope(h),
                                         in1=k.bank(i % 2).rearrange("p (m s) -> p m s", m=2),
                                         op0=ALU.mult, op1=ALU.add).then_inc(biased, 1)
                dve.wait_ge(biased, i + 1)
                dve.tensor_reduce(nmax[:, i % 2, :], s, AX.X, ALU.max, negate=True).then_inc(max_ready, 1)

            def combine(i):
                dve.wait_ge(exp_done, 2 * i + 2)
                if i >= 2:
                    dve.wait_ge(turned, i - 1)
                r = rl[:, i % 2, :]
                step(dve.reciprocal(r, l[:, i % 2, :]))
                step(dve.tensor_tensor(r[:, 1:2], r[:, 1:2], nlam, ALU.mult))
                s = sc[:, i % 2, :]
                step(dve.tensor_scalar(s[:, 0:S], s[:, 0:S], r[:, 0:1], None, ALU.mult))
                dve.scalar_tensor_tensor(out=a[:, i % 2, :], in0=s[:, S:2 * S], scalar=r[:, 1:2], in1=s[:, 0:S],
                                         op0=ALU.mult, op1=ALU.add).then_inc(combined, 1)

            def store(i):
                h, t = its[i]
                dve.wait_ge(pv_done, i + 1)
                dve.tensor_copy(out[:, h, bass.ts(t, P)], k.bank(4 + i % 2)[:, 0:P]).then_inc(out_ready, 1)

            for i in range(n + 3):
                if i < n:
                    bias(i)
                if 1 <= i <= n:
                    combine(i - 1)
                if i >= 3:
                    store(i - 3)

        @block.scalar
        def _(act):
            for i in range(n + 1):
                if i < n:
                    act.wait_ge(max_ready, i + 1)
                    for m in range(2):
                        act.activation(sc[:, i % 2, bass.ts(m, S)], sc[:, i % 2, bass.ts(m, S)], ACT.Exp,
                                       bias=nmax[:, i % 2, m:m + 1], accum_out=l[:, i % 2, m:m + 1]).then_inc(exp_done, 1)
                if i >= 1:
                    act.wait_ge(turned, i)
                    if i >= 3:
                        act.wait_ge(pv_done, i - 2)
                    act.activation(pt[:, (i - 1) % 2, :, :], k.bank(2 + (i - 1) % 2)[:, 0:2 * P], ACT.Copy).then_inc(moved, 1)


def gated_recurrence(k, name, q, f, vt, lb, tab, out):
    HW = 4 * S
    lbv, ln1m, lnlb, one_m, inf = (lb[:, i] for i in range(5))
    with ExitStack() as c:
        mk = lambda x, w=HW: k.sbuf(f"{name}_{x}", [P, w], F32, c)
        ls, kf, b, t1 = mk("ls"), mk("k"), mk("b"), mk("t1")
        reset = mk("reset")
        hs = lambda t: t.rearrange("p (h s) -> p h s", h=4)
        with stage(k, name + "g") as (block, sem, buf):
            vsteps, ssteps, made = sem("vector_steps"), sem("scalar_steps"), sem("reset_made")
            cb = lambda a: bc(a.unsqueeze(2), [P, 4, S])

            @block.gpsimd
            def _(pool):
                pool.memset(reset[:], 1.0).then_inc(made, 1)
                pool.wait_ge(made, 1)
                pool.memset(hs(reset[:])[:, :, 0:1], 0.0).then_inc(made, 1)

            @block.vector
            def _(dve):
                step = Chain(dve, vsteps)
                step(dve.scalar_tensor_tensor(out=t1[:], in0=f, scalar=-1.0, in1=f, op0=ALU.mult, op1=ALU.max))
                dve.wait_ge(ssteps, 2)
                step(dve.scalar_tensor_tensor(out=ls[:], in0=f, scalar=0.0, in1=t1[:], op0=ALU.min, op1=ALU.subtract))
                step(dve.tensor_tensor(kf[:], ls[:], f, ALU.subtract))
                step(dve.tensor_tensor(hs(ls[:]), hs(ls[:]), cb(ln1m), ALU.add))
                step(dve.tensor_tensor(hs(b[:]), hs(ls[:]), cb(lnlb), ALU.subtract))
                step(dve.scalar_tensor_tensor(out=t1[:], in0=b[:], scalar=-1.0, in1=b[:], op0=ALU.mult, op1=ALU.max))
                step(dve.tensor_tensor(hs(ls[:]), hs(ls[:]), cb(lnlb), ALU.max))
                dve.wait_ge(ssteps, 5)
                step(dve.tensor_tensor(ls[:], ls[:], t1[:], ALU.add))
                step(dve.tensor_tensor(hs(kf[:]), hs(kf[:]), cb(one_m), ALU.mult))
                dve.wait_ge(made, 2)
                step(dve.tensor_tensor_scan(b[:], reset[:], ls[:], 0.0, ALU.mult, ALU.add))

            @block.scalar
            def _(act):
                step = Chain(act, ssteps)
                act.wait_ge(vsteps, 1)
                step(act.activation(t1[:], t1[:], ACT.Exp, scale=-1.0))
                step(act.activation(t1[:], t1[:], ACT.Ln, bias=1.0))
                act.wait_ge(vsteps, 3)
                step(act.activation(kf[:], kf[:], ACT.Exp))
                act.wait_ge(vsteps, 6)
                step(act.activation(t1[:], t1[:], ACT.Exp, scale=-1.0))
                step(act.activation(t1[:], t1[:], ACT.Ln, bias=1.0))
        levels = 8
        with stage(k, name + "l") as (block, sem, buf):
            att = buf("att", [P, 8, P])
            cross = buf("cross", [P, 4, P])
            dd, ke, qe = buf("dd", [P, 2, HW]), buf("ke", [P, 2, HW]), buf("qe", [P, 2, HW])
            dd_ready, abs_ready, e_ready, ke_ready, qe_ready, att_done, taken, crossed, pv_done, out_ready = map(
                sem, ("dd_ready", "abs_ready", "e_ready", "ke_ready", "qe_ready", "att_done", "taken", "crossed",
                      "pv_done", "out_ready"))

            @block.vector
            def _(dve):
                def diff(j):
                    half = 1 << j
                    blocks = b[:].rearrange("p (n w) -> p n w", w=2 * half)
                    if j >= 2:
                        dve.wait_ge(qe_ready, j - 1)
                        dve.wait_ge(ke_ready, j - 1)
                    dve.tensor_tensor(dd[:, j % 2, :].rearrange("p (n w) -> p n w", w=2 * half), blocks,
                                      bc(blocks[:, :, half - 1:half], [P, HW // (2 * half), 2 * half]),
                                      ALU.subtract).then_inc(dd_ready, 1)

                def take(j):
                    dve.wait_ge(att_done, j + 2)
                    src = k.bank(2 * ((j + 1) % 3), 2).rearrange("p (n t) -> p n t", n=8)
                    if j < 0:
                        dve.tensor_tensor(att[:], src, bc(tab["ident"].unsqueeze(1), [P, 8, P]), ALU.mult).then_inc(taken, 1)
                    else:
                        dve.wait_ge(taken, j + 1)
                        dve.copy_predicated(att[:], bc(tab["lev"][:, j, :].bitcast(I32).unsqueeze(1), [P, 8, P]),
                                            src).then_inc(taken, 1)

                diff(0)
                for j in range(levels):
                    if j + 1 < levels:
                        diff(j + 1)
                    dve.wait_ge(e_ready, j + 1)
                    if j >= 2:
                        dve.wait_ge(att_done, j)
                    dve.tensor_tensor(ke[:, j % 2, :], kf[:], dd[:, j % 2, :], ALU.mult).then_inc(ke_ready, 1)
                    if j >= 1:
                        take(j - 2)
                take(levels - 2)
                for g in range(2):
                    dve.wait_ge(pv_done, g + 1)
                    dve.tensor_copy(out[:, 2 * g:2 * g + 2, :], k.bank(6 + g)).then_inc(out_ready, 1)

            @block.scalar
            def _(act):
                for j in range(levels):
                    act.wait_ge(dd_ready, j + 1)
                    act.activation(dd[:, j % 2, :], dd[:, j % 2, :], ACT.Abs).then_inc(abs_ready, 1)
                    act.wait_ge(abs_ready, j + 1)
                    act.activation(dd[:, j % 2, :], dd[:, j % 2, :], ACT.Exp, scale=-1.0).then_inc(e_ready, 1)
                act.wait_ge(att_done, levels + 1)
                act.activation(cross[:], k.bank(2 * (levels % 3)), ACT.Copy).then_inc(crossed, 1)

            @block.gpsimd
            def _(pool):
                for j in range(levels):
                    pool.wait_ge(e_ready, j + 1)
                    if j >= 2:
                        pool.wait_ge(att_done, j)
                    pool.tensor_tensor(qe[:, j % 2, :], q, dd[:, j % 2, :], ALU.mult).then_inc(qe_ready, 1)

            @block.tensor
            def _(pe):
                for j in range(-1, levels):
                    if j >= 0:
                        pe.wait_ge(ke_ready, j + 1)
                        pe.wait_ge(qe_ready, j + 1)
                    if j >= 2:
                        pe.wait_ge(taken, j - 1)
                    first = 2 * ((j + 1) % 3)
                    ks, qs = (kf[:], q) if j < 0 else (ke[:, j % 2, :], qe[:, j % 2, :])
                    if j < levels - 1:
                        for i in range(8):
                            mm = pe.matmul(k.bank(first, 2)[:, bass.ts(i, P)], ks[:, bass.ts(i, P)], qs[:, bass.ts(i, P)],
                                           start=True, stop=True)
                    else:
                        for h in range(4):
                            mm = pe.matmul(k.bank(first)[:, bass.ts(h, P)], ks[:, bass.ts(2 * h, P)],
                                           qs[:, bass.ts(2 * h + 1, P)], start=True, stop=True)
                    mm.then_inc(att_done, 1)
                pe.wait_ge(taken, levels)
                pe.wait_ge(crossed, 1)
                for h in range(4):
                    o = k.bank(6 + h // 2)[:, (h % 2) * S:(h % 2 + 1) * S]
                    pe.matmul(o[:, 0:P], vt[:, 0, h, :], att[:, 2 * h, :], start=True, stop=True)
                    pe.matmul(o[:, P:S], vt[:, 0, h, :], cross[:, h, :], start=True, stop=False)
                    mm = pe.matmul(o[:, P:S], vt[:, 1, h, :], att[:, 2 * h + 1, :], start=False, stop=True)
                    if h % 2:
                        mm.then_inc(pv_done, 1)


def mlstm(k, name, q, kk, vt, wif, bif, tab, out):
    H = 4
    with stage(k, name) as (block, sem, buf):
        gi, lf = buf("gi", [P, ST, 8]), buf("lf", [P, ST, 4])
        t1, fsum = buf("t1", [P, ST, 4]), buf("fsum", [P, ST, 4])
        gm = buf("gm", [P, 2, ST, S])
        w = buf("w", [P, 2, ST, S])
        wt = buf("wt", [P, 2, 3, P])
        mx, nm, em, dot, den = (buf(x, [P, 2, ST]) for x in ("mx", "nm", "em", "dot", "den"))
        projected, vsteps, ssteps, f_done, gm_ready, d_done, s_done, masked, max_ready, exp_done, w_ready, turned, \
            moved, pv_done, out_ready = map(
                sem, ("projected", "vector_steps", "scalar_steps", "f_done", "gm_ready", "d_done", "s_done", "masked",
                      "max_ready", "exp_done", "w_ready", "turned", "moved", "pv_done", "out_ready"))
        first_steps = 3

        @block.tensor
        def _(pe):
            for t in range(ST):
                for i in range(KD):
                    mm = pe.matmul(k.bank(7)[:, 8 * t:8 * t + 8], k.h[:, i, bass.ts(t, P)], wif[:, i, :],
                                   start=(i == 0), stop=(i == KD - 1))
            mm.then_inc(projected, 1)
            pe.wait_ge(vsteps, first_steps + 1)
            for t in range(ST):
                for kt in range(t + 1):
                    mm = pe.matmul(k.bank(6)[:, 4 * t:4 * t + 4], tab["le"][:, kt, bass.ts(t, P)], lf[:, kt, :],
                                   start=(kt == 0), stop=(kt == t))
            mm.then_inc(f_done, 1)

            def logs(h):
                pe.wait_ge(gm_ready, 4 * h + 4)
                if h >= 2:
                    pe.wait_ge(masked, h - 1)
                for t in range(ST):
                    for kt in range(t + 1):
                        mm = pe.matmul(k.bank(h % 2)[:, bass.ts(t, S)], tab["le"][:, kt, bass.ts(t, P)],
                                       gm[:, h % 2, kt, :], start=(kt == 0), stop=(kt == t))
                mm.then_inc(d_done, 1)
                if h >= 2:
                    pe.wait_ge(w_ready, h - 1)
                for t in range(ST):
                    mm = pe.matmul(k.bank(2 + h % 2)[:, bass.ts(t, S)], q[:, h, bass.ts(t, P)], kk[:, h, :],
                                   start=True, stop=True)
                mm.then_inc(s_done, 1)

            def outputs(h):
                pe.wait_ge(w_ready, h + 1)
                if h >= 2:
                    pe.wait_ge(moved, h - 1)
                for j, (t, s) in enumerate(((0, 0), (1, 0), (1, 1))):
                    mm = pe.transpose(k.bank(4 + h % 2)[:, bass.ts(j, P)], w[:, h % 2, t, bass.ts(s, P)], k.ident[:])
                mm.then_inc(turned, 1)
                pe.wait_ge(moved, h + 1)
                if h >= 2:
                    pe.wait_ge(out_ready, h - 1)
                else:
                    pe.wait_ge(vsteps, first_steps + 2)
                o = k.bank(6 + h % 2)
                pe.matmul(o[:, 0:P], vt[:, 0, h, :], wt[:, h % 2, 0, :], start=True, stop=True)
                pe.matmul(o[:, P:S], vt[:, 0, h, :], wt[:, h % 2, 1, :], start=True, stop=False)
                pe.matmul(o[:, P:S], vt[:, 1, h, :], wt[:, h % 2, 2, :], start=False, stop=True).then_inc(pv_done, 1)

            for h in range(H + 1):
                if h < H:
                    logs(h)
                if h >= 1:
                    outputs(h - 1)

        @block.vector
        def _(dve):
            step = Chain(dve, vsteps)
            dve.wait_ge(projected, 1)
            step(dve.tensor_tensor(gi[:], k.bank(7)[:, 0:16].rearrange("p (t g) -> p t g", t=ST),
                                   bc(bif.unsqueeze(1), [P, ST, 8]), ALU.add))
            f = gi[:, :, 4:8]
            step(dve.scalar_tensor_tensor(out=t1[:], in0=f, scalar=-1.0, in1=f, op0=ALU.mult, op1=ALU.max))
            step(dve.tensor_scalar(lf[:], f, 0.0, None, ALU.min))
            dve.wait_ge(ssteps, 2)
            step(dve.tensor_tensor(lf[:], lf[:], t1[:], ALU.subtract))
            dve.wait_ge(f_done, 1)
            step(dve.tensor_copy(fsum[:], k.bank(6)[:, 0:8].rearrange("p (t g) -> p t g", t=ST)))

            def gates(h):
                if h >= 2:
                    dve.wait_ge(d_done, h - 1)
                for kt in range(ST):
                    dve.tensor_scalar(gm[:, h % 2, kt, :], tab["gt"][:, kt, :], lf[:, kt, h:h + 1], None,
                                      ALU.mult).then_inc(gm_ready, 1)
                dve.wait_ge(gm_ready, 4 * h + 2)
                for kt in range(ST):
                    dve.scalar_tensor_tensor(out=gm[:, h % 2, kt, :], in0=tab["eq"][:, kt, :], scalar=gi[:, kt, h:h + 1],
                                             in1=gm[:, h % 2, kt, :], op0=ALU.mult, op1=ALU.add).then_inc(gm_ready, 1)

            def maxima(h):
                dve.wait_ge(d_done, h + 1)
                if h >= 2:
                    dve.wait_ge(turned, h - 1)
                ww = w[:, h % 2, :, :]
                dve.tensor_tensor(ww, k.bank(h % 2).rearrange("p (t s) -> p t s", t=ST), tab["mask"],
                                  ALU.add).then_inc(masked, 1)
                dve.wait_ge(masked, h + 1)
                step(dve.tensor_reduce(mx[:, h % 2, :], ww, AX.X, ALU.max))
                step(dve.tensor_tensor(mx[:, h % 2, :], mx[:, h % 2, :], fsum[:, :, h], ALU.max))
                dve.tensor_scalar(nm[:, h % 2, :], mx[:, h % 2, :], -1.0, None, ALU.mult).then_inc(max_ready, 1)

            def weights(h):
                dve.wait_ge(exp_done, 3 * h + 3)
                dve.wait_ge(s_done, h + 1)
                ww, dt, dn = w[:, h % 2, :, :], dot[:, h % 2, :], den[:, h % 2, :]
                step(dve.tensor_tensor(ww, k.bank(2 + h % 2).rearrange("p (t s) -> p t s", t=ST), ww, ALU.mult))
                step(dve.tensor_reduce(dt, ww, AX.X, ALU.add))
                step(dve.scalar_tensor_tensor(out=dn, in0=dt, scalar=-1.0, in1=dt, op0=ALU.mult, op1=ALU.max))
                step(dve.tensor_tensor(dn, dn, em[:, h % 2, :], ALU.max))
                step(dve.reciprocal(dn, dn))
                for t in range(ST):
                    ins = dve.tensor_scalar(w[:, h % 2, t, :], w[:, h % 2, t, :], dn[:, t:t + 1], None, ALU.mult)
                    if t == 0:
                        step(ins)
                ins.then_inc(w_ready, 1)

            def store(h):
                dve.wait_ge(pv_done, h + 1)
                dve.tensor_copy(out[:, h, :], k.bank(6 + h % 2)[:, 0:S]).then_inc(out_ready, 1)

            gates(0)
            for h in range(H + 2):
                if h < H:
                    maxima(h)
                    if h + 1 < H:
                        gates(h + 1)
                    weights(h)
                if 1 <= h <= H:
                    store(h - 1)

        @block.scalar
        def _(act):
            step = Chain(act, ssteps)
            act.wait_ge(vsteps, 2)
            step(act.activation(t1[:], t1[:], ACT.Exp, scale=-1.0))
            step(act.activation(t1[:], t1[:], ACT.Ln, bias=1.0))
            for h in range(H):
                act.wait_ge(max_ready, h + 1)
                for t in range(ST):
                    act.activation(w[:, h % 2, t, :], w[:, h % 2, t, :], ACT.Exp, bias=nm[:, h % 2, t:t + 1]).then_inc(exp_done, 1)
                act.activation(em[:, h % 2, :], nm[:, h % 2, :], ACT.Exp).then_inc(exp_done, 1)
                act.wait_ge(turned, h + 1)
                if h >= 2:
                    act.wait_ge(pv_done, h - 1)
                act.activation(wt[:, h % 2, :, :], k.bank(4 + h % 2)[:, 0:3 * P], ACT.Copy).then_inc(moved, 1)


def router(k, name, rw, rb, tri8, cb):
    with stage(k, name) as (block, sem, buf):
        lg, gt, tmp = buf("lg", [P, ST, NE]), buf("gt", [P, NE, NE]), buf("tmp", [P, NE, NE])
        rank, sel = buf("rank", [P, ST, NE]), buf("sel", [P, ST, NE])
        mx, l = buf("mx", [P, ST]), buf("l", [P, ST])
        dg = buf("dg", [P, ST, NE, P])
        projected, vsteps, ssteps, dg_ready, spread, placed = map(
            sem, ("projected", "vector_steps", "scalar_steps", "dg_ready", "spread", "placed"))

        @block.tensor
        def _(pe):
            for t in range(ST):
                for i in range(KD):
                    mm = pe.matmul(k.bank(0)[:, 8 * t:8 * t + 8], k.h[:, i, bass.ts(t, P)], rw[:, i, :],
                                   start=(i == 0), stop=(i == KD - 1))
            mm.then_inc(projected, 1)
            pe.wait_ge(dg_ready, ST * NE)
            for t in range(ST):
                for j in range(2):
                    mm = pe.matmul(k.bank(2 + 2 * t + j), k.ones[:], dg[:, t, 4 * j:4 * j + 4, :].rearrange("p e s -> p (e s)"),
                                   start=True, stop=True)
            mm.then_inc(spread, 1)

        @block.vector
        def _(dve):
            step = Chain(dve, vsteps)
            dve.wait_ge(projected, 1)
            step(dve.tensor_tensor(lg[:], k.bank(0)[:, 0:16].rearrange("p (t e) -> p t e", t=ST),
                                   bc(rb.unsqueeze(1), [P, ST, NE]), ALU.add))
            step(dve.tensor_reduce(mx[:], lg[:], AX.X, ALU.max, negate=True))
            dve.wait_ge(ssteps, 2)
            step(dve.reciprocal(l[:], l[:]))
            step(dve.tensor_tensor(lg[:], lg[:], bc(l[:].unsqueeze(2), [P, ST, NE]), ALU.mult))
            for t in range(ST):
                mine = bc(lg[:, t, :].unsqueeze(2), [P, NE, NE])
                other = bc(lg[:, t, :].unsqueeze(1), [P, NE, NE])
                step(dve.tensor_tensor(gt[:], other, mine, ALU.is_gt))
                step(dve.tensor_tensor(tmp[:], other, mine, ALU.is_equal))
                step(dve.tensor_tensor(tmp[:], tmp[:], tri8, ALU.mult))
                step(dve.tensor_tensor(gt[:], gt[:], tmp[:], ALU.add))
                step(dve.tensor_reduce(rank[:, t, :], gt[:], AX.X, ALU.add))
            step(dve.tensor_scalar(sel[:], rank[:], 1.5, None, ALU.is_lt))
            step(dve.tensor_tensor(sel[:], sel[:], lg[:], ALU.mult))
            step(dve.tensor_reduce(mx[:], sel[:], AX.X, ALU.add))
            step(dve.reciprocal(mx[:], mx[:]))
            step(dve.tensor_tensor(sel[:], sel[:], bc(mx[:].unsqueeze(2), [P, ST, NE]), ALU.mult))
            for t in range(ST):
                for e in range(NE):
                    dve.tensor_scalar(dg[:, t, e, :], k.ident[:], sel[:, t, e:e + 1], None, ALU.mult).then_inc(dg_ready, 1)
            dve.wait_ge(spread, 1)
            for t in range(ST):
                for j in range(2):
                    dve.tensor_copy(cb[:, 4 * j:4 * j + 4, bass.ts(t, P)],
                                    k.bank(2 + 2 * t + j).rearrange("p (e s) -> p e s", e=4)).then_inc(placed, 1)

        @block.scalar
        def _(act):
            act.wait_ge(vsteps, 2)
            for t in range(ST):
                act.activation(lg[:, t, :], lg[:, t, :], ACT.Exp, bias=mx[:, t:t + 1], accum_out=l[:, t:t + 1]).then_inc(ssteps, 1)


def experts(k, phase, cb, gain):
    start = k.start[phase]
    s0 = k.index[start]
    up = 2 * NF * KD // SLOT
    with ExitStack() as c:
        g_hi = k.sbuf("moe_g_hi", [P, NF, S], F32R, c)
        g_lo = k.sbuf("moe_g_lo", [P, NF, S], F32R, c)
        with stage(k, "moe") as (block, sem, buf):
            gate, g, y = buf("gate", [P, 2, S]), buf("g", [P, 2, S]), buf("y", [P, 2, S])
            gate_ready, product, rounded, g_split, weighted, added = map(
                sem, ("gate_ready", "product", "rounded", "g_split", "weighted", "added"))
            NS, ND = EXPERT_SLOTS, KD // 2
            down_end = lambda d: up + ((d + 1) * 2 * NF + SLOT - 1) // SLOT

            def raw_ready(eng, e, j):
                n = start + j
                eng.wait_ge(k.raw_loaded[n % RAW], e * (16 * NS // RAW) + 16 * (n // RAW + 1))

            def load(sp, e, j):
                sp.wait_ge(k.slot_split, e * NS + s0 + j - RAW + 1)
                sp.dma_start(k.raw[:, (start + j) % RAW, :],
                             k.dram["experts"][bass.ds(e * NS + j, 1)].rearrange("n p w -> (n p) w")).then_inc(k.raw_loaded[(start + j) % RAW], 16)

            assert k.loaded == start + RAW and k.hi_done == k.lo_done == start + LOOK

            @block.sync
            def _(sp):
                with sp.Fori(0, NE - 1) as e:
                    for j in range(RAW, NS + RAW):
                        load(sp, e, j)
                for j in range(RAW, NS):
                    load(sp, NE - 1, j)

            def split_hi(act, e, j):
                s = s0 + j
                raw_ready(act, e, j)
                act.wait_ge(k.slot_used, e * NS + s - SPLIT + 1)
                act.activation(k.w_hi[:, s % SPLIT, :], k.raw[:, (start + j) % RAW, :], ACT.Copy).then_inc(k.hi_ready, 1)

            def split_lo(dve, e, j):
                s = s0 + j
                raw_ready(dve, e, j)
                dve.wait_ge(k.hi_ready, e * NS + s + 1)
                dve.tensor_tensor(k.w_lo[:, s % SPLIT, :], k.raw[:, (start + j) % RAW, :],
                                  k.w_hi[:, s % SPLIT, :].bitcast(F32), ALU.subtract).then_inc(k.slot_split, 1)

            def act_expert(act, e, last):
                done = LOOK
                for f in range(NF):
                    for j in range(done, UPS * (f + 1) + LOOK):
                        split_hi(act, e, j)
                    done = UPS * (f + 1) + LOOK
                    act.wait_ge(k.slot_used, e * NS + s0 + UPS * (f + 1))
                    if f >= 2:
                        act.wait_ge(product, e * NF + f - 1)
                    act.activation(gate[:, f % 2, :], k.bank(f % 4)[:, 0:S], ACT.Silu).then_inc(gate_ready, 1)
                for j in range(done, NS if last else NS + LOOK):
                    split_hi(act, e, j)

            def dve_expert(dve, e, last):
                done = LOOK
                for f in range(NF):
                    for j in range(done, UPS * (f + 1) + LOOK):
                        split_lo(dve, e, j)
                    done = UPS * (f + 1) + LOOK
                    dve.wait_ge(gate_ready, e * NF + f + 1)
                    gb = g[:, f % 2, :]
                    dve.tensor_tensor(gb, k.bank(f % 4)[:, S:2 * S], gate[:, f % 2, :], ALU.mult).then_inc(product, 1)
                    dve.wait_ge(product, e * NF + f + 1)
                    dve.tensor_copy(g_hi[:, f, :], gb).then_inc(rounded, 1)
                    dve.wait_ge(rounded, e * NF + f + 1)
                    dve.tensor_tensor(g_lo[:, f, :], gb, g_hi[:, f, :].bitcast(F32), ALU.subtract).then_inc(g_split, 1)
                for d in range(ND):
                    upto = min(down_end(d) + LOOK, NS if last else NS + LOOK)
                    for j in range(done, upto):
                        split_lo(dve, e, j)
                    done = upto
                    dve.wait_ge(k.slot_used, e * NS + s0 + down_end(d))
                    for half in range(2):
                        i = 2 * d + half
                        if isinstance(e, int):
                            w = cb[:, e, :]
                        else:
                            w = cb[:, bass.ds(e, 1), :].rearrange("p n s -> p (n s)")
                        dve.tensor_tensor(y[:, half, :], k.bank(4 + d)[:, bass.ts(half, S)], w, ALU.mult).then_inc(weighted, 1)
                    for half in range(2):
                        i = 2 * d + half
                        dve.wait_ge(weighted, e * KD + 2 * d + 2)
                        dve.scalar_tensor_tensor(out=k.x[:, i, :], in0=y[:, half, :], scalar=gain[:, i:i + 1],
                                                 in1=k.x[:, i, :], op0=ALU.mult, op1=ALU.add).then_inc(added, 1)
                    dve.wait_ge(added, e * KD + 2 * d + 2)

            @block.scalar
            def _(act):
                with act.Fori(0, NE - 1) as e:
                    act_expert(act, e, False)
                act_expert(act, NE - 1, True)

            @block.vector
            def _(dve):
                with dve.Fori(0, NE - 1) as e:
                    dve_expert(dve, e, False)
                dve_expert(dve, NE - 1, True)

            @block.tensor
            def _(pe):
                with pe.Fori(0, NE) as e:
                    at = lambda v: e * NS + v
                    t = 0
                    for f in range(NF):
                        if f >= 4:
                            pe.wait_ge(product, e * NF + f - 3)
                        t = multiply_unit(k, pe, start, t, KD, k.h_hi[:], k.h_lo[:], k.bank(f % 4), at)
                    pe.wait_ge(g_split, e * NF + NF)
                    for d in range(ND):
                        t = multiply_unit(k, pe, start, t, NF, g_hi[:], g_lo[:], k.bank(4 + d), at)


def mixer_block(k, l):
    d = k.dram
    lam_init = 0.8 - 0.6 * float(np.exp(-0.3 * (l - 1)))
    n = lambda x: f"{x}{l}"
    fl = lambda t: t.rearrange("q a s -> q (a s)")
    with ExitStack() as c0:
        par = k.sbuf(n("cols"), [P, COLS1], F32, c0)
        col = {x: par[:, a:z] for x, (a, z) in COL1.items()}
        mod_t = k.sbuf(n("mod"), [P, 48], F32, c0)
        own = k.sbuf(n("own"), [P, 18 + 20], F32, c0)
        out = {"scale": own[:, 0:16], "lam": own[:, 16:17], "subln": own[:, 17:18]}
        lb = own[:, 18:38].rearrange("p (a h) -> p a h", a=5)
        mod = mod_t[:]
        load_stage(k, n("load"), [(par[:], d[n("cols")])])
        modulation(k, n("mod"), n("mod"), col["cond"], col["b_mod"], mod)
        block_columns(k, n("own"), col, mod, out, col["lam"].rearrange("p (a j) -> p a j", a=4), lam_init, lb, l)
        norm_stream(k, n("n1"), out["scale"][:, 0:8], mod[:, 0:8])
        with ExitStack() as c1:
            y_hi = k.sbuf(n("mix_hi"), [P, 3, 4, S], F32R, c1)
            y_lo = k.sbuf(n("mix_lo"), [P, 3, 4, S], F32R, c1)
            with ExitStack() as c2:
                dist = k.sbuf(n("da_dist"), [P, ST, S], F32, c2)
                qk = k.sbuf(n("a_qk"), [P, 8, S], F32, c2)
                vf = k.sbuf(n("a_v"), [P, 4, S], F32, c2)
                vt = k.sbuf(n("a_vt"), [P, ST, 4, P], F32, c2)
                load_stage(k, n("loada"), [(dist[:], d["da_dist"])])
                plain_projection(k, n("ax"), n("a_in"), 6,
                                 lambda u: (qk[:, 2 * u:2 * u + 2, :] if u < 4 else vf[:, 2 * u - 8:2 * u - 6, :], ACT.Copy))
                to_token_major(k, n("at"), [(vf[:, i, :], [vt[:, t, i, :] for t in range(ST)]) for i in range(4)])
                norm_heads(k, n("an"), [(fl(qk[:, 0:4, :]), fl(qk[:, 0:4, :]), col["qn"], None),
                                        (fl(qk[:, 4:8, :]), fl(qk[:, 4:8, :]), col["kn"], None)], k.head_ones[:], 64.0)
                scale_columns(k, n("as"), qk[:, 0:4, :], 64 ** -0.5)
                diff_attention(k, n("da"), qk[:], vt[:], dist[:], out["lam"], vf[:])
                norm_heads(k, n("ao"), [(fl(vf[:]), fl(vf[:]), out["subln"], None)], k.ones[:], float(P))
                split_stage(k, n("asp"), vf[:], y_hi[:, 0], y_lo[:, 0])
            with ExitStack() as c2:
                q, f, vf, g = (k.sbuf(n(x), [P, 4, S], F32, c2) for x in ("b_q", "b_f", "b_v", "b_g"))
                vt = k.sbuf(n("b_vt"), [P, ST, 4, P], F32, c2)
                lev = k.sbuf(n("b_lev"), [P, 7, P], F32, c2)
                load_stage(k, n("loadb"), [(lev[:], d["hg_levels"])])
                dst = (q, f, vf, g)
                fn = (ACT.Silu, ACT.Copy, ACT.Copy, ACT.Silu)
                plain_projection(k, n("bx"), n("b_in"), 8,
                                 lambda u: (dst[u // 2][:, 2 * (u % 2):2 * (u % 2) + 2, :], fn[u // 2]))
                to_token_major(k, n("bt"), [(vf[:, i, :], [vt[:, t, i, :] for t in range(ST)]) for i in range(4)])
                gated_recurrence(k, n("hg"), fl(q[:]), fl(f[:]), vt[:], lb, {"ident": k.ident[:], "lev": lev[:]}, vf[:])
                norm_heads(k, n("bo"), [(fl(vf[:]), fl(vf[:]), col["gnorm"], fl(g[:]))], k.ones[:], float(P))
                split_stage(k, n("bsp"), vf[:], y_hi[:, 1], y_lo[:, 1])
            with ExitStack() as c2:
                qk = k.sbuf(n("c_qk"), [P, 8, S], F32, c2)
                vf, og = (k.sbuf(n(x), [P, 4, S], F32, c2) for x in ("c_v", "c_o"))
                vt = k.sbuf(n("c_vt"), [P, ST, 4, P], F32, c2)
                wif = k.sbuf(n("c_wif"), [P, KD, 8], F32, c2)
                tabs = k.sbuf(n("c_tabs"), [P, 4, ST, S], F32, c2)
                load_stage(k, n("loadc"), [(tabs[:], d["ml_tables"]), (wif[:], d[n("wif")])])
                tab = dict(zip(("le", "gt", "eq", "mask"), (tabs[:, i] for i in range(4))))

                def place(u):
                    if u < 4:
                        return qk[:, 2 * u:2 * u + 2, :], ACT.Silu
                    if u < 6:
                        return vf[:, 2 * u - 8:2 * u - 6, :], ACT.Copy
                    return og[:, 2 * u - 12:2 * u - 10, :], ACT.Sigmoid
                taps = [col["conv"][:, 8 * j:8 * j + 8] for j in range(4)]
                conv_projection(k, n("cx"), n("c_in"), 8, 4, place, taps, 3, col["conv_b"])
                to_token_major(k, n("ct"), [(vf[:, i, :], [vt[:, t, i, :] for t in range(ST)]) for i in range(4)])
                scale_columns(k, n("cs"), qk[:, 4:8, :], 128 ** -0.5)
                mlstm(k, n("ml"), qk[:, 0:4, :], qk[:, 4:8, :], vt[:], wif, col["bif"], tab, vf[:])
                norm_heads(k, n("co"), [(fl(vf[:]), fl(vf[:]), col["cnorm"], fl(og[:]))], k.ones[:], float(P))
                split_stage(k, n("csp"), vf[:], y_hi[:, 2], y_lo[:, 2])
            with ExitStack() as c2:
                m_hi = k.sbuf(n("merged_hi"), [P, KD, S], F32R, c2)
                m_lo = k.sbuf(n("merged_lo"), [P, KD, S], F32R, c2)
                gated_branches(k, n("gb"), n("gates"), [(y_hi[:, i], y_lo[:, i]) for i in range(3)], m_hi, m_lo)
                residual_projection(k, n("wo"), n("out"), [KD] * 4, m_hi[:], m_lo[:], mod[:, 16:24])
        norm_stream(k, n("n2"), out["scale"][:, 8:16], mod[:, 24:32])
        if l == 1:
            feed_forward(k, n("ff"), n("ffn"), mod[:, 40:48])
        else:
            with ExitStack() as c1:
                rw = k.sbuf("router_w", [P, KD, NE], F32, c1)
                tri8 = k.sbuf("tri8", [P, NE, NE], F32, c1)
                cb = k.sbuf("token_weights", [P, NE, S], F32, c1)
                load_stage(k, "loadr", [(rw[:], d["router_w"]), (tri8[:], d["tri8"])])
                router(k, "rt", rw, col["router_b"], tri8[:], cb[:])
                experts(k, n("ffn"), cb[:], mod[:, 40:48])


def columns(sizes):
    at, out = 0, {}
    for name, n in sizes:
        out[name] = (at, at + n)
        at += n
    return out, at


COL0, COLS0 = columns((("norm1", 8), ("norm2", 8), ("dn_conv", 36), ("dn_norm", 1), ("qn", 1), ("kn", 1),
                       ("ffn_conv", 6 * NF), ("alog", 8), ("dtb", 8)))
COL1, COLS1 = columns((("norm1", 8), ("norm2", 8), ("b_mod", 48), ("cond", 8), ("conv", 32), ("conv_b", 8),
                       ("qn", 1), ("kn", 1), ("subln", 1), ("lb0", 4), ("lb1", 4), ("gnorm", 1), ("cnorm", 1),
                       ("bif", 8), ("lam", 256), ("router_b", 8)))
DN_TABLE = 4 * P + 3 * CH + 12 * CH


def shape_tables():
    f = lambda a: np.ascontiguousarray(a, dtype=np.float32)
    i, j = np.arange(P)[:, None], np.arange(P)[None, :]
    same = (i // CH) == (j // CH)
    r, cc = np.arange(P)[:, None] % CH, np.arange(CH)[None, :]
    lev = np.zeros((P, 2, 6, CH))
    for l in range(6):
        blk = (r >> (l + 1)) == (cc >> (l + 1))
        lev[:, 0, l] = blk & (((r >> l) & 1) == 0) & (((cc >> l) & 1) == 1)
        lev[:, 1, l] = blk & (((r >> l) & 1) == 1) & (((cc >> l) & 1) == 0)
    dn = np.concatenate([same & (i > j), same & (i < j), same & (i <= j), same & (i >= j),
                         r <= cc, r >= cc, r == cc, lev.reshape(P, -1)], axis=1)
    q = np.arange(S).reshape(ST, P).T[:, :, None]
    s = np.arange(S)[None, None, :]
    dist = np.abs(q - s)
    att = np.stack([np.where(ok, dist, BIG) for ok in (dist <= 64, dist % 4 == 0, dist % 16 == 0)], axis=2)
    da = np.where(s // 64 <= q // 64, dist, BIG)
    ml = np.stack([q <= s, q > s, q == s, np.where(s <= q, 0.0, -BIG)], axis=1)
    hg = np.stack([((i >> (l + 1)) == (j >> (l + 1))) & (((i >> l) & 1) == 0) & (((j >> l) & 1) == 1)
                   for l in range(7)], axis=1)
    e = np.arange(NE)
    return {"dn_tables": f(dn), "att_dist": f(att), "da_dist": f(da), "ml_tables": f(ml), "hg_levels": f(hg),
            "ident": f(i == j), "ones": f(np.ones((P, P))), "head_ones": f(same), "eps": f(np.full((P, 1), EPS)),
            "tri8": f(np.broadcast_to(e[None, :, None] > e[None, None, :], (P, NE, NE)))}


def lay_out(a):
    def tiles(w):
        kk, n = w.shape
        return w.reshape(kk // P, P, n // P, P).transpose(2, 0, 1, 3)

    def pieces(w, order=None):
        t = tiles(w)
        t = t if order is None else t[order]
        return t.reshape(-1, P, P)

    def slots(ps):
        t = np.concatenate(ps)
        return t.reshape(-1, SLOT, P, P).transpose(0, 2, 1, 3).reshape(-1, P, SLOT * P)

    def gates(w_gates, w_branches):
        out = []
        for dd in range(4):
            for wg, wb in zip(w_gates, w_branches):
                out += [pieces(wg, [2 * dd, 2 * dd + 1]), pieces(wb, [2 * dd, 2 * dd + 1])]
        return out

    interleave = [x for f in range(NF) for x in (f, NF + f)]
    w_in, w2 = a["w_in"][0], a["w_in_2"]
    parts = [slots([pieces(w_in[:, 0:2048])]),
             slots([pieces(w_in[:, 2080:6688])]),
             slots(gates([w_in[:, 6688:7712], w_in[:, 7712:8736]], [a["w_dn_out"][0], a["w_attn_out"][0]])),
             slots([pieces(a["w_o"][0])]),
             slots([pieces(a["w_ffn_up"][0], interleave), pieces(a["w_ffn_down"][0])])]
    ffn = lambda w1, w3, wd: [pieces(np.concatenate([w1, w3], axis=1), interleave), pieces(wd)]
    for l in range(2):
        w = w2[l]
        parts += [slots([pieces(a["w_mod_2"][l])]), slots([pieces(w[:, 0:1536])]), slots([pieces(w[:, 1536:3584])]),
                  slots([pieces(w[:, 3584:5632])]),
                  slots(gates([w[:, 5640 + D * i:5640 + D * (i + 1)] for i in range(3)], a["w_branch_2"][l])),
                  slots([pieces(a["w_out_2"][l])])]
        if l == 0:
            parts.append(slots(ffn(a["ffn_w1_2"][0], a["ffn_w3_2"][0], a["ffn_w2_2"][0])))
        else:
            for e in range(NE):
                parts.append(slots(ffn(a["moe_w1_2"][0, e], a["moe_w3_2"][0, e], a["moe_w2_2"][0, e])))

    def col(v):
        return v.reshape(-1, P).T

    def rows(w):
        return w.reshape(KD, P, -1).transpose(1, 0, 2)

    twice = lambda v: np.tile(v, 2)[:, None]
    over = lambda v: np.broadcast_to(v.reshape(1, -1), (P, v.size))
    pair = lambda v: np.repeat(v.reshape(2, 4, 2).transpose(2, 0, 1).reshape(2, 8), CH, axis=0)
    out = {"stream": np.concatenate(parts),
           "x_t": a["x"][0].T.reshape(KD, P, S).transpose(1, 0, 2),
           "wab": rows(w_in[:, 2048:2080]).reshape(P, KD, 4, 4, 2).transpose(0, 1, 4, 2, 3).reshape(P, KD, 2, 16),
           "cols0": np.concatenate(
               [col(a["norm1_w"][0]), col(a["norm2_w"][0])] + [col(a["dn_conv_w"][0][j]) for j in range(3)]
               + [twice(a["dn_out_norm_w"][0]), twice(a["attn_q_norm_w"][0]), twice(a["attn_k_norm_w"][0])]
               + [col(a["ffn_conv_w"][0][j]) for j in range(3)] + [pair(a["dn_a_log"][0]), pair(a["dn_dt_bias"][0])], axis=1),
           "router_w": rows(a["moe_router_w_2"][0])}
    for l in range(2):
        g = lambda n: a[n + "_2"][l]
        out[f"wif{l + 1}"] = rows(w2[l][:, 5632:5640])
        out[f"cols{l + 1}"] = np.concatenate(
            [col(g("norm1_w")), col(g("norm2_w")), col(g("b_mod")), col(a["c_2"][0])]
            + [col(g("c_conv_w")[j]) for j in range(4)]
            + [col(g("c_conv_b")), twice(g("a_qnorm_w")), twice(g("a_knorm_w")), g("a_subln_w")[:, None],
               col(a["b_lb_logits_2"][0]), col(a["b_lb_logits_2"][1]), g("b_gnorm_w")[:, None], g("c_norm_w")[:, None],
               over(g("c_igate_b")), over(g("c_fgate_b"))]
            + [over(g(f"a_lambda_{x}")) for x in ("q1", "k1", "q2", "k2")] + [over(a["moe_router_b_2"][0])], axis=1)
    return {n: np.ascontiguousarray(v) for n, v in {**out, **shape_tables()}.items()}


def build(nc, shapes, out):
    with ExitStack() as ctx:
        dram = {n: nc.dram_tensor(f"in_{n}", s, F32, kind="ExternalInput").ap() for n, s in shapes.items()}
        k = Kern(nc, ctx, dram)
        dram["experts"] = dram["stream"][k.start["ffn2"]:k.slots]
        first_block(k)
        mixer_block(k, 1)
        mixer_block(k, 2)
        with stage(k, "store") as (block, sem, buf):
            stored = sem("stored")

            @block.sync
            def _(sp):
                sp.dma_start(out, k.x[:]).then_inc(stored, 16)
                sp.wait_ge(stored, 16)


def kernel(**inputs):
    import concourse.bacc as bacc
    from concourse.bass_utils import run_bass_kernel_spmd

    arrays = lay_out({n: np.asarray(v) for n, v in inputs.items()})
    nc = bacc.Bacc("TRN2", target_bir_lowering=False, num_devices=1)
    out = nc.dram_tensor("x_out", (P, KD, S), F32, kind="ExternalOutput").ap()
    build(nc, {n: v.shape for n, v in arrays.items()}, out)
    r = run_bass_kernel_spmd(nc, [{f"in_{n}": v for n, v in arrays.items()}], core_ids=[0])
    y = np.asarray(r.results[0]["x_out"])
    return np.ascontiguousarray(y.transpose(1, 0, 2).reshape(D, S).T.reshape(1, S, D))
```

```python
from contextlib import ExitStack, contextmanager

import numpy as np

import concourse.bass as bass
from concourse import mybir

F32 = mybir.dt.float32
F32R = mybir.dt.float32r
I32 = mybir.dt.int32
ACT = mybir.ActivationFunctionType
ALU = mybir.AluOpType
AX = mybir.AxisListType

P = 128
S = 256
ST = S // P
D = 1024
KD = D // P
CH = 64
NCH = S // CH
DFF = 2816
NF = DFF // P
NE = 8
EPS = 1e-6
BIG = 1e30
BANK = 512
SLOT = 8
RAW = 11
SPLIT = 3
LOOK = 2
UPS = 2 * KD // SLOT
NMOD = 6 * KD
EXPERT_SLOTS = (2 * NF * KD + KD * NF) // SLOT

PAIRS0 = 4


def gemm_plan():
    plan = [("dn_in", 16), ("att_in", 36), ("gates0", 2 * 4 * 3), ("out0", KD), ("ffn0", EXPERT_SLOTS)]
    for l in (1, 2):
        plan += [(f"a_in{l}", 12), (f"b_in{l}", 16), (f"c_in{l}", 16), (f"gates{l}", 3 * 4 * 3), (f"out{l}", KD),
                 (f"ffn{l}", EXPERT_SLOTS * (NE if l == 2 else 1))]
    return plan


MOD_PLAN = {"att_in": (24, 0), "gates0": (12, 0), "out0": (3, 0), "ffn0": (9, 2 * NF * KD // SLOT),
            "gates1": (18, 0), "out1": (4, 0), "ffn1": (26, 0)}


def stream_order():
    order, g, m = [], 0, 0
    for name, slots in gemm_plan():
        count, behind = MOD_PLAN.get(name, (0, 0))
        assert count <= slots - behind
        for i in range(slots):
            order.append(("gemm", g))
            g += 1
            if i >= behind and (i + 1 - behind) * count // (slots - behind) > (i - behind) * count // (slots - behind):
                order.append(("mod", m))
                m += 1
    assert m == 2 * NMOD
    return order


class Kern:

    def __init__(self, nc, ctx, dram):
        self.nc, self.ctx, self.dram = nc, ctx, dram
        self.order = stream_order()
        self.place = [n for n, (kind, _) in enumerate(self.order) if kind == "gemm"]
        self.first, s = {}, 0
        for name, slots in gemm_plan():
            self.first[name] = s
            s += slots
        self.gemms = s
        self.to_clear = []
        self.loaded = self.hi_done = self.lo_done = 0

        self.x = self.sbuf("x", [P, KD, S])
        self.h = self.sbuf("h", [P, KD, S])
        self.h_hi = self.sbuf("h_hi", [P, KD, S], F32R)
        self.h_lo = self.sbuf("h_lo", [P, KD, S], F32R)
        self.raw = self.sbuf("raw_ring", [P, RAW, SLOT * P])
        self.w_hi = self.sbuf("w_hi_ring", [P, SPLIT, SLOT * P], F32R)
        self.w_lo = self.sbuf("w_lo_ring", [P, SPLIT, SLOT * P], F32R)
        self.cond = self.sbuf("cond", [P, D])
        self.mod = self.sbuf("mod", [P, 2 * NMOD])
        self.cols = {l: self.sbuf(f"cols{l}", [P, COLS1]) for l in (1, 2)}
        self.router_w = self.sbuf("router_w", [P, KD, NE])
        self.tri8 = self.sbuf("tri8", [P, NE, NE])
        self.consts = self.sbuf("consts", [P, 3 * P + 1])
        self.ident, self.ones = self.consts[:, 0:P], self.consts[:, P:2 * P]
        self.head_ones = self.consts[:, 2 * P:3 * P]
        self.eps = self.consts[:, 3 * P:3 * P + 1]
        self.ps = ctx.enter_context(nc.psum_tensor("ps", [P, 8 * BANK], F32))
        self.raw_loaded = [ctx.enter_context(nc.semaphore(f"raw_loaded{i}")) for i in range(RAW)]
        self.hi_ready = ctx.enter_context(nc.semaphore("hi_ready"))
        self.slot_split = ctx.enter_context(nc.semaphore("slot_split"))
        self.slot_used = ctx.enter_context(nc.semaphore("slot_used"))
        self.mod_used = ctx.enter_context(nc.semaphore("mod_used"))

    def sbuf(self, name, shape, dt=F32, ctx=None):
        return (ctx or self.ctx).enter_context(self.nc.sbuf_tensor(name, shape, dt))

    def bank(self, i, n=1):
        return self.ps[:, i * BANK:(i + n) * BANK]

    def raw_ready(self, eng, n):
        eng.wait_ge(self.raw_loaded[n % RAW], 16 * (n // RAW + 1))

    def load_slots(self, sp, upto):
        upto = min(upto, len(self.order))
        for n in range(self.loaded, upto):
            if n >= RAW:
                kind, m = self.order[n - RAW]
                sp.wait_ge(self.mod_used if kind == "mod" else self.slot_split, m + 1)
            sp.dma_start(self.raw[:, n % RAW, :], self.dram["stream"][n]).then_inc(self.raw_loaded[n % RAW], 16)
        self.loaded = max(self.loaded, upto)

    def split_hi(self, act, upto):
        upto = min(upto, self.gemms)
        for s in range(self.hi_done, upto):
            n = self.place[s]
            self.raw_ready(act, n)
            if s >= SPLIT:
                act.wait_ge(self.slot_used, s - SPLIT + 1)
            act.activation(self.w_hi[:, s % SPLIT, :], self.raw[:, n % RAW, :], ACT.Copy).then_inc(self.hi_ready, 1)
        self.hi_done = max(self.hi_done, upto)

    def split_lo(self, dve, upto):
        upto = min(upto, self.gemms)
        for s in range(self.lo_done, upto):
            n = self.place[s]
            self.raw_ready(dve, n)
            dve.wait_ge(self.hi_ready, s + 1)
            dve.tensor_tensor(self.w_lo[:, s % SPLIT, :], self.raw[:, n % RAW, :],
                              self.w_hi[:, s % SPLIT, :].bitcast(F32), ALU.subtract).then_inc(self.slot_split, 1)
            if n + 1 < len(self.order) and self.order[n + 1][0] == "mod":
                m, w = self.order[n + 1][1], self.raw[:, (n + 1) % RAW, :]
                self.raw_ready(dve, n + 1)
                dve.tensor_tensor_reduce(w, w, self.cond[:], 1.0, 0.0, ALU.mult, ALU.add,
                                         accum_out=self.mod[:, m:m + 1]).then_inc(self.mod_used, 1)
        self.lo_done = max(self.lo_done, upto)


class Chain:

    def __init__(self, eng, sem):
        self.eng, self.sem, self.n = eng, sem, 0

    def __call__(self, ins):
        ins.then_inc(self.sem, 1)
        self.n += 1
        self.eng.wait_ge(self.sem, self.n)


@contextmanager
def stage(k, name):
    cleared = k.to_clear
    for s in cleared:
        k.nc.gpsimd.sem_clear(s)
    mine = []
    with ExitStack() as c:
        def sem(what):
            mine.append(k.nc.alloc_semaphore(f"{name}_{what}"))
            return mine[-1]

        def buf(what, shape, dt=F32):
            return k.sbuf(f"{name}_{what}", shape, dt, c)
        yield c.enter_context(k.nc.Block()), sem, buf
    for s in cleared:
        k.nc.release_semaphore(s)
    k.to_clear = mine


def bc(ap, shape):
    return ap.to_broadcast(shape)


def projection(k, name, phase, units, rhs, evac_act=None, evac_dve=None, flush_act=None, flush_dve=None,
               banks=4, first_bank=0, sems=(), bufs=(), freed=None, loads=(), norm=None):
    start = k.first[phase] if isinstance(phase, str) else phase
    ends, t = [], 0
    for kt in units:
        t += 2 * kt
        ends.append(start + (t + SLOT - 1) // SLOT)
    with stage(k, name) as (block, sem, buf):
        s = {x: sem(x) for x in ("bank_freed", "table_loaded", *sems)}
        b = {x: buf(x, sh) for x, sh in bufs}
        bank = lambda u: k.bank(first_bank + u % banks)
        front = StreamNorm(k, sem, buf, *norm) if norm else None
        if front:
            block.gpsimd(front.pool)

        @block.sync
        def _(sp):
            for dst, src in loads:
                sp.dma_start(dst, src).then_inc(s["table_loaded"], 16)
            k.load_slots(sp, k.place[ends[-1] - 1] + 1 + RAW)
            if loads:
                sp.wait_ge(s["table_loaded"], 16 * len(loads))

        @block.scalar
        def _(act):
            if front:
                front.scalar(act)
            for u in range(len(units)):
                k.split_hi(act, ends[u] + LOOK)
                if evac_act:
                    act.wait_ge(k.slot_used, ends[u])
                    evac_act(act, u, bank(u), s, b)
            if flush_act:
                flush_act(act, s, b)

        @block.vector
        def _(dve):
            if front:
                front.vector(dve)
            for u in range(len(units)):
                k.split_lo(dve, ends[u] + LOOK)
                if evac_dve:
                    dve.wait_ge(k.slot_used, ends[u])
                    evac_dve(dve, u, bank(u), s, b)
            if flush_dve:
                flush_dve(dve, s, b)

        @block.tensor
        def _(pe):
            if front:
                front.tensor(pe)
            t = 0
            for u, kt in enumerate(units):
                if u >= banks and freed:
                    freed(pe, s, u - banks)
                elif u >= banks:
                    pe.wait_ge(s["bank_freed"], u - banks + 1)
                hi, lo = rhs(u)
                t = multiply_unit(k, pe, start, t, kt, hi, lo, bank(u),
                                  rhs_ready=(front.h_ready, 0) if front and u == 0 else None)


def multiply_unit(k, pe, start, t, kt, hi, lo, out, split_at=None, rhs_ready=None):
    for half in range(2):
        for kk in range(kt):
            i = start + t // SLOT
            if t % SLOT == 0:
                pe.wait_ge(k.slot_split, (split_at or (lambda v: v))(i + 1))
            if rhs_ready is not None and half == 0:
                pe.wait_ge(rhs_ready[0], rhs_ready[1] + kk + 1)
            w = bass.ts(t % SLOT, P)
            w_hi, w_lo = k.w_hi[:, i % SPLIT, w], k.w_lo[:, i % SPLIT, w]
            o = out[:, half * S:(half + 1) * S]
            pe.matmul(o, w_hi, hi[:, kk, :], start=(kk == 0), stop=False)
            pe.matmul(o, w_hi, lo[:, kk, :], start=False, stop=False)
            mm = pe.matmul(o, w_lo, hi[:, kk, :], start=False, stop=(kk == kt - 1))
            if t % SLOT == SLOT - 1:
                mm.then_inc(k.slot_used, 1)
            t += 1
    return t


def split_activation(eng, chain, src, hi, lo):
    chain(eng.tensor_copy(hi, src))
    chain(eng.tensor_tensor(lo, src, hi.bitcast(F32), ALU.subtract))


class StreamNorm:

    def __init__(self, k, sem, buf, scale, shift=None):
        self.k, self.scale, self.shift = k, scale, shift
        self.sq = k.h[:]
        self.ln, self.rs = buf("norm_ln", [P, S]), buf("norm_rs", [P, S])
        self.sq_ready, self.half_sum, self.sum_ready, self.ln_ready, self.rs_ready, self.scaled, self.shifted, \
            self.rounded, self.h_ready = (sem(f"norm_{x}") for x in (
                "sq_ready", "half_sum", "sum_ready", "ln_ready", "rs_ready", "scaled", "shifted", "rounded", "h_ready"))

    def pool(self, pool):
        pool.tensor_tensor(self.sq[:, 7, :], self.k.x[:, 7, :], self.k.x[:, 7, :], ALU.mult).then_inc(self.sq_ready, 1)

    def vector(self, dve):
        k, sq = self.k, self.sq
        dve.tensor_tensor(sq[:, 0:4, :], k.x[:, 0:4, :], k.x[:, 0:4, :], ALU.mult).then_inc(self.sq_ready, 1)
        dve.wait_ge(self.sq_ready, 3)
        dve.tensor_tensor(sq[:, 0:4, :], sq[:, 0:4, :], sq[:, 4:8, :], ALU.add).then_inc(self.half_sum, 1)
        dve.wait_ge(self.half_sum, 1)
        dve.tensor_tensor(sq[:, 0:2, :], sq[:, 0:2, :], sq[:, 2:4, :], ALU.add).then_inc(self.half_sum, 1)
        dve.wait_ge(self.rs_ready, 1)
        for i in range(KD):
            dve.scalar_tensor_tensor(out=k.h[:, i, :], in0=k.x[:, i, :], scalar=self.scale[:, i:i + 1],
                                     in1=self.rs[:], op0=ALU.mult, op1=ALU.mult).then_inc(self.scaled, 1)
            if i >= 2:
                self.low(dve, i - 2)
        self.low(dve, KD - 2)
        self.low(dve, KD - 1)

    def low(self, dve, i):
        k = self.k
        dve.wait_ge(self.rounded, i + 1)
        if self.shift is not None:
            dve.wait_ge(self.shifted, i + 1)
        dve.tensor_tensor(k.h_lo[:, i, :], k.h[:, i, :], k.h_hi[:, i, :].bitcast(F32), ALU.subtract).then_inc(self.h_ready, 1)

    def tensor(self, pe):
        pe.wait_ge(self.half_sum, 2)
        for i in range(2):
            mm = pe.matmul(self.k.bank(7)[:, 0:S], self.k.ones, self.sq[:, i, :], start=(i == 0), stop=(i == 1))
        mm.then_inc(self.sum_ready, 1)

    def scalar(self, act):
        k = self.k
        act.activation(self.sq[:, 4:7, :], k.x[:, 4:7, :], ACT.Square).then_inc(self.sq_ready, 1)
        act.wait_ge(self.sum_ready, 1)
        act.activation(self.ln[:], k.bank(7)[:, 0:S], ACT.Ln, scale=1.0 / D, bias=k.eps).then_inc(self.ln_ready, 1)
        act.wait_ge(self.ln_ready, 1)
        act.activation(self.rs[:], self.ln[:], ACT.Exp, scale=-0.5).then_inc(self.rs_ready, 1)
        for i in range(KD):
            act.wait_ge(self.scaled, i + 1)
            if self.shift is None:
                act.activation(k.h_hi[:, i, :], k.h[:, i, :], ACT.Copy).then_inc(self.rounded, 1)
            else:
                act.activation(k.h[:, i, :], k.h[:, i, :], ACT.Identity, bias=self.shift[:, i:i + 1]).then_inc(self.shifted, 1)
                act.wait_ge(self.shifted, i + 1)
                act.activation(k.h_hi[:, i, :], k.h[:, i, :], ACT.Copy).then_inc(self.rounded, 1)


def norm_stream(k, name, scale, shift=None):
    with stage(k, name) as (block, sem, buf):
        norm = StreamNorm(k, sem, buf, scale, shift)
        block.gpsimd(norm.pool)
        block.vector(norm.vector)
        block.tensor(norm.tensor)
        block.scalar(norm.scalar)


def norm_items(src, dst, w, after=None, split=None):
    fl = lambda t: t.rearrange("q a s -> q (a s)")
    part = lambda t, i: fl(t[:, i:i + 2, :])
    return [(part(src, i), part(dst, i), w, None if after is None else part(after, i),
             None if split is None else (part(split[0], i), part(split[1], i))) for i in range(0, src.shape[1], 2)]


def norm_heads(k, name, items, ones, width, batch, side=None, steps=0):
    n = len(items)
    side = side or ALONE
    assert n % batch == 0
    with stage(k, name) as (block, sem, buf):
        sq = buf("sq", [P, batch, BANK])
        sq_ready, sum_ready, ln_ready, rs_ready, scaled, done, rounded, low = map(
            sem, ("sq_ready", "sum_ready", "ln_ready", "rs_ready", "scaled", "done", "rounded", "low"))

        def square(eng, g, half):
            src, h = items[g][0], slice(half * S, (half + 1) * S)
            if g >= batch:
                eng.wait_ge(done, g - batch + 1)
            eng.tensor_tensor(sq[:, g % batch, h], src[:, h], src[:, h], ALU.mult).then_inc(sq_ready[half], 1)

        sq_ready = (sq_ready, sem("sq_ready_pool"))

        @block.gpsimd
        def _(pool):
            for g in range(n):
                square(pool, g, 1)

        @block.tensor
        def _(pe):
            for g in range(n):
                for half in range(2):
                    pe.wait_ge(sq_ready[half], g + 1)
                if g >= 8:
                    pe.wait_ge(ln_ready, g - 7)
                pe.matmul(k.bank(g % 8), ones, sq[:, g % batch, :], start=True, stop=True).then_inc(sum_ready, 1)
            side.step("pe", pe, steps)

        @block.scalar
        def _(act):
            for first in range(0, n, batch):
                for g in range(first, first + batch):
                    act.wait_ge(sum_ready, g + 1)
                    act.activation(sq[:, g % batch, :], k.bank(g % 8), ACT.Ln, scale=1.0 / width,
                                   bias=k.eps).then_inc(ln_ready, 1)
                for g in range(first, first + batch):
                    act.wait_ge(ln_ready, g + 1)
                    act.activation(sq[:, g % batch, :], sq[:, g % batch, :], ACT.Exp, scale=-0.5).then_inc(rs_ready, 1)
                if first + batch == n:
                    side.step("act", act, steps)
                for g in range(first, first + batch):
                    if items[g][4]:
                        act.wait_ge(done, g + 1)
                        act.activation(items[g][4][0], items[g][1], ACT.Copy).then_inc(rounded, 1)

        @block.vector
        def _(dve):
            products, split = 0, 0
            for first in range(0, n, batch):
                for g in range(first, first + batch):
                    square(dve, g, 0)
                for g in range(first, first + batch):
                    src, dst, w, after, _ = items[g]
                    dve.wait_ge(rs_ready, g + 1)
                    ins = dve.scalar_tensor_tensor(out=dst, in0=src, scalar=w, in1=sq[:, g % batch, :],
                                                   op0=ALU.mult, op1=ALU.mult)
                    if after is None:
                        ins.then_inc(done, 1)
                    else:
                        products += 1
                        ins.then_inc(scaled, 1)
                        dve.wait_ge(scaled, products)
                        dve.tensor_tensor(dst, dst, after, ALU.mult).then_inc(done, 1)
                if first + batch == n:
                    side.step("dve", dve, steps)
                for g in range(first, first + batch):
                    if items[g][4]:
                        split += 1
                        hi, lo = items[g][4]
                        dve.wait_ge(rounded, split)
                        dve.tensor_tensor(lo, items[g][1], hi.bitcast(F32), ALU.subtract).then_inc(low, 1)

        side.load(block)


def gate_parts(k, branches, merged):
    nb = len(branches)

    def rhs(u):
        return branches[u // 8] if u % 2 else (k.h_hi[:], k.h_lo[:])

    def freed(pe, s, v):
        pe.wait_ge(s["product_done"] if v % 2 else s["gate_ready"], v // 2 + 1)

    def evac_act(act, u, ps, s, b):
        if u % 2 == 0:
            if u >= 4:
                act.wait_ge(s["product_done"], u // 2 - 1)
            act.activation(b["gate"][:, (u // 2) % 2, :], ps, ACT.Sigmoid).then_inc(s["gate_ready"], 1)

    def evac_dve(dve, u, ps, s, b):
        if u % 2 == 0:
            return
        g = u // 2
        dve.wait_ge(s["gate_ready"], g + 1)
        acc = b["acc"][:, g % 4, :]
        dve.tensor_tensor(acc if g < 4 else b["term"][:], ps, b["gate"][:, g % 2, :],
                          ALU.mult).then_inc(s["product_done"], 1)
        dve.wait_ge(s["product_done"], g + 1)
        if g >= 4:
            dve.tensor_tensor(acc, acc, b["term"][:], ALU.add).then_inc(s["summed"], 1)
            dve.wait_ge(s["summed"], g - 3)
        if g // 4 == nb - 1:
            hi, lo = (t[:, 2 * (g % 4):2 * (g % 4) + 2, :] for t in merged())
            dve.tensor_copy(hi, acc).then_inc(s["merged"], 1)
            dve.wait_ge(s["merged"], 2 * (g % 4) + 1)
            dve.tensor_tensor(lo, acc, hi.bitcast(F32), ALU.subtract).then_inc(s["merged"], 1)

    return dict(units=[KD, KD // 2] * (4 * nb), rhs=rhs, evac_act=evac_act, evac_dve=evac_dve, freed=freed,
                sems=("gate_ready", "product_done", "summed", "merged"),
                bufs=(("gate", [P, 2, BANK]), ("acc", [P, 4, BANK]), ("term", [P, BANK])))


class Side:

    def __init__(self, k, ctx, name, phase, units, rhs, evac_act=None, evac_dve=None, flush_act=None,
                 freed=None, sems=(), bufs=()):
        self.k, self.name, self.start, self.rhs = k, name, k.first[phase], rhs
        self.evacs, self.flush_act, self.freed = {"act": evac_act, "dve": evac_dve}, flush_act, freed
        self.sems = {x: k.nc.alloc_semaphore(f"{name}_side_{x}") for x in ("bank_freed", *sems)}
        self.bufs = {x: k.sbuf(f"{name}_side_{x}", sh, F32, ctx) for x, sh in bufs}
        self.unit_of = []
        for u, kt in enumerate(units):
            self.unit_of += [(u, kt, i) for i in range(2 * kt // SLOT)]
        self.n = len(self.unit_of)
        self.done = {"pe": 0, "act": 0, "dve": 0}

    def bank(self, u):
        return self.k.bank(6 + u % 2)

    def multiply(self, pe, j):
        k = self.k
        u, kt, i = self.unit_of[j]
        if i == 0 and u >= 2:
            if self.freed:
                self.freed(pe, self.sems, u - 2)
            else:
                pe.wait_ge(self.sems["bank_freed"], u - 1)
        hi, lo = self.rhs(u)
        s = self.start + j
        pe.wait_ge(k.slot_split, s + 1)
        for t in range(SLOT):
            half, kk = (SLOT * i + t) // kt, (SLOT * i + t) % kt
            o = self.bank(u)[:, half * S:(half + 1) * S]
            w_hi, w_lo = (w[:, s % SPLIT, bass.ts(t, P)] for w in (k.w_hi, k.w_lo))
            pe.matmul(o, w_hi, hi[:, kk, :], start=(kk == 0), stop=False)
            pe.matmul(o, w_hi, lo[:, kk, :], start=False, stop=False)
            mm = pe.matmul(o, w_lo, hi[:, kk, :], start=False, stop=(kk == kt - 1))
        mm.then_inc(k.slot_used, 1)

    def evacuate(self, e, eng, j):
        u, kt, i = self.unit_of[j]
        if self.evacs[e] and i == 2 * kt // SLOT - 1:
            eng.wait_ge(self.k.slot_used, self.start + j + 1)
            self.evacs[e](eng, u, self.bank(u), self.sems, self.bufs)

    def step(self, e, eng, count=1):
        for _ in range(count):
            j = self.done[e]
            if j == self.n:
                return
            self.done[e] += 1
            if e == "pe":
                self.multiply(eng, j)
                continue
            upto = self.start + j + 1 + LOOK
            self.k.split_hi(eng, upto) if e == "act" else self.k.split_lo(eng, upto)
            if j >= 1:
                self.evacuate(e, eng, j - 1)

    def load(self, block):
        assert self.done["pe"] == self.done["act"] == self.done["dve"], self.done
        last = min(self.start + self.done["dve"] + LOOK, self.k.gemms) - 1
        block.sync(lambda sp: self.k.load_slots(sp, self.k.place[last] + 1 + RAW))

    def finish(self, loads=()):
        k = self.k
        with stage(k, f"{self.name}_end") as (block, sem, buf):
            loaded = sem("table_loaded")

            @block.scalar
            def _(act):
                self.step("act", act, self.n)
                self.evacuate("act", act, self.n - 1)
                if self.flush_act:
                    self.flush_act(act, self.sems, self.bufs)

            @block.vector
            def _(dve):
                self.step("dve", dve, self.n)
                self.evacuate("dve", dve, self.n - 1)

            @block.tensor
            def _(pe):
                self.step("pe", pe, self.n)

            @block.sync
            def _(sp):
                for dst, src in loads:
                    sp.dma_start(dst, src).then_inc(loaded, 16)
                k.load_slots(sp, k.place[self.start + self.n - 1] + 1 + RAW)
                if loads:
                    sp.wait_ge(loaded, 16 * len(loads))
        k.to_clear += self.sems.values()


class NoSide:

    def step(self, e, eng, count=1):
        pass

    def load(self, block):
        pass


ALONE = NoSide()


def residual_projection(k, name, phase, units, hi, lo, gain=None, first_bank=0):
    def evac_dve(dve, u, ps, s, b):
        for half in range(2):
            i = 2 * u + half
            o = ps[:, half * S:(half + 1) * S]
            if gain is None:
                ins = dve.tensor_tensor(k.x[:, i, :], o, k.x[:, i, :], ALU.add)
            else:
                ins = dve.scalar_tensor_tensor(out=k.x[:, i, :], in0=o, scalar=gain[:, i:i + 1],
                                               in1=k.x[:, i, :], op0=ALU.mult, op1=ALU.add)
        ins.then_inc(s["bank_freed"], 1)

    projection(k, name, phase, units, lambda u: (hi, lo), None, evac_dve, first_bank=first_bank)


def plain_parts(k, n_units, place):
    def evac_act(act, u, ps, s, b):
        dst, f = place(u)
        act.activation(dst, ps, f).then_inc(s["bank_freed"], 1)

    return dict(units=[KD] * n_units, rhs=lambda u: (k.h_hi[:], k.h_lo[:]), evac_act=evac_act)


def conv_parts(k, n_units, n_conv, place, taps, shift, bias=None):
    nt = len(taps)

    def evac_act(act, u, ps, s, b):
        if u >= n_conv:
            if u == n_conv:
                silu(act, u - 1, s, b)
            dst, f = place(u)
            act.activation(dst, ps, f).then_inc(s["bank_freed"], 1)
            return
        if u >= 2:
            act.wait_ge(s["silu_done"], u - 1)
        for half in range(2):
            i = 2 * u + half
            o, t = ps[:, half * S:(half + 1) * S], b["conv"][:, u % 2, half * S:(half + 1) * S]
            if bias is None:
                ins = act.activation(t, o, ACT.Copy, scale=taps[shift][:, i:i + 1])
            else:
                ins = act.activation(t, o, ACT.Identity, scale=taps[shift][:, i:i + 1], bias=bias[:, i:i + 1])
            ins.then_inc(s["centre"], 1)
        if u >= 1:
            silu(act, u - 1, s, b)

    def silu(act, u, s, b):
        act.wait_ge(s["bank_freed"], u + 1)
        act.activation(place(u)[0], b["conv"][:, u % 2, :], ACT.Silu).then_inc(s["silu_done"], 1)

    def flush_act(act, s, b):
        if n_conv == n_units:
            silu(act, n_units - 1, s, b)

    def evac_dve(dve, u, ps, s, b):
        if u >= n_conv:
            return
        dve.wait_ge(s["centre"], 2 * u + 2)
        for j in range(nt):
            if j == shift:
                continue
            d = j - shift
            for half in range(2):
                i = 2 * u + half
                a, z = max(0, -d), S - max(0, d)
                o = ps[:, half * S + a + d:half * S + z + d]
                t = b["conv"][:, u % 2, half * S + a:half * S + z]
                ins = dve.scalar_tensor_tensor(out=t, in0=o, scalar=taps[j][:, i:i + 1], in1=t,
                                               op0=ALU.mult, op1=ALU.add)
                ins.then_inc(s["tap"], 1)
                if half == 1 and (j, half) != last_tap:
                    tapped = 2 * (nt - 1) * u + 2 * (j + 1 - (j > shift))
                    dve.wait_ge(s["tap"], tapped)
        dve.wait_ge(s["tap"], 2 * (nt - 1) * (u + 1))
        dve.sem_inc(s["bank_freed"], 1)

    last_tap = (nt - 1 if shift != nt - 1 else nt - 2, 1)
    return dict(units=[KD] * n_units, rhs=lambda u: (k.h_hi[:], k.h_lo[:]), evac_act=evac_act, evac_dve=evac_dve,
                flush_act=flush_act, sems=("centre", "tap", "silu_done"), bufs=(("conv", [P, 2, BANK]),))


def feed_forward(k, name, phase, norm, gain=None, conv=None):
    with ExitStack() as c:
        g_hi = k.sbuf(f"{name}_g_hi", [P, NF, S], F32R, c)
        g_lo = k.sbuf(f"{name}_g_lo", [P, NF, S], F32R, c)

        def finish(dve, f, gate, up, s, b):
            g = b["g"][:, f % 2, :]
            dve.tensor_tensor(g, up, gate, ALU.mult).then_inc(s["product"], 1)
            dve.wait_ge(s["product"], f + 1)
            dve.tensor_copy(g_hi[:, f, :], g).then_inc(s["rounded"], 1)
            dve.wait_ge(s["rounded"], f + 1)
            dve.tensor_tensor(g_lo[:, f, :], g, g_hi[:, f, :].bitcast(F32), ALU.subtract).then_inc(s["g_split"], 1)

        if conv is None:
            def evac_act(act, f, ps, s, b):
                if f >= 2:
                    act.wait_ge(s["product"], f - 1)
                act.activation(b["gate"][:, f % 2, 0:S], ps[:, 0:S], ACT.Silu).then_inc(s["gate_ready"], 1)

            def evac_dve(dve, f, ps, s, b):
                dve.wait_ge(s["gate_ready"], f + 1)
                finish(dve, f, b["gate"][:, f % 2, 0:S], ps[:, S:2 * S], s, b)

            freed = lambda pe, s, v: pe.wait_ge(s["product"], v + 1)
            flush_act = flush_dve = None
        else:
            def silu(act, f, s, b):
                act.wait_ge(s["convolved"], f + 1)
                act.activation(b["gate"][:, f % 2, 0:S], b["gate"][:, f % 2, 0:S], ACT.Silu).then_inc(s["gate_ready"], 1)

            def evac_act(act, f, ps, s, b):
                if f >= 2:
                    act.wait_ge(s["product"], f - 1)
                for half in range(2):
                    act.activation(b["gate"][:, f % 2, half * S:(half + 1) * S], ps[:, half * S:(half + 1) * S],
                                   ACT.Copy, scale=conv[1][:, half * NF + f:half * NF + f + 1]).then_inc(s["centre"], 1)
                if f >= 1:
                    silu(act, f - 1, s, b)

            def product(dve, f, s, b):
                dve.wait_ge(s["gate_ready"], f + 1)
                t = b["gate"][:, f % 2, :]
                finish(dve, f, t[:, 0:S], t[:, S:2 * S], s, b)

            def evac_dve(dve, f, ps, s, b):
                dve.wait_ge(s["centre"], 2 * f + 2)
                t = b["gate"][:, f % 2, :]
                for j, (a, z) in ((0, (1, S)), (2, (0, S - 1))):
                    for half in range(2):
                        o = half * S
                        w = conv[j][:, half * NF + f:half * NF + f + 1]
                        ins = dve.scalar_tensor_tensor(out=t[:, o + a:o + z], in0=ps[:, o + a + j - 1:o + z + j - 1],
                                                       scalar=w, in1=t[:, o + a:o + z], op0=ALU.mult, op1=ALU.add)
                        ins.then_inc(s["tap"] if (j, half) != (2, 1) else s["convolved"], 1)
                    if j == 0:
                        dve.wait_ge(s["tap"], 3 * f + 2)
                dve.wait_ge(s["tap"], 3 * f + 3)
                dve.wait_ge(s["convolved"], f + 1)
                if f >= 1:
                    product(dve, f - 1, s, b)

            freed = lambda pe, s, v: pe.wait_ge(s["convolved"], v + 1)
            flush_act = lambda act, s, b: silu(act, NF - 1, s, b)
            flush_dve = lambda dve, s, b: product(dve, NF - 1, s, b)

        projection(k, f"{name}_up", phase, [KD] * NF, lambda u: (k.h_hi[:], k.h_lo[:]), evac_act, evac_dve,
                   flush_act, flush_dve, freed=freed, norm=norm,
                   sems=("centre", "tap", "convolved", "gate_ready", "product", "rounded", "g_split"),
                   bufs=(("gate", [P, 2, BANK]), ("g", [P, 2, S])))
        residual_projection(k, f"{name}_down", k.first[phase] + 2 * NF * KD // SLOT, [NF] * (KD // 2), g_hi[:], g_lo[:],
                            gain, first_bank=4)


def to_token_major(k, name, items, loads=()):
    flat = [(src[:, t * P:(t + 1) * P], dst[t]) for src, dst in items for t in range(ST)]
    assert len(flat) <= 32
    with stage(k, name) as (block, sem, buf):
        transposed, moved, loaded = sem("transposed"), sem("moved"), sem("table_loaded")

        if loads:
            @block.sync
            def _(sp):
                for dst, src in loads:
                    sp.dma_start(dst, src).then_inc(loaded, 16)
                sp.wait_ge(loaded, 16 * len(loads))

        @block.tensor
        def _(pe):
            for i, (src, dst) in enumerate(flat):
                mm = pe.transpose(k.bank(i // 4 % 8)[:, bass.ts(i % 4, P)], src, k.ident)
                if i % 4 == 3:
                    mm.then_inc(transposed, 1)

        def move(e, q):
            def go(eng):
                for g in range(q, len(flat) // 4, 2):
                    eng.wait_ge(transposed, g + 1)
                    for i in range(4 * g, 4 * g + 4):
                        o = k.bank(g % 8)[:, bass.ts(i % 4, P)]
                        if e == "dve":
                            ins = eng.tensor_copy(flat[i][1], o)
                        else:
                            ins = eng.activation(flat[i][1], o, ACT.Copy)
                    ins.then_inc(moved, 1)
            return go

        block.vector(move("dve", 0))
        block.scalar(move("act", 1))


def window_attention(k, name, q, kk, vt, dist, o_hi, o_lo):
    G = 3
    H = 8
    slope = lambda g, h: 2.0 ** (-8.0 * (g * H + h + 1) / (G * H))
    its = [(hp, t, par) for hp in range(H // 2) for t in range(ST) for par in range(2)]
    n = len(its)
    with stage(k, name) as (block, sem, buf):
        sc = buf("scores", [P, 3, G * S])
        pt = buf("pt", [P, 2, 2 * G, P])
        out = buf("out", [P, H // 2, S])
        nmax, l, rl = buf("nmax", [P, 2]), buf("l", [P, 2]), buf("rl", [P, 2])
        qk_done, biased, max_ready, exp_done, recip, probs, turned, moved, pv_done, out_ready, rounded = map(
            sem, ("qk_done", "biased", "max_ready", "exp_done", "recip", "probs", "turned", "moved", "pv_done",
                  "out_ready", "rounded"))
        score = lambda i: k.bank(2 * its[i][2], 2)

        @block.tensor
        def _(pe):
            def qk(i):
                hp, t, par = its[i]
                if i >= 2:
                    pe.wait_ge(biased, G * (i - 1))
                rows = slice(64 * par, 64 * par + 64)
                for g in range(G):
                    mm = pe.matmul(score(i)[:, bass.ts(g, S)], q[rows, g * 4 + hp, bass.ts(t, P)],
                                   kk[rows, g * 4 + hp, :], start=True, stop=True)
                mm.then_inc(qk_done, 1)

            def turn(i):
                pe.wait_ge(probs, i + 1)
                if i >= 1:
                    pe.wait_ge(moved, 2 * i)
                for j in range(2 * G):
                    mm = pe.transpose(k.bank(4, 2)[:, bass.ts(j, P)], sc[:, i % 3, bass.ts(j, P)], k.ident)
                mm.then_inc(turned, 1)

            def pv(i):
                hp, t, par = its[i]
                pe.wait_ge(moved, 2 * i + 2)
                if i >= 2:
                    pe.wait_ge(out_ready, i - 1)
                for j in range(2 * G):
                    g, st = j // 2, j % 2
                    mm = pe.matmul(k.bank(6 + par)[64 * par:64 * par + 64, 0:P],
                                   vt[:, st, g * 4 + hp, 64 * par:64 * par + 64], pt[:, i % 2, j, :],
                                   start=(j == 0), stop=(j == 2 * G - 1))
                mm.then_inc(pv_done, 1)

            for i in range(n + 3):
                if i < n:
                    qk(i)
                if 2 <= i < n + 2:
                    turn(i - 2)
                if i >= 3:
                    pv(i - 3)

        @block.vector
        def _(dve):
            def bias(i):
                hp, t, par = its[i]
                dve.wait_ge(qk_done, i + 1)
                if i >= 3:
                    dve.wait_ge(turned, i - 2)
                for g in range(G):
                    dve.scalar_tensor_tensor(out=sc[:, i % 3, bass.ts(g, S)], in0=dist[:, t, g, :],
                                             scalar=-slope(g, 2 * hp + par), in1=score(i)[:, bass.ts(g, S)],
                                             op0=ALU.mult, op1=ALU.add).then_inc(biased, 1)
                dve.wait_ge(biased, G * (i + 1))
                dve.tensor_reduce(nmax[:, i % 2:i % 2 + 1], sc[:, i % 3, :], AX.X, ALU.max,
                                  negate=True).then_inc(max_ready, 1)

            def normalise(i):
                dve.wait_ge(exp_done, i + 1)
                dve.reciprocal(rl[:, i % 2:i % 2 + 1], l[:, i % 2:i % 2 + 1]).then_inc(recip, 1)
                dve.wait_ge(recip, i + 1)
                dve.tensor_scalar(sc[:, i % 3, :], sc[:, i % 3, :], rl[:, i % 2:i % 2 + 1], None,
                                  ALU.mult).then_inc(probs, 1)

            def store(i):
                hp, t, par = its[i]
                dve.wait_ge(pv_done, i + 1)
                dve.tensor_copy(out[64 * par:64 * par + 64, hp, bass.ts(t, P)],
                                k.bank(6 + par)[64 * par:64 * par + 64, 0:P]).then_inc(out_ready, 1)

            for i in range(n + 4):
                if i < n:
                    bias(i)
                if 1 <= i <= n:
                    normalise(i - 1)
                if i >= 4:
                    store(i - 4)
            dve.wait_ge(out_ready, n)
            split_activation(dve, Chain(dve, rounded), out[:], o_hi, o_lo)

        @block.scalar
        def _(act):
            def expo(i):
                act.wait_ge(max_ready, i + 1)
                act.activation(sc[:, i % 3, :], sc[:, i % 3, :], ACT.Exp, bias=nmax[:, i % 2:i % 2 + 1],
                               accum_out=l[:, i % 2:i % 2 + 1]).then_inc(exp_done, 1)

            def move(i):
                act.wait_ge(turned, i + 1)
                if i >= 2:
                    act.wait_ge(pv_done, i - 1)
                act.activation(pt[:, i % 2, 0:4, :], k.bank(4), ACT.Copy).then_inc(moved, 1)
                act.activation(pt[:, i % 2, 4:6, :], k.bank(5)[:, 0:2 * P], ACT.Copy).then_inc(moved, 1)

            for i in range(n + 2):
                if i < n:
                    expo(i)
                if i >= 2:
                    move(i - 2)


NU = NCH * PAIRS0
UW = NU * CH


def halves():
    for par in range(2):
        yield par, slice(64 * par, 64 * par + 64)


def dn_gates(k, wab, dtb, alog, g, beta):
    with stage(k, "dng") as (block, sem, buf):
        sa, sb, ab, e1, l1, e2, na = (buf(x, [P, 2, NU]) for x in ("sa", "sb", "abs", "e1", "l1", "e2", "na"))
        ea = buf("ea", [P, 8])
        projected, dsteps, asteps = map(sem, ("projected", "vector_steps", "scalar_steps"))
        o = k.bank(0)[:, 0:64].rearrange("q (c n d p) -> q c n d p", c=NCH, n=2, d=2)

        @block.tensor
        def _(pe):
            for c in range(NCH):
                for par, rows in halves():
                    for i in range(KD):
                        mm = pe.matmul(k.bank(0)[rows, bass.ts(c, 16)], k.h[:, i, bass.ts(c, CH)],
                                       wab[:, i, par, :], start=(i == 0), stop=(i == KD - 1))
            mm.then_inc(projected, 1)

        @block.vector
        def _(dve):
            step = Chain(dve, dsteps)
            dve.wait_ge(projected, 1)
            for d in range(2):
                step(dve.tensor_tensor(sa[:, d].rearrange("q (c p) -> q c p", c=NCH), o[:, :, 0, d, :],
                                       bc(dtb[:, 4 * d:4 * d + 4].unsqueeze(1), [P, NCH, 4]), ALU.add))
                step(dve.tensor_copy(sb[:, d].rearrange("q (c p) -> q c p", c=NCH), o[:, :, 1, d, :]))
            step(dve.scalar_tensor_tensor(out=ab[:], in0=sa[:], scalar=-1.0, in1=sa[:], op0=ALU.mult, op1=ALU.max))
            dve.wait_ge(asteps, 4)
            step(dve.scalar_tensor_tensor(out=l1[:], in0=sa[:], scalar=0.0, in1=l1[:], op0=ALU.max, op1=ALU.add))
            step(dve.tensor_scalar(ea[:], ea[:], -1.0, None, ALU.mult))
            for d in range(2):
                step(dve.tensor_tensor(g[:, d].rearrange("q (c p) -> q c p", c=NCH),
                                       l1[:, d].rearrange("q (c p) -> q c p", c=NCH),
                                       bc(ea[:, 4 * d:4 * d + 4].unsqueeze(1), [P, NCH, 4]), ALU.mult))
            step(dve.tensor_scalar(e2[:], e2[:], 1.0, None, ALU.add))
            step(dve.reciprocal(beta, e2[:]))

        @block.scalar
        def _(act):
            step = Chain(act, asteps)
            act.wait_ge(dsteps, 5)
            step(act.activation(e1[:], ab[:], ACT.Exp, scale=-1.0))
            step(act.activation(l1[:], e1[:], ACT.Ln, bias=1.0))
            step(act.activation(e2[:], sb[:], ACT.Exp, scale=-1.0))
            step(act.activation(ea[:], alog[:], ACT.Exp))


def dn_decays(k, c, g, beta, A, q, ee, bg):
    gm, decay, qd, bm = A["gm"], A["decay"], A["qd"], A["bm"]
    units = lambda t, d: t[:, d * UW:(d + 1) * UW].rearrange("q (u i) -> q u i", i=CH)
    with stage(k, "dnd") as (block, sem, buf):
        gm_ready, bm_ready, sums, exps, qd_done, ee_sum, ee_done = map(
            sem, ("gm_ready", "bm_ready", "sums", "exps", "qd_done", "ee_sum", "ee_done"))

        def spread(eng, dst, col, pattern, d, s):
            eng.tensor_tensor(units(dst, d), bc(col[:, d].unsqueeze(2), [P, NU, CH]),
                              bc(pattern.unsqueeze(1), [P, NU, CH]), ALU.mult).then_inc(s, 1)

        @block.gpsimd
        def _(pool):
            spread(pool, bm, beta, c["eye64"], 0, bm_ready)
            spread(pool, bm, beta, c["eye64"], 1, bm_ready)

        @block.vector
        def _(dve):
            spread(dve, gm, g, c["tri"][:, 0], 0, gm_ready)
            spread(dve, gm, g, c["tri"][:, 1], 1, gm_ready)
            for d in range(2):
                dve.wait_ge(exps, 3 + 3 * d)
                for p in range(PAIRS0):
                    u = units(qd, d).rearrange("q (c p) i -> q c p i", p=PAIRS0)[:, :, p, :]
                    dve.tensor_tensor(u, u, q[:, p, :].rearrange("q (c i) -> q c i", c=NCH), ALU.mult).then_inc(qd_done, 1)
            dve.wait_ge(ee_done, 1)
            dve.tensor_tensor(bg, beta, ee[:, 0], ALU.mult).then_inc(qd_done, 1)

        @block.tensor
        def _(pe):
            for d in range(2):
                pe.wait_ge(gm_ready, d + 1)
                for i in range(2):
                    mm = pe.matmul(k.bank(2 * d + i), c["seg"][:, d, :], gm[:, bass.ts(2 * d + i, BANK)],
                                   start=True, stop=True).then_inc(sums, 1)
                for i in range(2):
                    mm = pe.matmul(k.bank(4 + 2 * d + i), k.head_ones, gm[:, bass.ts(2 * d + i, BANK)],
                                   start=True, stop=True).then_inc(sums, 1)
            pe.wait_ge(exps, 1)
            for d in range(2):
                for i, m in enumerate((c["cum"][:, d, :], c["seg"][:, d, :], k.head_ones)):
                    mm = pe.matmul(k.bank(0)[:, (2 * i + d) * NU:(2 * i + d + 1) * NU], m, g[:, d, :],
                                   start=True, stop=True)
            mm.then_inc(ee_sum, 1)

        @block.scalar
        def _(act):
            for n, (d, what) in enumerate(((0, 0), (0, 1), (1, 0), (1, 1))):
                act.wait_ge(sums, 2 * n + 2)
                if what == 0:
                    for i in range(2):
                        act.activation(decay[:, bass.ts(2 * d + i, BANK)], k.bank(2 * d + i), ACT.Exp).then_inc(exps, 1)
                else:
                    act.activation(qd[:, d * UW:(d + 1) * UW], k.bank(4 + 2 * d, 2), ACT.Exp).then_inc(exps, 1)
            act.wait_ge(ee_sum, 1)
            act.activation(ee.rearrange("q a d u -> q (a d u)"), k.bank(0)[:, 0:6 * NU], ACT.Exp).then_inc(ee_done, 1)


def dn_systems(k, c, A, q, kk):
    decay, qk, bm = A["decay"], A["qk"], A["bm"]
    units = lambda t, d: t[:, d * UW:(d + 1) * UW].rearrange("q (u i) -> q u i", i=CH)
    with stage(k, "dns") as (block, sem, buf):
        betas, grams, steps = map(sem, ("betas", "grams", "steps"))

        @block.tensor
        def _(pe):
            for i in range(4):
                mm = pe.matmul(k.bank(i), k.head_ones, bm[:, bass.ts(i, BANK)], start=True, stop=True)
            mm.then_inc(betas, 1)
            for rhs, first in ((q, 6), (kk, 4)):
                for ch in range(NCH):
                    for p in range(PAIRS0):
                        u = ch * PAIRS0 + p
                        for par, rows in halves():
                            mm = pe.matmul(k.bank(first, 2)[rows, bass.ts(u, CH)], kk[rows, p, bass.ts(ch, CH)],
                                           rhs[rows, p, bass.ts(ch, CH)], start=True, stop=True)
                mm.then_inc(grams, 1)

        @block.vector
        def _(dve):
            step = Chain(dve, steps)
            for d in range(2):
                step(dve.tensor_tensor(units(decay, d), units(decay, d),
                                       bc(c["tri"][:, d].unsqueeze(1), [P, NU, CH]), ALU.mult))
            dve.wait_ge(betas, 1)
            dve.wait_ge(grams, 1)
            for d in range(2):
                w = slice(d * UW, (d + 1) * UW)
                step(dve.tensor_tensor(qk[:, w], k.bank(6, 2), decay[:, w], ALU.mult))
                step(dve.tensor_tensor(decay[:, w], k.bank(2 * d, 2), decay[:, w], ALU.mult))
            dve.wait_ge(grams, 2)
            for d in range(2):
                w = slice(d * UW, (d + 1) * UW)
                step(dve.tensor_tensor(decay[:, w], k.bank(4, 2), decay[:, w], ALU.mult))


def dn_inverse(k, c, A):
    b, y, t, rs, bl = A["decay"], A["y"], A["t"], A["r"], A["bl"]
    units = lambda x, d: x[:, d * UW:(d + 1) * UW].rearrange("q (u i) -> q u i", i=CH)
    levels = 6
    with stage(k, "dni") as (block, sem, buf):
        bl_ready, y_ready, t_ready, r_done, r_moved, z_done, zt_done = map(
            sem, ("bl_ready", "y_ready", "t_ready", "r_done", "r_moved", "z_done", "zt_done"))

        def each(f):
            for u in range(NU):
                for par, rows in halves():
                    mm = f(u, rows)
            return mm

        r_bank = lambda l, d: 4 * (l % 2) + 2 * d
        zt_bank = lambda l, d: 4 * ((l + 1 + d) % 2)
        z_bank = lambda l, d: zt_bank(l, d) + 2

        @block.gpsimd
        def _(pool):
            for l in range(levels):
                for d in range(2):
                    if l >= 2:
                        pool.wait_ge(r_done, 2 * (l - 1) + d + 1)
                    elif l == 1:
                        pool.wait_ge(y_ready, d + 1)
                    pool.tensor_tensor(units(bl, d), units(b, d), bc(c["lev"][:, d, l].unsqueeze(1), [P, NU, CH]),
                                       ALU.mult).then_inc(bl_ready, 1)

        @block.vector
        def _(dve):
            for d in range(2):
                dve.wait_ge(bl_ready, d + 1)
                dve.tensor_tensor(units(y, d), bc(c["eye64"].unsqueeze(1), [P, NU, CH]), units(bl, d),
                                  ALU.subtract).then_inc(y_ready, 1)
            for l in range(1, levels):
                for d in range(2):
                    w = slice(d * UW, (d + 1) * UW)
                    n = 2 * (l - 1) + d
                    dve.wait_ge(y_ready, n + 1)
                    if l < levels - 1:
                        dve.wait_ge(zt_done, n + 1)
                        dve.wait_ge(t_ready, n + 1)
                        dve.tensor_tensor(t[:, w], t[:, w], k.bank(zt_bank(l, d), 2), ALU.subtract).then_inc(t_ready, 1)
                    dve.wait_ge(z_done, n + 1)
                    dve.tensor_tensor(y[:, w], y[:, w], k.bank(z_bank(l, d), 2), ALU.subtract).then_inc(y_ready, 1)

        @block.tensor
        def _(pe):
            def product(first, d, lhs, rhs):
                return each(lambda u, rows: pe.matmul(k.bank(first, 2)[rows, bass.ts(u, CH)],
                                                      lhs[rows, bass.ts(d * NU + u, CH)],
                                                      rhs[rows, bass.ts(d * NU + u, CH)] if rhs is not None
                                                      else c["eye64"][rows, :], start=True, stop=True))
            for d in range(2):
                pe.wait_ge(y_ready, d + 1)
                product(r_bank(0, d), d, y, None).then_inc(r_done, 1)
            for l in range(1, levels):
                for d in range(2):
                    n = 2 * l + d
                    pe.wait_ge(bl_ready, n + 1)
                    pe.wait_ge(t_ready, n - 1)
                    if d == 1:
                        pe.wait_ge(y_ready, n - 2)
                    product(r_bank(l, d), d, bl, t).then_inc(r_done, 1)
                for d in range(2):
                    n = 2 * l + d
                    pe.wait_ge(r_moved, n + 1)
                    pe.wait_ge(y_ready, 2 * l)
                    if l < levels - 1:
                        product(zt_bank(l, d), d, y, rs).then_inc(zt_done, 1)
                    product(z_bank(l, d), d, rs, y).then_inc(z_done, 1)

        @block.scalar
        def _(act):
            for l in range(levels):
                for d in range(2):
                    n = 2 * l + d
                    w = slice(d * UW, (d + 1) * UW)
                    act.wait_ge(r_done, n + 1)
                    if l == 0:
                        act.activation(t[:, w], k.bank(r_bank(l, d), 2), ACT.Copy).then_inc(t_ready, 1)
                        act.sem_inc(r_moved, 1)
                    else:
                        if l >= 2:
                            act.wait_ge(z_done, n - 3)
                        act.activation(rs[:, w], k.bank(r_bank(l, d), 2), ACT.Copy).then_inc(r_moved, 1)


def dn_prepare(k, c, A, ktm, vtm, kk, v, beta, ee, bg):
    y = A["y"]
    units = lambda x, d: x[:, d * UW:(d + 1) * UW].rearrange("q (u i) -> q u i", i=CH)
    with stage(k, "dnp") as (block, sem, buf):
        turned, moved, scaled, w_done, w_moved = map(sem, ("turned", "moved", "scaled", "w_done", "w_moved"))

        @block.tensor
        def _(pe):
            for first, src in ((0, kk), (2, v)):
                for ch in range(NCH):
                    for p in range(PAIRS0):
                        for par, rows in halves():
                            mm = pe.matmul(k.bank(first, 2)[rows, bass.ts(ch * PAIRS0 + p, CH)],
                                           src[rows, p, bass.ts(ch, CH)], c["eye64"][rows, :], start=True, stop=True)
                mm.then_inc(turned, 1)
            for d in range(2):
                pe.wait_ge(scaled, d + 1)
                for u in range(NU):
                    for par, rows in halves():
                        mm = pe.matmul(k.bank(4 + 2 * d, 2)[rows, bass.ts(u, CH)], A["kb"][rows, bass.ts(d * NU + u, CH)],
                                       y[rows, bass.ts(d * NU + u, CH)], start=True, stop=True)
                mm.then_inc(w_done, 1)

        @block.scalar
        def _(act):
            act.wait_ge(turned, 1)
            act.activation(ktm, k.bank(0, 2), ACT.Copy).then_inc(moved, 1)
            act.wait_ge(turned, 2)
            act.activation(vtm, k.bank(2, 2), ACT.Copy).then_inc(moved, 1)
            for d in range(2):
                act.wait_ge(w_done, d + 1)
                act.activation(A["wn"][:, d * UW:(d + 1) * UW], k.bank(4 + 2 * d, 2), ACT.Copy, scale=-1.0).then_inc(w_moved, 1)

        def scale(eng, dst, src, col, d):
            eng.tensor_tensor(units(dst, d), src.rearrange("q (u i) -> q u i", i=CH),
                              bc(col[:, d].unsqueeze(2), [P, NU, CH]), ALU.mult).then_inc(scaled, 1)

        @block.vector
        def _(dve):
            dve.wait_ge(moved, 1)
            for d in range(2):
                scale(dve, A["kb"], ktm, bg, d)
            dve.wait_ge(moved, 2)
            for d in range(2):
                scale(dve, A["vb"], vtm, beta, d)

        @block.gpsimd
        def _(pool):
            pool.wait_ge(scaled, 2)
            for d in range(2):
                scale(pool, A["kd"], ktm, ee[:, 1], d)


def dn_scan(k, A, ee, state, vn, o):
    y, vb, wn, qd, qk, kd = (A[x] for x in ("y", "vb", "wn", "qd", "qk", "kd"))
    with stage(k, "dnr") as (block, sem, buf):
        v_done, v_moved, o_done, o_added, up_done, decayed, state_ready = map(
            sem, ("v_done", "v_moved", "o_done", "o_added", "up_done", "decayed", "state_ready"))

        def cells(s):
            for d in range(2):
                ch = (s, NCH - 1 - s)[d]
                for p in range(PAIRS0):
                    u = (d * NCH + ch) * PAIRS0 + p
                    for par, rows in halves():
                        yield rows, bass.ts(d * PAIRS0 + p, CH), bass.ts(u, CH)

        @block.tensor
        def _(pe):
            for s in range(NCH):
                if s >= 1:
                    pe.wait_ge(state_ready, s)
                if s >= 2:
                    pe.wait_ge(v_moved, s - 1)
                for rows, w, u in cells(s):
                    mm = pe.matmul(k.bank(s % 2)[rows, w], y[rows, u], vb[rows, u], start=True, stop=(s == 0))
                    if s:
                        mm = pe.matmul(k.bank(s % 2)[rows, w], wn[rows, u], state[s % 2][rows, w], start=False, stop=True)
                mm.then_inc(v_done, 1)
                pe.wait_ge(v_moved, s + 1)
                if s < NCH - 1:
                    for rows, w, u in cells(s):
                        mm = pe.matmul(k.bank(4 + s % 2)[rows, w], kd[rows, u], vn[rows, w], start=True, stop=True)
                    mm.then_inc(up_done, 1)
                if s >= 2:
                    pe.wait_ge(o_added, 2 * (s - 1))
                for rows, w, u in cells(s):
                    if s:
                        pe.matmul(k.bank(2 + s % 2)[rows, w], state[s % 2][rows, w], qd[rows, u], start=True, stop=False)
                    mm = pe.matmul(k.bank(2 + s % 2)[rows, w], vn[rows, w], qk[rows, u], start=(s == 0), stop=True)
                mm.then_inc(o_done, 1)

        @block.scalar
        def _(act):
            for s in range(NCH):
                act.wait_ge(v_done, s + 1)
                if s >= 1:
                    act.wait_ge(o_done, s)
                act.activation(vn, k.bank(s % 2), ACT.Copy).then_inc(v_moved, 1)

        @block.vector
        def _(dve):
            n = 0
            for s in range(NCH):
                if s < NCH - 1:
                    if s == 0:
                        dve.wait_ge(up_done, 1)
                        dve.tensor_copy(state[1], k.bank(4)).then_inc(state_ready, 1)
                    else:
                        dve.wait_ge(state_ready, s)
                        dve.wait_ge(o_done, s)
                        new = state[(s + 1) % 2]
                        for d in range(2):
                            ch = (s, NCH - 1 - s)[d]
                            part = lambda t: t[:, d * 256:(d + 1) * 256].rearrange("q (p v) -> q p v", v=64)
                            dve.tensor_tensor(part(new), part(state[s % 2]),
                                              bc(ee[:, 2, d, ch * 4:ch * 4 + 4].unsqueeze(2), [P, 4, 64]),
                                              ALU.mult).then_inc(decayed, 1)
                        dve.wait_ge(decayed, 2 * s)
                        dve.wait_ge(up_done, s + 1)
                        dve.tensor_tensor(new, new, k.bank(4 + s % 2), ALU.add).then_inc(state_ready, 1)
                dve.wait_ge(o_done, s + 1)
                for d in range(2):
                    ch = (s, NCH - 1 - s)[d]
                    dst = o[:, :, bass.ts(ch, CH)]
                    src = k.bank(2 + s % 2)[:, d * 256:(d + 1) * 256].rearrange("q (p i) -> q p i", i=CH)
                    if s < 2:
                        dve.tensor_copy(dst, src).then_inc(o_added, 1)
                    else:
                        dve.wait_ge(o_added, 4)
                        dve.tensor_tensor(dst, dst, src, ALU.add).then_inc(o_added, 1)


def first_loads(k, par, qn):
    d = k.dram
    with stage(k, "load") as (block, sem, buf):
        loaded, cond_loaded, cond_ready, qn_scaled = map(sem, ("loaded", "cond_loaded", "cond_ready", "qn_scaled"))

        @block.sync
        def _(sp):
            for dst, src in ((k.x[:], d["x_t"]), (k.consts[:], d["consts"]), (par, d["cols0"])):
                sp.dma_start(dst, src).then_inc(loaded, 16)
            k.load_slots(sp, RAW)
            sp.wait_ge(loaded, 3 * 16)

        @block.vector
        def _(dve):
            dve.wait_ge(loaded, 3 * 16)
            dve.tensor_scalar(qn, qn, 64 ** -0.5, None, ALU.mult).then_inc(qn_scaled, 1)

        @block.scalar
        def _(act):
            act.dma_start(k.cond[:], d["cond"].to_broadcast([P, D])).then_inc(cond_loaded, 16)
            act.wait_ge(cond_loaded, 16)
            act.activation(k.cond[:], k.cond[:], ACT.Silu).then_inc(cond_ready, 1)


def first_block(k):
    d = k.dram
    with ExitStack() as c0:
        par = k.sbuf("cols0", [P, COLS0], F32, c0)
        col = {n: par[:, a:z] for n, (a, z) in COL0.items()}
        with ExitStack() as c1:
            y_hi = k.sbuf("mix_hi", [P, 2, 4, S], F32R, c1)
            y_lo = k.sbuf("mix_lo", [P, 2, 4, S], F32R, c1)
            with ExitStack() as c2:
                wab = k.sbuf("wab", [P, KD, 2, 16], F32, c2)
                tab = k.sbuf("dn_tables", [P, DN_TABLE], F32, c2)
                qkv = k.sbuf("qkv", [P, 12, S], F32, c2)
                z = k.sbuf("z", [P, 4, S], F32, c2)
                cols = k.sbuf("dn_cols", [P, 10, NU], F32, c2)
                first_loads(k, par[:], col["qn"])
                c = {"seg": tab[:, 0:256].rearrange("q (d j) -> q d j", d=2),
                     "cum": tab[:, 256:512].rearrange("q (d j) -> q d j", d=2),
                     "tri": tab[:, 512:640].rearrange("q (d j) -> q d j", d=2),
                     "eye64": tab[:, 640:704],
                     "lev": tab[:, 704:1472].rearrange("q (d l j) -> q d l j", d=2, l=6)}

                def place(u):
                    if u < 6:
                        return qkv[:, 2 * u:2 * u + 2, :], ACT.Silu
                    return z[:, 2 * u - 12:2 * u - 10, :], ACT.Silu
                taps = [col["dn_conv"][:, 12 * j:12 * j + 12] for j in range(3)]
                projection(k, "dnx", "dn_in", **conv_parts(k, 8, 6, place, taps, 1), norm=(col["norm1"],),
                           loads=[(wab[:], d["wab"]), (tab[:], d["dn_tables"])])
                q, kk, v = qkv[:, 0:4, :], qkv[:, 4:8, :], qkv[:, 8:12, :]
                fl = lambda t: t.rearrange("q a s -> q (a s)")
                norm_heads(k, "dnn", norm_items(q, q, 64 ** -0.5) + norm_items(kk, kk, 1.0), k.head_ones, 1.0, 4)
                cc = cols[:]
                g, beta, bg = cc[:, 0:2], cc[:, 2:4], cc[:, 4:6]
                with ExitStack() as c3:
                    ee_t = k.sbuf("dn_ee", [P, 3, 2, NU], F32, c3)
                    ee = ee_t[:]
                    names = ("a0", "a1", "a2", "a3", "a4", "a5", "a6")
                    a = {n: k.sbuf(f"dn_{n}", [P, 2 * UW], F32, c3) for n in names}
                    A = {"gm": a["a0"], "bm": a["a1"], "decay": a["a2"], "qk": a["a3"], "qd": a["a4"],
                         "y": a["a0"], "t": a["a1"], "r": a["a5"], "bl": a["a6"],
                         "kb": a["a1"], "vb": a["a2"], "kd": a["a5"], "wn": a["a6"]}
                    dn_gates(k, wab, col["dtb"], col["alog"], g, beta)
                    dn_decays(k, c, g, beta, A, q, ee, bg)
                    dn_systems(k, c, A, q, kk)
                    dn_inverse(k, c, A)
                    ktm = fl(k.h[:, 0:UW // S, :])
                    vtm = fl(q)
                    dn_prepare(k, c, A, ktm, vtm, kk, v, beta, ee, bg)
                    state, vn = (fl(qkv[:, 4:6, :]), fl(qkv[:, 0:2, :])), fl(qkv[:, 6:8, :])
                    dn_scan(k, A, ee, state, vn, v)
                norm_heads(k, "dno", norm_items(v, v, col["dn_norm"], z[:], (y_hi[:, 0], y_lo[:, 0])), k.head_ones, 64.0, 2)
            with ExitStack() as c2:
                dist = k.sbuf("att_dist", [P, ST, 3, S], F32, c2)
                qt = k.sbuf("att_q", [P, 12, S], F32, c2)
                kt = k.sbuf("att_k", [P, 12, S], F32, c2)
                vt = k.sbuf("att_vt", [P, ST, 12, P], F32, c2)
                with ExitStack() as c3:
                    vf = k.sbuf("att_v", [P, 12, S], F32, c3)
                    dst = (qt, kt, vf)
                    parts = plain_parts(k, 18, lambda u: (dst[u // 6][:, 2 * (u % 6):2 * (u % 6) + 2, :], ACT.Copy))
                    projection(k, "atx", "att_in", **parts, loads=[(dist[:], d["att_dist"])])
                    to_token_major(k, "att", [(vf[:, i, :], [vt[:, t, i, :] for t in range(ST)]) for i in range(12)])
                norm_heads(k, "atn", norm_items(qt[:], qt[:], col["qn"])
                           + norm_items(kt[:], kt[:], col["kn"]), k.head_ones, 64.0, 6)
                window_attention(k, "atw", qt[:], kt[:], vt[:], dist[:], y_hi[:, 1], y_lo[:, 1])
            with ExitStack() as c2:
                m_hi = k.sbuf("merged_hi", [P, KD, S], F32R, c2)
                m_lo = k.sbuf("merged_lo", [P, KD, S], F32R, c2)
                parts = gate_parts(k, [(y_hi[:, i], y_lo[:, i]) for i in range(2)], lambda: (m_hi, m_lo))
                projection(k, "gb0", "gates0", **parts, loads=[(k.cols[l][:], d[f"cols{l}"]) for l in (1, 2)]
                           + [(k.router_w[:], d["router_w"]), (k.tri8[:], d["tri8"])])
                residual_projection(k, "wo0", "out0", [KD] * 4, m_hi[:], m_lo[:])
        feed_forward(k, "ff0", "ffn0", (col["norm2"],), conv=[col["ffn_conv"][:, 2 * NF * j:2 * NF * (j + 1)] for j in range(3)])


def block_columns(k, name, col, mod, out, lam, lam_init, lb, layer):
    with stage(k, name) as (block, sem, buf):
        prod, sums, ex = buf("prod", [P, 2, 64]), buf("sums", [P, 2]), buf("ex", [P, 2])
        lo, e, tot, r = buf("lmax", [P, 4]), buf("e", [P, 2, 4]), buf("tot", [P, 4]), buf("r", [P, 4])
        vsteps, ssteps = sem("vector_steps"), sem("scalar_steps")
        lbv, ln1m, lnlb, one_m, inf = (lb[:, i] for i in range(5))

        @block.vector
        def _(dve):
            step = Chain(dve, vsteps)
            step(dve.tensor_tensor(mod, mod, col["b_mod"], ALU.add))
            step(dve.tensor_scalar(col["qn"], col["qn"], 64 ** -0.5, None, ALU.mult))
            for i in range(2):
                step(dve.tensor_tensor(prod[:, i, :], lam[:, 2 * i, :], lam[:, 2 * i + 1, :], ALU.mult))
            step(dve.tensor_reduce(sums[:], prod[:], AX.X, ALU.add))
            step(dve.tensor_tensor(lo[:], col["lb0"], col["lb1"], ALU.max))
            step(dve.tensor_tensor(e[:, 0, :], col["lb0"], lo[:], ALU.subtract))
            step(dve.tensor_tensor(e[:, 1, :], col["lb1"], lo[:], ALU.subtract))
            for i, (norm, sc) in enumerate((("norm1", 8), ("norm2", 32))):
                step(dve.scalar_tensor_tensor(out=out["scale"][:, 8 * i:8 * i + 8], in0=mod[:, sc:sc + 8], scalar=1.0,
                                              in1=col[norm], op0=ALU.add, op1=ALU.mult))
            dve.wait_ge(ssteps, 2)
            step(dve.tensor_tensor(out["lam"], ex[:, 1:2], ex[:, 0:1], ALU.subtract))
            step(dve.tensor_scalar(out["lam"], out["lam"], -lam_init, None, ALU.add))
            step(dve.tensor_scalar(out["subln"], col["subln"], 1.0 - lam_init, None, ALU.mult))
            step(dve.tensor_tensor(tot[:], e[:, 0, :], e[:, 1, :], ALU.add))
            step(dve.reciprocal(r[:], tot[:]))
            step(dve.tensor_tensor(e[:, 0, :], e[:, 0, :], r[:], ALU.mult))
            step(dve.tensor_tensor(e[:, 1, :], e[:, 1, :], r[:], ALU.mult))
            if layer == 1:
                step(dve.memset(lbv, 0.0))
            else:
                step(dve.tensor_tensor(tot[:], e[:, 0, :], e[:, 1, :], ALU.add))
                step(dve.tensor_tensor(lbv, tot[:], e[:, 0, :], ALU.subtract))
            step(dve.tensor_scalar(one_m, lbv, -1.0, 1.0, ALU.mult, ALU.add))
            step(dve.tensor_scalar(ln1m, one_m, 1e-18, None, ALU.max))
            step(dve.tensor_scalar(lnlb, lbv, 1e-18, None, ALU.max))
            step(dve.tensor_scalar(inf, lbv, 1e-18, -BIG, ALU.is_lt, ALU.mult))
            dve.wait_ge(ssteps, 4)
            step(dve.tensor_tensor(lnlb, lnlb, inf, ALU.add))

        @block.scalar
        def _(act):
            step = Chain(act, ssteps)
            act.wait_ge(vsteps, 8)
            step(act.activation(ex[:], sums[:], ACT.Exp))
            step(act.activation(e[:], e[:], ACT.Exp))
            act.wait_ge(vsteps, 10 + 7 + (1 if layer == 1 else 2) + 4)
            step(act.activation(ln1m, ln1m, ACT.Ln))
            step(act.activation(lnlb, lnlb, ACT.Ln))


def diff_attention(k, name, qk, vt, dist, nlam, out, side):
    H = 4
    slope = lambda h: 2.0 ** (-8.0 * (h + 1) / H)
    its = [(h, t) for h in range(H) for t in range(ST)]
    n = len(its)
    with stage(k, name) as (block, sem, buf):
        sc, a = buf("scores", [P, 2, 2 * S]), buf("a", [P, 2, S])
        pt = buf("pt", [P, 2, 2, P])
        nmax, l, rl = buf("nmax", [P, 2, 2]), buf("l", [P, 2, 2]), buf("rl", [P, 2, 2])
        qk_done, biased, max_ready, exp_done, steps, combined, turned, moved, pv_done, out_ready = map(
            sem, ("qk_done", "biased", "max_ready", "exp_done", "steps", "combined", "turned", "moved", "pv_done",
                  "out_ready"))

        @block.tensor
        def _(pe):
            def scores(i):
                h, t = its[i]
                if i >= 2:
                    pe.wait_ge(biased, i - 1)
                rows = slice(64 * (h % 2), 64 * (h % 2) + 64)
                for m in range(2):
                    mm = pe.matmul(k.bank(i % 2)[:, bass.ts(m, S)], qk[rows, 2 * m + h // 2, bass.ts(t, P)],
                                   qk[rows, 4 + 2 * m + h // 2, :], start=True, stop=True)
                mm.then_inc(qk_done, 1)

            def turn(i):
                pe.wait_ge(combined, i + 1)
                if i >= 2:
                    pe.wait_ge(moved, i - 1)
                for j in range(2):
                    mm = pe.transpose(k.bank(2 + i % 2)[:, bass.ts(j, P)], a[:, i % 2, bass.ts(j, P)], k.ident)
                mm.then_inc(turned, 1)

            def pv(i):
                h, t = its[i]
                pe.wait_ge(moved, i + 1)
                if i >= 2:
                    pe.wait_ge(out_ready, i - 1)
                for j in range(2):
                    mm = pe.matmul(k.bank(4 + i % 2)[:, 0:P], vt[:, j, h, :], pt[:, i % 2, j, :],
                                   start=(j == 0), stop=(j == 1))
                mm.then_inc(pv_done, 1)

            for i in range(n + 3):
                if i < n:
                    scores(i)
                if i < n + 2:
                    side.step("pe", pe)
                if 2 <= i < n + 2:
                    turn(i - 2)
                if i >= 3:
                    pv(i - 3)

        @block.vector
        def _(dve):
            step = Chain(dve, steps)

            def bias(i):
                h, t = its[i]
                dve.wait_ge(qk_done, i + 1)
                if i >= 2:
                    dve.wait_ge(combined, i - 1)
                s = sc[:, i % 2, :].rearrange("p (m s) -> p m s", m=2)
                dve.scalar_tensor_tensor(out=s, in0=bc(dist[:, t, :].unsqueeze(1), [P, 2, S]), scalar=-slope(h),
                                         in1=k.bank(i % 2).rearrange("p (m s) -> p m s", m=2),
                                         op0=ALU.mult, op1=ALU.add).then_inc(biased, 1)
                dve.wait_ge(biased, i + 1)
                dve.tensor_reduce(nmax[:, i % 2, :], s, AX.X, ALU.max, negate=True).then_inc(max_ready, 1)

            def combine(i):
                dve.wait_ge(exp_done, 2 * i + 2)
                if i >= 2:
                    dve.wait_ge(turned, i - 1)
                r = rl[:, i % 2, :]
                step(dve.reciprocal(r, l[:, i % 2, :]))
                step(dve.tensor_tensor(r[:, 1:2], r[:, 1:2], nlam, ALU.mult))
                s = sc[:, i % 2, :]
                step(dve.tensor_scalar(s[:, 0:S], s[:, 0:S], r[:, 0:1], None, ALU.mult))
                dve.scalar_tensor_tensor(out=a[:, i % 2, :], in0=s[:, S:2 * S], scalar=r[:, 1:2], in1=s[:, 0:S],
                                         op0=ALU.mult, op1=ALU.add).then_inc(combined, 1)

            def store(i):
                h, t = its[i]
                dve.wait_ge(pv_done, i + 1)
                dve.tensor_copy(out[:, h, bass.ts(t, P)], k.bank(4 + i % 2)[:, 0:P]).then_inc(out_ready, 1)

            for i in range(n + 4):
                if i < n:
                    bias(i)
                if 1 <= i <= n:
                    combine(i - 1)
                if i >= 4:
                    store(i - 4)
                if i < n + 2:
                    side.step("dve", dve)

        @block.scalar
        def _(act):
            for i in range(n + 2):
                side.step("act", act)
                if i < n:
                    act.wait_ge(max_ready, i + 1)
                    for m in range(2):
                        act.activation(sc[:, i % 2, bass.ts(m, S)], sc[:, i % 2, bass.ts(m, S)], ACT.Exp,
                                       bias=nmax[:, i % 2, m:m + 1], accum_out=l[:, i % 2, m:m + 1]).then_inc(exp_done, 1)
                j = i - 2
                if j >= 0:
                    act.wait_ge(turned, j + 1)
                    if j >= 2:
                        act.wait_ge(pv_done, j - 1)
                    act.activation(pt[:, j % 2, :, :], k.bank(2 + j % 2)[:, 0:2 * P], ACT.Copy).then_inc(moved, 1)

        side.load(block)


def gated_recurrence(k, name, q, f, vt, lb, tab, out, side, steps):
    HW = 4 * S
    lbv, ln1m, lnlb, one_m, inf = (lb[:, i] for i in range(5))
    with ExitStack() as c:
        mk = lambda x, w=HW: k.sbuf(f"{name}_{x}", [P, w], F32, c)
        ls, kf, b, t1 = mk("ls"), mk("k"), mk("b"), mk("t1")
        reset = mk("reset")
        hs = lambda t: t.rearrange("p (h s) -> p h s", h=4)
        with stage(k, name + "g") as (block, sem, buf):
            vsteps, ssteps, made = sem("vector_steps"), sem("scalar_steps"), sem("reset_made")
            cb = lambda a: bc(a.unsqueeze(2), [P, 4, S])

            @block.gpsimd
            def _(pool):
                pool.memset(reset[:], 1.0).then_inc(made, 1)
                pool.wait_ge(made, 1)
                pool.memset(hs(reset[:])[:, :, 0:1], 0.0).then_inc(made, 1)

            @block.vector
            def _(dve):
                step = Chain(dve, vsteps)
                step(dve.scalar_tensor_tensor(out=t1[:], in0=f, scalar=-1.0, in1=f, op0=ALU.mult, op1=ALU.max))
                side.step("dve", dve, steps[0])
                dve.wait_ge(ssteps, 2)
                step(dve.scalar_tensor_tensor(out=ls[:], in0=f, scalar=0.0, in1=t1[:], op0=ALU.min, op1=ALU.subtract))
                step(dve.tensor_tensor(kf[:], ls[:], f, ALU.subtract))
                step(dve.tensor_tensor(hs(ls[:]), hs(ls[:]), cb(ln1m), ALU.add))
                step(dve.tensor_tensor(hs(b[:]), hs(ls[:]), cb(lnlb), ALU.subtract))
                step(dve.scalar_tensor_tensor(out=t1[:], in0=b[:], scalar=-1.0, in1=b[:], op0=ALU.mult, op1=ALU.max))
                side.step("dve", dve, steps[1])
                step(dve.tensor_tensor(hs(ls[:]), hs(ls[:]), cb(lnlb), ALU.max))
                dve.wait_ge(ssteps, 5)
                step(dve.tensor_tensor(ls[:], ls[:], t1[:], ALU.add))
                step(dve.tensor_tensor(hs(kf[:]), hs(kf[:]), cb(one_m), ALU.mult))
                dve.wait_ge(made, 2)
                step(dve.tensor_tensor_scan(b[:], reset[:], ls[:], 0.0, ALU.mult, ALU.add))
                side.step("dve", dve, steps[2])

            @block.scalar
            def _(act):
                step = Chain(act, ssteps)
                side.step("act", act, steps[0])
                act.wait_ge(vsteps, 1)
                step(act.activation(t1[:], t1[:], ACT.Exp, scale=-1.0))
                step(act.activation(t1[:], t1[:], ACT.Ln, bias=1.0))
                act.wait_ge(vsteps, 3)
                step(act.activation(kf[:], kf[:], ACT.Exp))
                side.step("act", act, steps[1])
                act.wait_ge(vsteps, 6)
                step(act.activation(t1[:], t1[:], ACT.Exp, scale=-1.0))
                step(act.activation(t1[:], t1[:], ACT.Ln, bias=1.0))
                side.step("act", act, steps[2])

            block.tensor(lambda pe: side.step("pe", pe, sum(steps)))
            side.load(block)
        levels = 8
        with stage(k, name + "l") as (block, sem, buf):
            att = buf("att", [P, 8, P])
            dd, ke = (ls[:], t1[:]), (reset[:], f)
            qe = (buf("qe", [P, HW])[:], out.rearrange("p h s -> p (h s)"))
            cross = ls[:, 0:4 * P].rearrange("p (h t) -> p h t", h=4)
            dd_ready, abs_ready, e_ready, ke_ready, qe_ready, att_done, taken, crossed, pv_done, out_ready = map(
                sem, ("dd_ready", "abs_ready", "e_ready", "ke_ready", "qe_ready", "att_done", "taken", "crossed",
                      "pv_done", "out_ready"))

            @block.vector
            def _(dve):
                def diff(j):
                    half = 1 << j
                    blocks = b[:].rearrange("p (n w) -> p n w", w=2 * half)
                    if j >= 2:
                        dve.wait_ge(qe_ready, j - 1)
                        dve.wait_ge(ke_ready, j - 1)
                    dve.tensor_tensor(dd[j % 2].rearrange("p (n w) -> p n w", w=2 * half), blocks,
                                      bc(blocks[:, :, half - 1:half], [P, HW // (2 * half), 2 * half]),
                                      ALU.subtract).then_inc(dd_ready, 1)

                def take(j):
                    dve.wait_ge(att_done, j + 2)
                    src = k.bank(2 * ((j + 1) % 3), 2).rearrange("p (n t) -> p n t", n=8)
                    if j < 0:
                        dve.tensor_tensor(att[:], src, bc(tab["ident"].unsqueeze(1), [P, 8, P]), ALU.mult).then_inc(taken, 1)
                    else:
                        dve.wait_ge(taken, j + 1)
                        dve.copy_predicated(att[:], bc(tab["lev"][:, j, :].bitcast(I32).unsqueeze(1), [P, 8, P]),
                                            src).then_inc(taken, 1)

                diff(0)
                for j in range(levels):
                    if j + 1 < levels:
                        diff(j + 1)
                    dve.wait_ge(e_ready, j + 1)
                    if j >= 2:
                        dve.wait_ge(att_done, j)
                    dve.tensor_tensor(ke[j % 2], kf[:], dd[j % 2], ALU.mult).then_inc(ke_ready, 1)
                    if j >= 1:
                        take(j - 2)
                    side.step("dve", dve)
                take(levels - 2)
                for g in range(2):
                    dve.wait_ge(pv_done, g + 1)
                    dve.tensor_copy(out[:, 2 * g:2 * g + 2, :], k.bank(g)).then_inc(out_ready, 1)

            @block.scalar
            def _(act):
                for j in range(levels):
                    act.wait_ge(dd_ready, j + 1)
                    act.activation(dd[j % 2], dd[j % 2], ACT.Abs).then_inc(abs_ready, 1)
                    act.wait_ge(abs_ready, j + 1)
                    act.activation(dd[j % 2], dd[j % 2], ACT.Exp, scale=-1.0).then_inc(e_ready, 1)
                    side.step("act", act)
                act.wait_ge(att_done, levels + 1)
                act.activation(cross, k.bank(2 * (levels % 3)), ACT.Copy).then_inc(crossed, 1)

            @block.gpsimd
            def _(pool):
                for j in range(levels):
                    pool.wait_ge(e_ready, j + 1)
                    if j >= 2:
                        pool.wait_ge(att_done, j)
                    pool.tensor_tensor(qe[j % 2], q, dd[j % 2], ALU.mult).then_inc(qe_ready, 1)

            @block.tensor
            def _(pe):
                for j in range(-1, levels):
                    if j >= 0:
                        pe.wait_ge(ke_ready, j + 1)
                        pe.wait_ge(qe_ready, j + 1)
                    if j >= 2:
                        pe.wait_ge(taken, j - 1)
                    first = 2 * ((j + 1) % 3)
                    ks, qs = (kf[:], q) if j < 0 else (ke[j % 2], qe[j % 2])
                    if j < levels - 1:
                        for i in range(8):
                            mm = pe.matmul(k.bank(first, 2)[:, bass.ts(i, P)], ks[:, bass.ts(i, P)], qs[:, bass.ts(i, P)],
                                           start=True, stop=True)
                    else:
                        for h in range(4):
                            mm = pe.matmul(k.bank(first)[:, bass.ts(h, P)], ks[:, bass.ts(2 * h, P)],
                                           qs[:, bass.ts(2 * h + 1, P)], start=True, stop=True)
                    mm.then_inc(att_done, 1)
                    if j < levels - 1:
                        side.step("pe", pe)
                pe.wait_ge(taken, levels)
                pe.wait_ge(crossed, 1)
                for h in range(4):
                    o = k.bank(h // 2)[:, (h % 2) * S:(h % 2 + 1) * S]
                    pe.matmul(o[:, 0:P], vt[:, 0, h, :], att[:, 2 * h, :], start=True, stop=True)
                    pe.matmul(o[:, P:S], vt[:, 0, h, :], cross[:, h, :], start=True, stop=False)
                    mm = pe.matmul(o[:, P:S], vt[:, 1, h, :], att[:, 2 * h + 1, :], start=False, stop=True)
                    if h % 2:
                        mm.then_inc(pv_done, 1)

            side.load(block)


def mlstm(k, name, q, kk, vt, wif, bif, tab, out, side, steps):
    H = 4
    with stage(k, name) as (block, sem, buf):
        gi, lf = buf("gi", [P, ST, 8]), buf("lf", [P, ST, 4])
        t1, fsum = buf("t1", [P, ST, 4]), buf("fsum", [P, ST, 4])
        gm = buf("gm", [P, 2, ST, S])
        w = buf("w", [P, 2, ST, S])
        wt = buf("wt", [P, 2, 3, P])
        mx, nm, em, dot, den = (buf(x, [P, 2, ST]) for x in ("mx", "nm", "em", "dot", "den"))
        projected, vsteps, ssteps, f_done, gm_ready, d_done, s_done, masked, max_ready, exp_done, w_ready, turned, \
            moved, pv_done, out_ready = map(
                sem, ("projected", "vector_steps", "scalar_steps", "f_done", "gm_ready", "d_done", "s_done", "masked",
                      "max_ready", "exp_done", "w_ready", "turned", "moved", "pv_done", "out_ready"))
        first_steps = 3

        @block.tensor
        def _(pe):
            for t in range(ST):
                for i in range(KD):
                    mm = pe.matmul(k.bank(5)[:, 8 * t:8 * t + 8], k.h[:, i, bass.ts(t, P)], wif[:, i, :],
                                   start=(i == 0), stop=(i == KD - 1))
            mm.then_inc(projected, 1)
            side.step("pe", pe, steps[0])
            pe.wait_ge(vsteps, first_steps + 1)
            for t in range(ST):
                for kt in range(t + 1):
                    mm = pe.matmul(k.bank(4)[:, 4 * t:4 * t + 4], tab["le"][:, kt, bass.ts(t, P)], lf[:, kt, :],
                                   start=(kt == 0), stop=(kt == t))
            mm.then_inc(f_done, 1)

            def logs(h):
                pe.wait_ge(gm_ready, 4 * h + 4)
                if h >= 2:
                    pe.wait_ge(masked, h - 1)
                for t in range(ST):
                    for kt in range(t + 1):
                        mm = pe.matmul(k.bank(h % 2)[:, bass.ts(t, S)], tab["le"][:, kt, bass.ts(t, P)],
                                       gm[:, h % 2, kt, :], start=(kt == 0), stop=(kt == t))
                mm.then_inc(d_done, 1)
                if h >= 2:
                    pe.wait_ge(w_ready, h - 1)
                for t in range(ST):
                    mm = pe.matmul(k.bank(2 + h % 2)[:, bass.ts(t, S)], q[:, h, bass.ts(t, P)], kk[:, h, :],
                                   start=True, stop=True)
                mm.then_inc(s_done, 1)

            def outputs(h):
                pe.wait_ge(w_ready, h + 1)
                if h >= 1:
                    pe.wait_ge(moved, h)
                else:
                    pe.wait_ge(vsteps, first_steps + 2)
                for j, (t, s) in enumerate(((0, 0), (1, 0), (1, 1))):
                    mm = pe.transpose(k.bank(4)[:, bass.ts(j, P)], w[:, h % 2, t, bass.ts(s, P)], k.ident)
                mm.then_inc(turned, 1)
                side.step("pe", pe, steps[1])
                pe.wait_ge(moved, h + 1)
                if h >= 1:
                    pe.wait_ge(out_ready, h)
                o = k.bank(5)
                pe.matmul(o[:, 0:P], vt[:, 0, h, :], wt[:, h % 2, 0, :], start=True, stop=True)
                pe.matmul(o[:, P:S], vt[:, 0, h, :], wt[:, h % 2, 1, :], start=True, stop=False)
                pe.matmul(o[:, P:S], vt[:, 1, h, :], wt[:, h % 2, 2, :], start=False, stop=True).then_inc(pv_done, 1)

            for h in range(H + 1):
                if h < H:
                    logs(h)
                side.step("pe", pe, steps[1])
                if h >= 1:
                    outputs(h - 1)
                else:
                    side.step("pe", pe, steps[1])
                side.step("pe", pe, steps[1])

        @block.vector
        def _(dve):
            step = Chain(dve, vsteps)
            dve.wait_ge(projected, 1)
            step(dve.tensor_tensor(gi[:], k.bank(5)[:, 0:16].rearrange("p (t g) -> p t g", t=ST),
                                   bc(bif.unsqueeze(1), [P, ST, 8]), ALU.add))
            f = gi[:, :, 4:8]
            step(dve.scalar_tensor_tensor(out=t1[:], in0=f, scalar=-1.0, in1=f, op0=ALU.mult, op1=ALU.max))
            step(dve.tensor_scalar(lf[:], f, 0.0, None, ALU.min))
            dve.wait_ge(ssteps, 2)
            step(dve.tensor_tensor(lf[:], lf[:], t1[:], ALU.subtract))
            side.step("dve", dve, steps[0])
            dve.wait_ge(f_done, 1)
            step(dve.tensor_copy(fsum[:], k.bank(4)[:, 0:8].rearrange("p (t g) -> p t g", t=ST)))

            def gates(h):
                if h >= 2:
                    dve.wait_ge(d_done, h - 1)
                for kt in range(ST):
                    dve.tensor_scalar(gm[:, h % 2, kt, :], tab["gt"][:, kt, :], lf[:, kt, h:h + 1], None,
                                      ALU.mult).then_inc(gm_ready, 1)
                dve.wait_ge(gm_ready, 4 * h + 2)
                for kt in range(ST):
                    dve.scalar_tensor_tensor(out=gm[:, h % 2, kt, :], in0=tab["eq"][:, kt, :], scalar=gi[:, kt, h:h + 1],
                                             in1=gm[:, h % 2, kt, :], op0=ALU.mult, op1=ALU.add).then_inc(gm_ready, 1)

            def maxima(h):
                dve.wait_ge(d_done, h + 1)
                if h >= 2:
                    dve.wait_ge(turned, h - 1)
                ww = w[:, h % 2, :, :]
                dve.tensor_tensor(ww, k.bank(h % 2).rearrange("p (t s) -> p t s", t=ST), tab["mask"],
                                  ALU.add).then_inc(masked, 1)
                dve.wait_ge(masked, h + 1)
                step(dve.tensor_reduce(mx[:, h % 2, :], ww, AX.X, ALU.max))
                step(dve.tensor_tensor(mx[:, h % 2, :], mx[:, h % 2, :], fsum[:, :, h], ALU.max))
                dve.tensor_scalar(nm[:, h % 2, :], mx[:, h % 2, :], -1.0, None, ALU.mult).then_inc(max_ready, 1)

            def weights(h):
                dve.wait_ge(exp_done, 3 * h + 3)
                dve.wait_ge(s_done, h + 1)
                ww, dt, dn = w[:, h % 2, :, :], dot[:, h % 2, :], den[:, h % 2, :]
                step(dve.scalar_tensor_tensor(out=ww, in0=k.bank(2 + h % 2).rearrange("p (t s) -> p t s", t=ST),
                                              scalar=P ** -0.5, in1=ww, op0=ALU.mult, op1=ALU.mult))
                step(dve.tensor_reduce(dt, ww, AX.X, ALU.add))
                step(dve.scalar_tensor_tensor(out=dn, in0=dt, scalar=-1.0, in1=dt, op0=ALU.mult, op1=ALU.max))
                step(dve.tensor_tensor(dn, dn, em[:, h % 2, :], ALU.max))
                step(dve.reciprocal(dn, dn))
                for t in range(ST):
                    ins = dve.tensor_scalar(w[:, h % 2, t, :], w[:, h % 2, t, :], dn[:, t:t + 1], None, ALU.mult)
                    if t == 0:
                        step(ins)
                ins.then_inc(w_ready, 1)

            def store(h):
                dve.wait_ge(pv_done, h + 1)
                dve.tensor_copy(out[:, h, :], k.bank(5)[:, 0:S]).then_inc(out_ready, 1)

            gates(0)
            gates(1)
            for h in range(H + 2):
                if h >= 2:
                    store(h - 2)
                if 1 <= h <= H:
                    weights(h - 1)
                if h < H:
                    maxima(h)
                if h <= H:
                    side.step("dve", dve, steps[1])
                if h + 2 < H:
                    gates(h + 2)
                if h <= H:
                    side.step("dve", dve, 2 * steps[1])

        @block.scalar
        def _(act):
            step = Chain(act, ssteps)
            act.wait_ge(vsteps, 2)
            step(act.activation(t1[:], t1[:], ACT.Exp, scale=-1.0))
            step(act.activation(t1[:], t1[:], ACT.Ln, bias=1.0))
            side.step("act", act, steps[0])

            def exponentials(h):
                act.wait_ge(max_ready, h + 1)
                for t in range(ST):
                    act.activation(w[:, h % 2, t, :], w[:, h % 2, t, :], ACT.Exp, bias=nm[:, h % 2, t:t + 1]).then_inc(exp_done, 1)
                act.activation(em[:, h % 2, :], nm[:, h % 2, :], ACT.Exp).then_inc(exp_done, 1)

            def move(h):
                act.wait_ge(turned, h + 1)
                if h >= 2:
                    act.wait_ge(pv_done, h - 1)
                act.activation(wt[:, h % 2, :, :], k.bank(4)[:, 0:3 * P], ACT.Copy).then_inc(moved, 1)

            for h in range(H + 1):
                side.step("act", act, steps[1])
                if h < H:
                    exponentials(h)
                side.step("act", act, steps[1])
                if h >= 1:
                    move(h - 1)
                side.step("act", act, steps[1])

        side.load(block)


def router(k, name, rw, rb, tri8, cb):
    with stage(k, name) as (block, sem, buf):
        lg, gt, tmp = buf("lg", [P, ST, NE]), buf("gt", [P, NE, NE]), buf("tmp", [P, NE, NE])
        rank, sel = buf("rank", [P, ST, NE]), buf("sel", [P, ST, NE])
        mx, l = buf("mx", [P, ST]), buf("l", [P, ST])
        dg = buf("dg", [P, ST, NE, P])
        projected, vsteps, ssteps, dg_ready, spread, placed = map(
            sem, ("projected", "vector_steps", "scalar_steps", "dg_ready", "spread", "placed"))

        @block.tensor
        def _(pe):
            for t in range(ST):
                for i in range(KD):
                    mm = pe.matmul(k.bank(0)[:, 8 * t:8 * t + 8], k.h[:, i, bass.ts(t, P)], rw[:, i, :],
                                   start=(i == 0), stop=(i == KD - 1))
            mm.then_inc(projected, 1)
            pe.wait_ge(dg_ready, ST * NE)
            for t in range(ST):
                for j in range(2):
                    mm = pe.matmul(k.bank(2 + 2 * t + j), k.ones, dg[:, t, 4 * j:4 * j + 4, :].rearrange("p e s -> p (e s)"),
                                   start=True, stop=True)
            mm.then_inc(spread, 1)

        @block.vector
        def _(dve):
            step = Chain(dve, vsteps)
            dve.wait_ge(projected, 1)
            step(dve.tensor_tensor(lg[:], k.bank(0)[:, 0:16].rearrange("p (t e) -> p t e", t=ST),
                                   bc(rb.unsqueeze(1), [P, ST, NE]), ALU.add))
            step(dve.tensor_reduce(mx[:], lg[:], AX.X, ALU.max, negate=True))
            dve.wait_ge(ssteps, 2)
            step(dve.reciprocal(l[:], l[:]))
            step(dve.tensor_tensor(lg[:], lg[:], bc(l[:].unsqueeze(2), [P, ST, NE]), ALU.mult))
            for t in range(ST):
                mine = bc(lg[:, t, :].unsqueeze(2), [P, NE, NE])
                other = bc(lg[:, t, :].unsqueeze(1), [P, NE, NE])
                step(dve.tensor_tensor(gt[:], other, mine, ALU.is_gt))
                step(dve.tensor_tensor(tmp[:], other, mine, ALU.is_equal))
                step(dve.tensor_tensor(tmp[:], tmp[:], tri8, ALU.mult))
                step(dve.tensor_tensor(gt[:], gt[:], tmp[:], ALU.add))
                step(dve.tensor_reduce(rank[:, t, :], gt[:], AX.X, ALU.add))
            step(dve.tensor_scalar(sel[:], rank[:], 1.5, None, ALU.is_lt))
            step(dve.tensor_tensor(sel[:], sel[:], lg[:], ALU.mult))
            step(dve.tensor_reduce(mx[:], sel[:], AX.X, ALU.add))
            step(dve.reciprocal(mx[:], mx[:]))
            step(dve.tensor_tensor(sel[:], sel[:], bc(mx[:].unsqueeze(2), [P, ST, NE]), ALU.mult))
            for t in range(ST):
                for e in range(NE):
                    dve.tensor_scalar(dg[:, t, e, :], k.ident, sel[:, t, e:e + 1], None, ALU.mult).then_inc(dg_ready, 1)
            dve.wait_ge(spread, 1)
            for t in range(ST):
                for j in range(2):
                    dve.tensor_copy(cb[:, 4 * j:4 * j + 4, bass.ts(t, P)],
                                    k.bank(2 + 2 * t + j).rearrange("p (e s) -> p e s", e=4)).then_inc(placed, 1)

        @block.scalar
        def _(act):
            act.wait_ge(vsteps, 2)
            for t in range(ST):
                act.activation(lg[:, t, :], lg[:, t, :], ACT.Exp, bias=mx[:, t:t + 1], accum_out=l[:, t:t + 1]).then_inc(ssteps, 1)


def experts(k, phase, cb, gain):
    s0 = k.first[phase]
    start = k.place[s0]
    up = 2 * NF * KD // SLOT
    with ExitStack() as c:
        g_hi = k.sbuf("moe_g_hi", [P, NF, S], F32R, c)
        g_lo = k.sbuf("moe_g_lo", [P, NF, S], F32R, c)
        with stage(k, "moe") as (block, sem, buf):
            gate, g, y = buf("gate", [P, 2, S]), buf("g", [P, 2, S]), buf("y", [P, 2, S])
            gate_ready, product, rounded, g_split, weighted, added = map(
                sem, ("gate_ready", "product", "rounded", "g_split", "weighted", "added"))
            NS, ND = EXPERT_SLOTS, KD // 2
            down_end = lambda d: up + ((d + 1) * 2 * NF + SLOT - 1) // SLOT

            def raw_ready(eng, e, j):
                n = start + j
                eng.wait_ge(k.raw_loaded[n % RAW], e * (16 * NS // RAW) + 16 * (n // RAW + 1))

            def load(sp, e, j):
                sp.wait_ge(k.slot_split, e * NS + s0 + j - RAW + 1)
                sp.dma_start(k.raw[:, (start + j) % RAW, :],
                             k.dram["experts"][bass.ds(e * NS + j, 1)].rearrange("n p w -> (n p) w")).then_inc(k.raw_loaded[(start + j) % RAW], 16)

            assert k.loaded == start + RAW and k.hi_done == k.lo_done == s0 + LOOK

            @block.sync
            def _(sp):
                with sp.Fori(0, NE - 1) as e:
                    for j in range(RAW, NS + RAW):
                        load(sp, e, j)
                for j in range(RAW, NS):
                    load(sp, NE - 1, j)

            def split_hi(act, e, j):
                s = s0 + j
                raw_ready(act, e, j)
                act.wait_ge(k.slot_used, e * NS + s - SPLIT + 1)
                act.activation(k.w_hi[:, s % SPLIT, :], k.raw[:, (start + j) % RAW, :], ACT.Copy).then_inc(k.hi_ready, 1)

            def split_lo(dve, e, j):
                s = s0 + j
                raw_ready(dve, e, j)
                dve.wait_ge(k.hi_ready, e * NS + s + 1)
                dve.tensor_tensor(k.w_lo[:, s % SPLIT, :], k.raw[:, (start + j) % RAW, :],
                                  k.w_hi[:, s % SPLIT, :].bitcast(F32), ALU.subtract).then_inc(k.slot_split, 1)

            def act_expert(act, e, last):
                done = LOOK
                for f in range(NF):
                    for j in range(done, UPS * (f + 1) + LOOK):
                        split_hi(act, e, j)
                    done = UPS * (f + 1) + LOOK
                    act.wait_ge(k.slot_used, e * NS + s0 + UPS * (f + 1))
                    if f >= 2:
                        act.wait_ge(product, e * NF + f - 1)
                    act.activation(gate[:, f % 2, :], k.bank(f % 4)[:, 0:S], ACT.Silu).then_inc(gate_ready, 1)
                for j in range(done, NS if last else NS + LOOK):
                    split_hi(act, e, j)

            def dve_expert(dve, e, last):
                done = LOOK
                for f in range(NF):
                    for j in range(done, UPS * (f + 1) + LOOK):
                        split_lo(dve, e, j)
                    done = UPS * (f + 1) + LOOK
                    dve.wait_ge(gate_ready, e * NF + f + 1)
                    gb = g[:, f % 2, :]
                    dve.tensor_tensor(gb, k.bank(f % 4)[:, S:2 * S], gate[:, f % 2, :], ALU.mult).then_inc(product, 1)
                    dve.wait_ge(product, e * NF + f + 1)
                    dve.tensor_copy(g_hi[:, f, :], gb).then_inc(rounded, 1)
                    dve.wait_ge(rounded, e * NF + f + 1)
                    dve.tensor_tensor(g_lo[:, f, :], gb, g_hi[:, f, :].bitcast(F32), ALU.subtract).then_inc(g_split, 1)
                for d in range(ND):
                    upto = min(down_end(d) + LOOK, NS if last else NS + LOOK)
                    for j in range(done, upto):
                        split_lo(dve, e, j)
                    done = upto
                    dve.wait_ge(k.slot_used, e * NS + s0 + down_end(d))
                    for half in range(2):
                        i = 2 * d + half
                        if isinstance(e, int):
                            w = cb[:, e, :]
                        else:
                            w = cb[:, bass.ds(e, 1), :].rearrange("p n s -> p (n s)")
                        dve.tensor_tensor(y[:, half, :], k.bank(4 + d)[:, bass.ts(half, S)], w, ALU.mult).then_inc(weighted, 1)
                    for half in range(2):
                        i = 2 * d + half
                        dve.wait_ge(weighted, e * KD + 2 * d + 2)
                        dve.scalar_tensor_tensor(out=k.x[:, i, :], in0=y[:, half, :], scalar=gain[:, i:i + 1],
                                                 in1=k.x[:, i, :], op0=ALU.mult, op1=ALU.add).then_inc(added, 1)
                    dve.wait_ge(added, e * KD + 2 * d + 2)

            @block.scalar
            def _(act):
                with act.Fori(0, NE - 1) as e:
                    act_expert(act, e, False)
                act_expert(act, NE - 1, True)

            @block.vector
            def _(dve):
                with dve.Fori(0, NE - 1) as e:
                    dve_expert(dve, e, False)
                dve_expert(dve, NE - 1, True)

            @block.tensor
            def _(pe):
                with pe.Fori(0, NE) as e:
                    at = lambda v: e * NS + v
                    t = 0
                    for f in range(NF):
                        if f >= 4:
                            pe.wait_ge(product, e * NF + f - 3)
                        t = multiply_unit(k, pe, s0, t, KD, k.h_hi[:], k.h_lo[:], k.bank(f % 4), at)
                    for d in range(ND):
                        t = multiply_unit(k, pe, s0, t, NF, g_hi[:], g_lo[:], k.bank(4 + d), at,
                                          rhs_ready=(g_split, e * NF) if d == 0 else None)


def mixer_block(k, l):
    d = k.dram
    lam_init = 0.8 - 0.6 * float(np.exp(-0.3 * (l - 1)))
    n = lambda x: f"{x}{l}"
    fl = lambda t: t.rearrange("q a s -> q (a s)")
    with ExitStack() as c0:
        par = k.cols[l]
        col = {x: par[:, a:z] for x, (a, z) in COL1.items()}
        own = k.sbuf(n("own"), [P, 18 + 20], F32, c0)
        out = {"scale": own[:, 0:16], "lam": own[:, 16:17], "subln": own[:, 17:18]}
        lb = own[:, 18:38].rearrange("p (a h) -> p a h", a=5)
        mod = k.mod[:, (l - 1) * NMOD:l * NMOD]
        block_columns(k, n("own"), col, mod, out, col["lam"].rearrange("p (a j) -> p a j", a=4), lam_init, lb, l)
        with ExitStack() as c1:
            y_hi = k.sbuf(n("mix_hi"), [P, 3, 4, S], F32R, c1)
            y_lo = k.sbuf(n("mix_lo"), [P, 3, 4, S], F32R, c1)
            y = [(y_hi[:, i], y_lo[:, i]) for i in range(3)]
            m = []
            with ExitStack() as cc:
                c_qk = k.sbuf(n("c_qk"), [P, 8, S], F32, cc)
                c_v, c_o = (k.sbuf(n(x), [P, 4, S], F32, cc) for x in ("c_v", "c_o"))
                with ExitStack() as cb:
                    b_q, b_f, b_v, b_g = (k.sbuf(n(x), [P, 4, S], F32, cb) for x in ("b_q", "b_f", "b_v", "b_g"))
                    lev = k.sbuf(n("b_lev"), [P, 7, P], F32, cb)

                    with ExitStack() as ca:
                        dist = k.sbuf(n("da_dist"), [P, ST, S], F32, ca)
                        qk = k.sbuf(n("a_qk"), [P, 8, S], F32, ca)
                        vf = k.sbuf(n("a_v"), [P, 4, S], F32, ca)
                        vt = k.sbuf(n("a_vt"), [P, ST, 4, P], F32, ca)
                        parts = plain_parts(k, 6, lambda u: (qk[:, 2 * u:2 * u + 2, :] if u < 4
                                                             else vf[:, 2 * u - 8:2 * u - 6, :], ACT.Copy))
                        projection(k, n("ax"), n("a_in"), **parts, norm=(out["scale"][:, 0:8], mod[:, 0:8]),
                                   loads=[(dist[:], d["da_dist"]), (lev[:], d["hg_levels"])])
                        dst, fn = (b_q, b_f, b_v, b_g), (ACT.Silu, ACT.Copy, ACT.Copy, ACT.Silu)
                        side = Side(k, ca, n("bx"), n("b_in"), **plain_parts(
                            k, 8, lambda u: (dst[u // 2][:, 2 * (u % 2):2 * (u % 2) + 2, :], fn[u // 2])))
                        to_token_major(k, n("at"), [(vf[:, i, :], [vt[:, t, i, :] for t in range(ST)]) for i in range(4)])
                        norm_heads(k, n("an"), norm_items(qk[:, 0:4, :], qk[:, 0:4, :], col["qn"])
                                   + norm_items(qk[:, 4:8, :], qk[:, 4:8, :], col["kn"]), k.head_ones, 64.0, 4, side, 3)
                        diff_attention(k, n("da"), qk[:], vt[:], dist[:], out["lam"], vf[:], side)
                        norm_heads(k, n("ao"), norm_items(vf[:], vf[:], out["subln"], None, y[0]),
                                   k.ones, float(P), 2, side, 3)
                        side.finish()

                    vt = k.sbuf(n("b_vt"), [P, ST, 4, P], F32, cb)

                    def place(u):
                        if u < 4:
                            return c_qk[:, 2 * u:2 * u + 2, :], ACT.Silu
                        if u < 6:
                            return c_v[:, 2 * u - 8:2 * u - 6, :], ACT.Copy
                        return c_o[:, 2 * u - 12:2 * u - 10, :], ACT.Sigmoid
                    taps = [col["conv"][:, 8 * j:8 * j + 8] for j in range(4)]
                    side = Side(k, cb, n("cx"), n("c_in"), **conv_parts(k, 8, 4, place, taps, 3, col["conv_b"]))
                    to_token_major(k, n("bt"), [(b_v[:, i, :], [vt[:, t, i, :] for t in range(ST)]) for i in range(4)])
                    gated_recurrence(k, n("hg"), fl(b_q[:]), fl(b_f[:]), vt[:], lb, {"ident": k.ident, "lev": lev[:]},
                                     b_v[:], side, (1, 2, 2))
                    norm_heads(k, n("bo"), norm_items(b_v[:], b_v[:], col["gnorm"], b_g[:], y[1]),
                               k.ones, float(P), 2, side, 3)
                    side.finish()

                side = Side(k, cc, n("gb"), n("gates"), **gate_parts(k, y, lambda: m))
                with ExitStack() as ct:
                    vt = k.sbuf(n("c_vt"), [P, ST, 4, P], F32, ct)
                    wif = k.sbuf(n("c_wif"), [P, KD, 8], F32, ct)
                    tabs = k.sbuf(n("c_tabs"), [P, 4, ST, S], F32, ct)
                    to_token_major(k, n("ct"), [(c_v[:, i, :], [vt[:, t, i, :] for t in range(ST)]) for i in range(4)],
                                   loads=[(tabs[:], d["ml_tables"]), (wif[:], d[n("wif")])])
                    tab = dict(zip(("le", "gt", "eq", "mask"), (tabs[:, i] for i in range(4))))
                    mlstm(k, n("ml"), c_qk[:, 0:4, :], c_qk[:, 4:8, :], vt[:], wif, col["bif"], tab, c_v[:], side, (3, 1))
                    norm_heads(k, n("co"), norm_items(c_v[:], c_v[:], col["cnorm"], c_o[:], y[2]),
                               k.ones, float(P), 2, side, 3)
                m += [k.sbuf(n(f"merged_{x}"), [P, KD, S], F32R, cc) for x in ("hi", "lo")]
                side.finish()
                residual_projection(k, n("wo"), n("out"), [KD] * 4, m[0][:], m[1][:], mod[:, 16:24])
        norm = (out["scale"][:, 8:16], mod[:, 24:32])
        if l == 1:
            feed_forward(k, n("ff"), n("ffn"), norm, mod[:, 40:48])
        else:
            norm_stream(k, n("n2"), *norm)
            with ExitStack() as c1:
                cb = k.sbuf("token_weights", [P, NE, S], F32, c1)
                router(k, "rt", k.router_w, col["router_b"], k.tri8[:], cb[:])
                experts(k, n("ffn"), cb[:], mod[:, 40:48])


def columns(sizes):
    at, out = 0, {}
    for name, n in sizes:
        out[name] = (at, at + n)
        at += n
    return out, at


COL0, COLS0 = columns((("norm1", 8), ("norm2", 8), ("dn_conv", 36), ("dn_norm", 1), ("qn", 1), ("kn", 1),
                       ("ffn_conv", 6 * NF), ("alog", 8), ("dtb", 8)))
COL1, COLS1 = columns((("norm1", 8), ("norm2", 8), ("b_mod", 48), ("conv", 32), ("conv_b", 8),
                       ("qn", 1), ("kn", 1), ("subln", 1), ("lb0", 4), ("lb1", 4), ("gnorm", 1), ("cnorm", 1),
                       ("bif", 8), ("lam", 256), ("router_b", 8)))
DN_TABLE = 4 * P + 3 * CH + 12 * CH


def shape_tables():
    f = lambda a: np.ascontiguousarray(a, dtype=np.float32)
    i, j = np.arange(P)[:, None], np.arange(P)[None, :]
    same = (i // CH) == (j // CH)
    r, cc = np.arange(P)[:, None] % CH, np.arange(CH)[None, :]
    lev = np.zeros((P, 2, 6, CH))
    for l in range(6):
        blk = (r >> (l + 1)) == (cc >> (l + 1))
        lev[:, 0, l] = blk & (((r >> l) & 1) == 0) & (((cc >> l) & 1) == 1)
        lev[:, 1, l] = blk & (((r >> l) & 1) == 1) & (((cc >> l) & 1) == 0)
    dn = np.concatenate([same & (i > j), same & (i < j), same & (i <= j), same & (i >= j),
                         r <= cc, r >= cc, r == cc, lev.reshape(P, -1)], axis=1)
    q = np.arange(S).reshape(ST, P).T[:, :, None]
    s = np.arange(S)[None, None, :]
    dist = np.abs(q - s)
    att = np.stack([np.where(ok, dist, BIG) for ok in (dist <= 64, dist % 4 == 0, dist % 16 == 0)], axis=2)
    da = np.where(s // 64 <= q // 64, dist, BIG)
    ml = np.stack([q <= s, q > s, q == s, np.where(s <= q, 0.0, -BIG)], axis=1)
    hg = np.stack([((i >> (l + 1)) == (j >> (l + 1))) & (((i >> l) & 1) == 0) & (((j >> l) & 1) == 1)
                   for l in range(7)], axis=1)
    e = np.arange(NE)
    return {"dn_tables": f(dn), "att_dist": f(att), "da_dist": f(da), "ml_tables": f(ml), "hg_levels": f(hg),
            "consts": f(np.concatenate([i == j, np.ones((P, P)), same, np.full((P, 1), EPS)], axis=1)),
            "tri8": f(np.broadcast_to(e[None, :, None] > e[None, None, :], (P, NE, NE)))}


def lay_out(a):
    def tiles(w):
        kk, n = w.shape
        return w.reshape(kk // P, P, n // P, P).transpose(2, 0, 1, 3)

    def pieces(w, order=None):
        t = tiles(w)
        t = t if order is None else t[order]
        return t.reshape(-1, P, P)

    def slots(ps):
        t = np.concatenate(ps)
        return t.reshape(-1, SLOT, P, P).transpose(0, 2, 1, 3).reshape(-1, P, SLOT * P)

    def gates(w_gates, w_branches):
        out = []
        for wg, wb in zip(w_gates, w_branches):
            for dd in range(4):
                out += [pieces(wg, [2 * dd, 2 * dd + 1]), pieces(wb, [2 * dd, 2 * dd + 1])]
        return out

    interleave = [x for f in range(NF) for x in (f, NF + f)]
    w_in, w2 = a["w_in"][0], a["w_in_2"]
    parts = [slots([pieces(w_in[:, 0:2048])]),
             slots([pieces(w_in[:, 2080:6688])]),
             slots(gates([w_in[:, 6688:7712], w_in[:, 7712:8736]], [a["w_dn_out"][0], a["w_attn_out"][0]])),
             slots([pieces(a["w_o"][0])]),
             slots([pieces(a["w_ffn_up"][0], interleave), pieces(a["w_ffn_down"][0])])]
    ffn = lambda w1, w3, wd: [pieces(np.concatenate([w1, w3], axis=1), interleave), pieces(wd)]
    for l in range(2):
        w = w2[l]
        parts += [slots([pieces(w[:, 0:1536])]), slots([pieces(w[:, 1536:3584])]),
                  slots([pieces(w[:, 3584:5632])]),
                  slots(gates([w[:, 5640 + D * i:5640 + D * (i + 1)] for i in range(3)], a["w_branch_2"][l])),
                  slots([pieces(a["w_out_2"][l])])]
        if l == 0:
            parts.append(slots(ffn(a["ffn_w1_2"][0], a["ffn_w3_2"][0], a["ffn_w2_2"][0])))
        else:
            for e in range(NE):
                parts.append(slots(ffn(a["moe_w1_2"][0, e], a["moe_w3_2"][0, e], a["moe_w2_2"][0, e])))

    def col(v):
        return v.reshape(-1, P).T

    def rows(w):
        return w.reshape(KD, P, -1).transpose(1, 0, 2)

    twice = lambda v: np.tile(v, 2)[:, None]
    over = lambda v: np.broadcast_to(v.reshape(1, -1), (P, v.size))
    pair = lambda v: np.repeat(v.reshape(2, 4, 2).transpose(2, 0, 1).reshape(2, 8), CH, axis=0)
    kinds = {"gemm": np.concatenate(parts),
             "mod": np.concatenate([a["w_mod_2"][l].T.reshape(NMOD, P, D) for l in range(2)])}
    out = {"stream": np.stack([kinds[kind][i] for kind, i in stream_order()]),
           "cond": a["c_2"].reshape(1, D),
           "x_t": a["x"][0].T.reshape(KD, P, S).transpose(1, 0, 2),
           "wab": rows(w_in[:, 2048:2080]).reshape(P, KD, 4, 4, 2).transpose(0, 1, 4, 2, 3).reshape(P, KD, 2, 16),
           "cols0": np.concatenate(
               [col(a["norm1_w"][0]), col(a["norm2_w"][0])] + [col(a["dn_conv_w"][0][j]) for j in range(3)]
               + [twice(a["dn_out_norm_w"][0]), twice(a["attn_q_norm_w"][0]), twice(a["attn_k_norm_w"][0])]
               + [col(a["ffn_conv_w"][0][j]) for j in range(3)] + [pair(a["dn_a_log"][0]), pair(a["dn_dt_bias"][0])], axis=1),
           "router_w": rows(a["moe_router_w_2"][0])}
    for l in range(2):
        g = lambda n: a[n + "_2"][l]
        out[f"wif{l + 1}"] = rows(w2[l][:, 5632:5640])
        out[f"cols{l + 1}"] = np.concatenate(
            [col(g("norm1_w")), col(g("norm2_w")), col(g("b_mod"))]
            + [col(g("c_conv_w")[j]) for j in range(4)]
            + [col(g("c_conv_b")), twice(g("a_qnorm_w")), twice(g("a_knorm_w")), g("a_subln_w")[:, None],
               col(a["b_lb_logits_2"][0]), col(a["b_lb_logits_2"][1]), g("b_gnorm_w")[:, None], g("c_norm_w")[:, None],
               over(g("c_igate_b")), over(g("c_fgate_b"))]
            + [over(g(f"a_lambda_{x}")) for x in ("q1", "k1", "q2", "k2")] + [over(a["moe_router_b_2"][0])], axis=1)
    return {n: np.ascontiguousarray(v) for n, v in {**out, **shape_tables()}.items()}


def build(nc, shapes, out):
    with ExitStack() as ctx:
        dram = {n: nc.dram_tensor(f"in_{n}", s, F32, kind="ExternalInput").ap() for n, s in shapes.items()}
        k = Kern(nc, ctx, dram)
        dram["experts"] = dram["stream"][k.place[k.first["ffn2"]]:len(k.order)]
        first_block(k)
        mixer_block(k, 1)
        mixer_block(k, 2)
        with stage(k, "store") as (block, sem, buf):
            stored = sem("stored")

            @block.sync
            def _(sp):
                sp.dma_start(out, k.x[:]).then_inc(stored, 16)
                sp.wait_ge(stored, 16)


def kernel(**inputs):
    import concourse.bacc as bacc
    from concourse.bass_utils import run_bass_kernel_spmd

    arrays = lay_out({n: np.asarray(v) for n, v in inputs.items()})
    nc = bacc.Bacc("TRN2", target_bir_lowering=False, num_devices=1)
    out = nc.dram_tensor("x_out", (P, KD, S), F32, kind="ExternalOutput").ap()
    build(nc, {n: v.shape for n, v in arrays.items()}, out)
    r = run_bass_kernel_spmd(nc, [{f"in_{n}": v for n, v in arrays.items()}], core_ids=[0])
    y = np.asarray(r.results[0]["x_out"])
    return np.ascontiguousarray(y.transpose(1, 0, 2).reshape(D, S).T.reshape(1, S, D))
```
